# Optimizing a Trainium2 kernel written in Bass

```python
import math
import jax, jax.numpy as jnp
from jax import lax
import numpy as np

D_MODEL = 1024
BATCH = 1
SEQ = 256
DEPTH = 2

GRID_W = 64
N_MIXERS = 4
GROUP_WIDTH = D_MODEL // N_MIXERS
HEAD_DIM = 64
Q_BLOCK = 128
EPS = 1e-6

NA_HEADS = GROUP_WIDTH // HEAD_DIM
NA_WIN_ROWS = 8
NA_WIN_COLS = 16

DIFF_HEADS = GROUP_WIDTH // HEAD_DIM
DIFF_QK_DIM = HEAD_DIM // 2
DIFF_V_DIM = HEAD_DIM

GQA_HEADS = GROUP_WIDTH // HEAD_DIM
GQA_KV_HEADS = GQA_HEADS // 2
ROPE_THETA = 10000.0

MLA_HEADS = GROUP_WIDTH // HEAD_DIM
MLA_Q_LORA = GROUP_WIDTH
MLA_KV_LORA = GROUP_WIDTH // 2
MLA_NOPE_DIM = HEAD_DIM
MLA_ROPE_DIM = HEAD_DIM // 2
MLA_V_DIM = HEAD_DIM

D_FF = -(-8 * D_MODEL // (3 * 256)) * 256

IN_SIZES = (
    NA_HEADS * HEAD_DIM, NA_HEADS * HEAD_DIM, NA_HEADS * HEAD_DIM,
    DIFF_HEADS * 2 * DIFF_QK_DIM, DIFF_HEADS * 2 * DIFF_QK_DIM, DIFF_HEADS * DIFF_V_DIM,
    GQA_HEADS * HEAD_DIM, GQA_KV_HEADS * HEAD_DIM, GQA_KV_HEADS * HEAD_DIM,
    MLA_Q_LORA, MLA_KV_LORA, MLA_ROPE_DIM,
)
IN_WIDTH = sum(IN_SIZES)
MIX_WIDTH = NA_HEADS * HEAD_DIM + DIFF_HEADS * DIFF_V_DIM + GQA_HEADS * HEAD_DIM + MLA_HEADS * MLA_V_DIM


def rms_norm(x, w):
    xf = x.astype(jnp.float32)
    y = xf * lax.rsqrt(jnp.mean(xf * xf, axis=-1, keepdims=True) + EPS)
    return (y * w.astype(jnp.float32)).astype(x.dtype)

def rope(x, pos):
    d = x.shape[-1]
    inv = ROPE_THETA ** (-jnp.arange(0, d, 2, dtype=jnp.float32) / d)
    ang = pos.astype(jnp.float32)[:, None] * inv[None, :]
    ang = jnp.concatenate([ang, ang], axis=-1)
    xf = x.astype(jnp.float32)
    x1, x2 = jnp.split(xf, 2, axis=-1)
    rot = jnp.concatenate([-x2, x1], axis=-1)
    return (xf * jnp.cos(ang) + rot * jnp.sin(ang)).astype(x.dtype)

def axial_rope(x, row, col):
    half = x.shape[-1] // 2
    return jnp.concatenate([rope(x[..., :half], row), rope(x[..., half:], col)], axis=-1)

def split_heads(t, n):
    b, s, _ = t.shape
    return t.reshape(b, s, n, -1).transpose(0, 2, 1, 3)

def merge_heads(t):
    b, h, s, d = t.shape
    return t.transpose(0, 2, 1, 3).reshape(b, s, h * d)

def to_blocks(t):
    b, h, s, d = t.shape
    return t.reshape(b, h, s // Q_BLOCK, Q_BLOCK, d).transpose(2, 0, 1, 3, 4)

def from_blocks(t):
    nb, b, h, qb, d = t.shape
    return t.transpose(1, 2, 0, 3, 4).reshape(b, h, nb * qb, d)

def neighbourhood_attention(q, k, v, rel_bias):
    b, h, s, d = q.shape
    rows = s // GRID_W
    wr = min(NA_WIN_ROWS, rows)
    wc = NA_WIN_COLS
    q5 = q.reshape(b, h, rows, GRID_W, d)
    k5 = k.reshape(b, h, rows, GRID_W, d)
    v5 = v.reshape(b, h, rows, GRID_W, d)
    r = jnp.arange(rows)
    row_start = jnp.clip(r - wr // 2, 0, rows - wr)
    c = jnp.arange(GRID_W)
    col_idx = jnp.clip(c - wc // 2, 0, GRID_W - wc)[:, None] + jnp.arange(wc)[None, :]
    dc_idx = col_idx - c[:, None] + (NA_WIN_COLS - 1)
    scale = d ** -0.5

    def row_block(args):
        q_r, rs, r_i = args
        k_band = lax.dynamic_slice_in_dim(k5, rs, wr, axis=2)
        v_band = lax.dynamic_slice_in_dim(v5, rs, wr, axis=2)
        k_win = k_band[:, :, :, col_idx, :]
        v_win = v_band[:, :, :, col_idx, :]
        dr_idx = rs + jnp.arange(wr) - r_i + (NA_WIN_ROWS - 1)
        bias = rel_bias[:, dr_idx[None, :, None], dc_idx[:, None, :]]
        sc = jnp.einsum('bhcd,bhrcwd->bhcrw', q_r, k_win).astype(jnp.float32) * scale + bias.astype(jnp.float32)
        p = jax.nn.softmax(sc.reshape(b, h, GRID_W, wr * wc), axis=-1).reshape(b, h, GRID_W, wr, wc)
        return jnp.einsum('bhcrw,bhrcwd->bhcd', p.astype(v.dtype), v_win)

    out = lax.map(row_block, (q5.transpose(2, 0, 1, 3, 4), row_start, r))
    return out.transpose(1, 2, 0, 3, 4).reshape(b, h, s, d)

def diff_attention(q1, q2, k1, k2, v, lam, slopes):
    s = k1.shape[2]
    pos = jnp.arange(s)
    scale = DIFF_QK_DIM ** -0.5

    def block(args):
        qb1, qb2, qp = args
        dist = jnp.abs(qp[:, None] - pos[None, :]).astype(jnp.float32)
        alibi = -slopes[:, None, None] * dist
        s1 = jnp.einsum('bhqd,bhkd->bhqk', qb1, k1).astype(jnp.float32) * scale + alibi
        s2 = jnp.einsum('bhqd,bhkd->bhqk', qb2, k2).astype(jnp.float32) * scale + alibi
        a = jax.nn.softmax(s1, axis=-1) - lam * jax.nn.softmax(s2, axis=-1)
        return jnp.einsum('bhqk,bhkd->bhqd', a.astype(v.dtype), v)

    out = lax.map(block, (to_blocks(q1), to_blocks(q2), pos.reshape(-1, Q_BLOCK)))
    return from_blocks(out)

def gqa_attention(q, k, v):
    b, h, s, d = q.shape
    kvh = k.shape[1]
    g = h // kvh
    scale = d ** -0.5

    def block(qb):
        qg = qb.reshape(b, kvh, g, Q_BLOCK, d)
        sc = jnp.einsum('bkgqd,bksd->bkgqs', qg, k).astype(jnp.float32) * scale
        o = jnp.einsum('bkgqs,bksd->bkgqd', jax.nn.softmax(sc, axis=-1).astype(v.dtype), v)
        return o.reshape(b, h, Q_BLOCK, d)

    return from_blocks(lax.map(block, to_blocks(q)))

def mla_attention(q_nope, q_rope, k_nope, k_rope, v):
    scale = (MLA_NOPE_DIM + MLA_ROPE_DIM) ** -0.5

    def block(args):
        qn, qr = args
        sc = (jnp.einsum('bhqd,bhkd->bhqk', qn, k_nope)
              + jnp.einsum('bhqd,bkd->bhqk', qr, k_rope)).astype(jnp.float32) * scale
        return jnp.einsum('bhqk,bhkd->bhqd', jax.nn.softmax(sc, axis=-1).astype(v.dtype), v)

    return from_blocks(lax.map(block, (to_blocks(q_nope), to_blocks(q_rope))))

def first_inputs(seed: int = 0) -> dict:
    key = jax.random.key(seed)
    ks = jax.random.split(key, 21)

    def normal(k, shape, scale):
        return scale * jax.random.normal(k, shape, jnp.float32)

    def gain(k, shape):
        return 1.0 + normal(k, shape, 0.05)

    return {
        "x": normal(ks[0], (BATCH, SEQ, D_MODEL), 1.0),
        "pre_mix_norm": gain(ks[1], (DEPTH, D_MODEL)),
        "w_in": normal(ks[2], (DEPTH, D_MODEL, IN_WIDTH), D_MODEL ** -0.5),
        "na_rel_bias": normal(ks[3], (DEPTH, NA_HEADS, 2 * NA_WIN_ROWS - 1, 2 * NA_WIN_COLS - 1), 0.1),
        "diff_lambda_q1": normal(ks[4], (DEPTH, DIFF_QK_DIM), 0.1),
        "diff_lambda_k1": normal(ks[5], (DEPTH, DIFF_QK_DIM), 0.1),
        "diff_lambda_q2": normal(ks[6], (DEPTH, DIFF_QK_DIM), 0.1),
        "diff_lambda_k2": normal(ks[7], (DEPTH, DIFF_QK_DIM), 0.1),
        "diff_subln": gain(ks[8], (DEPTH, DIFF_V_DIM)),
        "gqa_q_norm": gain(ks[9], (DEPTH, HEAD_DIM)),
        "gqa_k_norm": gain(ks[10], (DEPTH, HEAD_DIM)),
        "mla_q_norm": gain(ks[11], (DEPTH, MLA_Q_LORA)),
        "mla_kv_norm": gain(ks[12], (DEPTH, MLA_KV_LORA)),
        "mla_w_uq": normal(ks[13], (DEPTH, MLA_Q_LORA, MLA_HEADS * (MLA_NOPE_DIM + MLA_ROPE_DIM)), MLA_Q_LORA ** -0.5),
        "mla_w_ukv": normal(ks[14], (DEPTH, MLA_KV_LORA, MLA_HEADS * (MLA_NOPE_DIM + MLA_V_DIM)), MLA_KV_LORA ** -0.5),
        "w_o": normal(ks[15], (DEPTH, MIX_WIDTH, D_MODEL), MIX_WIDTH ** -0.5),
        "post_mix_norm": gain(ks[16], (DEPTH, D_MODEL)),
        "pre_ffn_norm": gain(ks[17], (DEPTH, D_MODEL)),
        "ffn_w_gate_up": normal(ks[18], (DEPTH, D_MODEL, 2 * D_FF), D_MODEL ** -0.5),
        "ffn_w_down": normal(ks[19], (DEPTH, D_FF, D_MODEL), D_FF ** -0.5),
        "post_ffn_norm": gain(ks[20], (DEPTH, D_MODEL)),
    }

def first_block(x, pre_mix_norm, w_in, na_rel_bias, diff_lambda_q1, diff_lambda_k1, diff_lambda_q2,
              diff_lambda_k2, diff_subln, gqa_q_norm, gqa_k_norm, mla_q_norm, mla_kv_norm, mla_w_uq,
              mla_w_ukv, w_o, post_mix_norm, pre_ffn_norm, ffn_w_gate_up, ffn_w_down, post_ffn_norm):
    b, s, _ = x.shape
    pos = jnp.arange(s)
    grid_row = pos // GRID_W
    grid_col = pos % GRID_W
    offsets = [int(o) for o in np.cumsum(IN_SIZES)[:-1]]
    alibi_slopes = jnp.asarray([2.0 ** (-8.0 * (i + 1) / DIFF_HEADS) for i in range(DIFF_HEADS)], dtype=jnp.float32)

    for l in range(DEPTH):
        h = rms_norm(x, pre_mix_norm[l])
        proj = jnp.einsum('bsd,de->bse', h, w_in[l])
        (na_q, na_k, na_v, df_q, df_k, df_v, gq_q, gq_k, gq_v,
         ml_cq, ml_ckv, ml_kr) = jnp.split(proj, offsets, axis=-1)

        a_out = neighbourhood_attention(split_heads(na_q, NA_HEADS), split_heads(na_k, NA_HEADS),
                                        split_heads(na_v, NA_HEADS), na_rel_bias[l])

        lambda_init = 0.8 - 0.6 * math.exp(-0.3 * l)
        dq = df_q.reshape(b, s, DIFF_HEADS, 2, DIFF_QK_DIM).transpose(3, 0, 2, 1, 4)
        dk = df_k.reshape(b, s, DIFF_HEADS, 2, DIFF_QK_DIM).transpose(3, 0, 2, 1, 4)
        lam = (jnp.exp(jnp.sum(diff_lambda_q1[l].astype(jnp.float32) * diff_lambda_k1[l].astype(jnp.float32)))
               - jnp.exp(jnp.sum(diff_lambda_q2[l].astype(jnp.float32) * diff_lambda_k2[l].astype(jnp.float32)))
               + lambda_init)
        b_out = diff_attention(dq[0], dq[1], dk[0], dk[1], split_heads(df_v, DIFF_HEADS), lam, alibi_slopes)
        b_out = rms_norm(b_out, diff_subln[l]) * (1.0 - lambda_init)

        cq = axial_rope(rms_norm(split_heads(gq_q, GQA_HEADS), gqa_q_norm[l]), grid_row, grid_col)
        ck = axial_rope(rms_norm(split_heads(gq_k, GQA_KV_HEADS), gqa_k_norm[l]), grid_row, grid_col)
        c_out = gqa_attention(cq, ck, split_heads(gq_v, GQA_KV_HEADS))

        c_q = rms_norm(ml_cq, mla_q_norm[l])
        q_full = split_heads(jnp.einsum('bsr,re->bse', c_q, mla_w_uq[l]), MLA_HEADS)
        q_nope, q_rope = q_full[..., :MLA_NOPE_DIM], rope(q_full[..., MLA_NOPE_DIM:], pos)
        c_kv = rms_norm(ml_ckv, mla_kv_norm[l])
        kv = split_heads(jnp.einsum('bsr,re->bse', c_kv, mla_w_ukv[l]), MLA_HEADS)
        k_nope, mla_v = kv[..., :MLA_NOPE_DIM], kv[..., MLA_NOPE_DIM:]
        k_rope = rope(ml_kr, pos)
        d_out = mla_attention(q_nope, q_rope, k_nope, k_rope, mla_v)

        mix = jnp.concatenate([merge_heads(a_out), merge_heads(b_out),
                               merge_heads(c_out), merge_heads(d_out)], axis=-1)
        mix = jnp.einsum('bse,ed->bsd', mix, w_o[l])
        x = x + rms_norm(mix, post_mix_norm[l])

        h = rms_norm(x, pre_ffn_norm[l])
        gate, up = jnp.split(jnp.einsum('bsd,df->bsf', h, ffn_w_gate_up[l]), 2, axis=-1)
        f = jnp.einsum('bsf,fd->bsd', jax.nn.silu(gate) * up, ffn_w_down[l])
        x = x + rms_norm(f, post_ffn_norm[l])
    return x


DEPTH_2 = 4

N_MIXERS_2 = 3
RMS_EPS = 1e-6
SWA_Q_HEADS = D_MODEL // HEAD_DIM
SWA_KV_HEADS = SWA_Q_HEADS // 4
SWA_WINDOW = 128
ROPE_THETA_2 = 150000.0
GLA_HEADS = 4
GLA_DK = D_MODEL // 2
GLA_DV = D_MODEL
GLA_RANK = 16
GLA_TAU = 16.0
GLA_CHUNK = 64
FOX_HEADS = D_MODEL // HEAD_DIM
FOX_BLOCK = 128
D_FF_2 = -(-8 * D_MODEL // (3 * 256)) * 256


def rmsnorm(x, g):
    xf = x.astype(jnp.float32)
    y = xf * lax.rsqrt(jnp.mean(xf * xf, axis=-1, keepdims=True) + RMS_EPS)
    return (y * g.astype(jnp.float32)).astype(x.dtype)

def modulate(h, shift, scale):
    return h * (1 + scale[:, None, :]) + shift[:, None, :]

def rope_2(x, pos):
    hd = x.shape[-1]
    inv = 1.0 / (ROPE_THETA_2 ** (jnp.arange(0, hd, 2, dtype=jnp.float32) / hd))
    ang = pos[:, None] * inv[None, :]
    cos = jnp.cos(ang)[None, :, None, :]
    sin = jnp.sin(ang)[None, :, None, :]
    xf = x.astype(jnp.float32)
    x1, x2 = jnp.split(xf, 2, axis=-1)
    return jnp.concatenate([x1 * cos - x2 * sin, x2 * cos + x1 * sin], axis=-1).astype(x.dtype)

def swa_mixer(h, w_in, sinks, w_o):
    B, S, _ = h.shape
    W, hd, Hq, Hkv = SWA_WINDOW, HEAD_DIM, SWA_Q_HEADS, SWA_KV_HEADS
    G = Hq // Hkv
    nb = S // W
    proj = h @ w_in
    q, k, v = jnp.split(proj, [Hq * hd, (Hq + Hkv) * hd], axis=-1)
    pos = jnp.arange(S, dtype=jnp.float32)
    q = rope_2(q.reshape(B, S, Hq, hd), pos)
    k = rope_2(k.reshape(B, S, Hkv, hd), pos)
    v = v.reshape(B, S, Hkv, hd)
    qb = q.reshape(B, nb, W, Hkv, G, hd)
    kb = k.reshape(B, nb, W, Hkv, hd)
    vb = v.reshape(B, nb, W, Hkv, hd)
    pad = ((0, 0), (1, 0), (0, 0), (0, 0), (0, 0))
    kk = jnp.concatenate([jnp.pad(kb, pad)[:, :-1], kb], axis=2)
    vv = jnp.concatenate([jnp.pad(vb, pad)[:, :-1], vb], axis=2)
    scores = jnp.einsum('bnqkgd,bnskd->bnkgqs', qb, kk).astype(jnp.float32) * (hd ** -0.5)
    i = jnp.arange(W)[:, None]
    j = jnp.arange(2 * W)[None, :]
    diff = i - j + W
    band = (diff >= 0) & (diff < W)
    has_prev = (jnp.arange(nb) > 0)[:, None, None] | (j >= W)[None]
    mask = band[None] & has_prev
    scores = jnp.where(mask[None, :, None, None], scores, -jnp.inf)
    sink_col = jnp.broadcast_to(
        sinks.astype(jnp.float32).reshape(Hkv, G)[None, None, :, :, None, None],
        scores.shape[:-1] + (1,))
    probs = jax.nn.softmax(jnp.concatenate([scores, sink_col], axis=-1), axis=-1)[..., :-1]
    out = jnp.einsum('bnkgqs,bnskd->bnqkgd', probs.astype(vv.dtype), vv)
    return out.reshape(B, S, Hq * hd) @ w_o

def gla_chunk_step(state, inp):
    q, k, v, b = inp
    C = q.shape[2]
    causal = jnp.tril(jnp.ones((C, C), dtype=bool))
    diff = b[:, :, :, None, :] - b[:, :, None, :, :]
    decay = jnp.exp(jnp.where(causal[None, None, :, :, None], diff, -jnp.inf))
    attn = jnp.einsum('bhtd,bhsd,bhtsd->bhts', q, k, decay)
    o = attn @ v + jnp.einsum('bhtd,bhde->bhte', q * jnp.exp(b), state)
    b_last = b[:, :, -1:, :]
    state = jnp.exp(b_last[:, :, 0, :])[..., None] * state + \
        jnp.einsum('bhsd,bhse->bhde', k * jnp.exp(b_last - b), v)
    return state, o

def gla_mixer(h, w_in, w_gate_up, b_gate, head_norm, w_o):
    B, S, _ = h.shape
    H, C = GLA_HEADS, GLA_CHUNK
    dk, dv = GLA_DK // H, GLA_DV // H
    nc = S // C
    proj = h @ w_in
    q, k, v, r, a_low = jnp.split(
        proj, [GLA_DK, 2 * GLA_DK, 2 * GLA_DK + GLA_DV, 2 * GLA_DK + 2 * GLA_DV], axis=-1)
    log_alpha = jax.nn.log_sigmoid((a_low @ w_gate_up + b_gate).astype(jnp.float32)) / GLA_TAU

    def to_chunks(t, d):
        return t.astype(jnp.float32).reshape(B, nc, C, H, d).transpose(1, 0, 3, 2, 4)

    qc = to_chunks(q, dk) * (dk ** -0.5)
    kc = to_chunks(k, dk)
    vc = to_chunks(v, dv)
    bc = jnp.cumsum(to_chunks(log_alpha, dk), axis=3)
    state0 = jnp.zeros((B, H, dk, dv), jnp.float32)
    _, o = lax.scan(gla_chunk_step, state0, (qc, kc, vc, bc))
    o = o.transpose(1, 0, 3, 2, 4).reshape(B, S, H, dv).astype(h.dtype)
    o = rmsnorm(o, head_norm)
    o = o * jax.nn.silu(r).reshape(B, S, H, dv)
    return o.reshape(B, S, GLA_DV) @ w_o

def fox_mixer(h, w_in, b_f, w_o):
    B, S, D = h.shape
    H, hd, blk = FOX_HEADS, HEAD_DIM, FOX_BLOCK
    proj = h @ w_in
    q, k, v, f_logit = jnp.split(proj, [D, 2 * D, 3 * D], axis=-1)
    log_f = jax.nn.log_sigmoid(f_logit.astype(jnp.float32) + b_f.astype(jnp.float32))
    lc = jnp.cumsum(log_f, axis=1).transpose(0, 2, 1)
    q = q.reshape(B, S, H, hd).transpose(0, 2, 1, 3)
    k = k.reshape(B, S, H, hd).transpose(0, 2, 1, 3)
    v = v.reshape(B, S, H, hd).transpose(0, 2, 1, 3)
    outs = []
    for i in range(S // blk):
        t0, t1 = i * blk, (i + 1) * blk
        s = jnp.einsum('bhqd,bhkd->bhqk', q[:, :, t0:t1], k[:, :, :t1]).astype(jnp.float32) * (hd ** -0.5)
        s = s + lc[:, :, t0:t1, None] - lc[:, :, None, :t1]
        mask = jnp.arange(t1)[None, :] <= (t0 + jnp.arange(blk))[:, None]
        p = jax.nn.softmax(jnp.where(mask[None, None], s, -jnp.inf), axis=-1)
        outs.append(jnp.einsum('bhqk,bhkd->bhqd', p.astype(v.dtype), v[:, :, :t1]))
    o = jnp.concatenate(outs, axis=2).transpose(0, 2, 1, 3).reshape(B, S, D)
    return o @ w_o

def swiglu(h, w_gu, w_down):
    g, u = jnp.split(h @ w_gu, 2, axis=-1)
    return (jax.nn.silu(g) * u) @ w_down

def second_inputs(seed: int = 0) -> dict:
    key = jax.random.key(seed)
    ks = iter(jax.random.split(key, 32))
    D = D_MODEL
    n_swa, n_gla, n_fox = (DEPTH_2 + 2) // 3, (DEPTH_2 + 1) // 3, DEPTH_2 // 3
    nrm = lambda k, shape, s: s * jax.random.normal(k, shape, jnp.float32)
    swa_cols = (SWA_Q_HEADS + 2 * SWA_KV_HEADS) * HEAD_DIM
    gla_cols = 2 * GLA_DK + 2 * GLA_DV + GLA_RANK
    fox_cols = 3 * D + FOX_HEADS
    return {
        "x": nrm(next(ks), (BATCH, SEQ, D), 1.0),
        "c": nrm(next(ks), (BATCH, D), 1.0),
        "ada_w": nrm(next(ks), (DEPTH_2, D, 6 * D), 0.5 * D ** -0.5),
        "ada_b": nrm(next(ks), (DEPTH_2, 6 * D), 0.02),
        "norm_gain": 1.0 + nrm(next(ks), (DEPTH_2, 2, D), 0.05),
        "ffn_w_gu": nrm(next(ks), (DEPTH_2, D, 2 * D_FF_2), D ** -0.5),
        "ffn_w_down": nrm(next(ks), (DEPTH_2, D_FF_2, D), D_FF_2 ** -0.5),
        "swa_w_in": nrm(next(ks), (n_swa, D, swa_cols), D ** -0.5),
        "swa_sinks": nrm(next(ks), (n_swa, SWA_Q_HEADS), 0.5),
        "swa_w_o": nrm(next(ks), (n_swa, SWA_Q_HEADS * HEAD_DIM, D), (SWA_Q_HEADS * HEAD_DIM) ** -0.5),
        "gla_w_in": nrm(next(ks), (n_gla, D, gla_cols), D ** -0.5),
        "gla_w_gate_up": nrm(next(ks), (n_gla, GLA_RANK, GLA_DK), GLA_RANK ** -0.5),
        "gla_b_gate": nrm(next(ks), (n_gla, GLA_DK), 0.1),
        "gla_head_norm": 1.0 + nrm(next(ks), (n_gla, GLA_DV // GLA_HEADS), 0.05),
        "gla_w_o": nrm(next(ks), (n_gla, GLA_DV, D), GLA_DV ** -0.5),
        "fox_w_in": nrm(next(ks), (n_fox, D, fox_cols), D ** -0.5),
        "fox_b_f": jax.random.uniform(next(ks), (n_fox, FOX_HEADS), jnp.float32, 0.0, 3.0),
        "fox_w_o": nrm(next(ks), (n_fox, D, D), D ** -0.5),
        "final_norm": 1.0 + nrm(next(ks), (D,), 0.05),
    }

def second_block(x, c, ada_w, ada_b, norm_gain, ffn_w_gu, ffn_w_down,
              swa_w_in, swa_sinks, swa_w_o,
              gla_w_in, gla_w_gate_up, gla_b_gate, gla_head_norm, gla_w_o,
              fox_w_in, fox_b_f, fox_w_o, final_norm):
    c_act = jax.nn.silu(c)
    for i in range(DEPTH_2):
        kind, j = i % N_MIXERS_2, i // N_MIXERS_2
        mod = c_act @ ada_w[i] + ada_b[i]
        sh1, sc1, g1, sh2, sc2, g2 = jnp.split(mod, 6, axis=-1)
        h = modulate(rmsnorm(x, norm_gain[i, 0]), sh1, sc1)
        if kind == 0:
            y = swa_mixer(h, swa_w_in[j], swa_sinks[j], swa_w_o[j])
        elif kind == 1:
            y = gla_mixer(h, gla_w_in[j], gla_w_gate_up[j], gla_b_gate[j], gla_head_norm[j], gla_w_o[j])
        else:
            y = fox_mixer(h, fox_w_in[j], fox_b_f[j], fox_w_o[j])
        x = x + g1[:, None, :] * y
        h = modulate(rmsnorm(x, norm_gain[i, 1]), sh2, sc2)
        x = x + g2[:, None, :] * swiglu(h, ffn_w_gu[i], ffn_w_down[i])
    return rmsnorm(x, final_norm)


def setup_inputs(seed=0):
    out = dict(first_inputs(seed))
    for name, value in second_inputs(seed + 1).items():
        if name != "x":
            out[name + "_2"] = value
    return out


def reference(
    x, pre_mix_norm, w_in, na_rel_bias, diff_lambda_q1, diff_lambda_k1, diff_lambda_q2,
    diff_lambda_k2, diff_subln, gqa_q_norm, gqa_k_norm, mla_q_norm, mla_kv_norm, mla_w_uq,
    mla_w_ukv, w_o, post_mix_norm, pre_ffn_norm, ffn_w_gate_up, ffn_w_down, post_ffn_norm, c_2,
    ada_w_2, ada_b_2, norm_gain_2, ffn_w_gu_2, ffn_w_down_2, swa_w_in_2, swa_sinks_2, swa_w_o_2,
    gla_w_in_2, gla_w_gate_up_2, gla_b_gate_2, gla_head_norm_2, gla_w_o_2, fox_w_in_2,
    fox_b_f_2, fox_w_o_2, final_norm_2,
):
    x = first_block(
        x, pre_mix_norm, w_in, na_rel_bias, diff_lambda_q1, diff_lambda_k1, diff_lambda_q2,
        diff_lambda_k2, diff_subln, gqa_q_norm, gqa_k_norm, mla_q_norm, mla_kv_norm, mla_w_uq,
        mla_w_ukv, w_o, post_mix_norm, pre_ffn_norm, ffn_w_gate_up, ffn_w_down, post_ffn_norm,
    )
    return second_block(
        x, c_2, ada_w_2, ada_b_2, norm_gain_2, ffn_w_gu_2, ffn_w_down_2, swa_w_in_2,
        swa_sinks_2, swa_w_o_2, gla_w_in_2, gla_w_gate_up_2, gla_b_gate_2, gla_head_norm_2,
        gla_w_o_2, fox_w_in_2, fox_b_f_2, fox_w_o_2, final_norm_2,
    )


_drawn_inputs = setup_inputs


def setup_inputs(seed=0):
    import zlib

    import numpy as np

    out = dict(_drawn_inputs(seed))
    spreads = {}
    factors = {'diff_lambda_q2': 3.659,
     'gqa_q_norm': 7.432,
     'gqa_k_norm': 7.125,
     'mla_q_norm': 6.372,
     'mla_kv_norm': 3.713,
     'ada_b_2': 2.767,
     'norm_gain_2': 3.075,
     'swa_sinks_2': 8.0,
     'gla_b_gate_2': 8.0,
     'gla_head_norm_2': 8.0}
    for name, (base, spread) in spreads.items():
        noise = np.random.default_rng([zlib.crc32(name.encode()), seed]).standard_normal(out[name].shape)
        drawn = base * np.exp(spread * noise) if base else spread * noise
        out[name] = __import__('jax').numpy.asarray(drawn.astype(out[name].dtype))
    for name, factor in factors.items():
        out[name] = (out[name] * factor).astype(out[name].dtype)
    return out
```

```python
import math
from contextlib import ExitStack

import numpy as np
import concourse.bass as bass
from concourse import mybir

P = 128
D = 1024
SEQ = 256
NT = SEQ // P
KT = D // P
HD = 64
DFF = 2816
NF = DFF // P
GRID = 64
DEPTH1, DEPTH2 = 2, 4
EPS = 1e-6
NEG = -1.0e30

UNIT = 2048
RAW = 6
SPLIT = 2
C1_IN, C1_SMALL, C1_O, C1_FFN = 0, 10, 11, 15
FFN_UNITS = NF + NF // 2
PER1 = C1_FFN + FFN_UNITS
SIZES1 = [UNIT] * 9 + [KT * 160, 2 * 384 + 512] + [UNIT] * (4 + FFN_UNITS)
IN2 = {"swa": [UNIT] * 6, "gla": [UNIT] * 4 + [KT * P] + [UNIT] * 8, "fox": [UNIT] * 12 + [KT * 16]}
KINDS2 = ["swa", "gla", "fox", "swa"]
BASE2, SIZES2 = [], []
for _kind in KINDS2:
    BASE2.append(len(SIZES2))
    SIZES2 += IN2[_kind] + [UNIT] * (4 + FFN_UNITS)
UNITS = DEPTH1 * PER1 + len(SIZES2)
STEPS = NF // 2 + 1
ADA = UNIT // 4
ADA_LAYERS = 4

ROW1 = {"subln": (0, 64), "gq": (64, 128), "gk": (128, 192), "lq": (192, 256), "lk": (256, 320), "lam": (320, 322)}
NROW1 = 322
COL1 = {"pre_mix": 0, "pre_ffn": 8, "mla_q": 16, "mla_kv": 18}
NCOL1 = 19
CB1 = {"dist": (0, 512), "na": (512, 576), "rope_c": (576, 1088), "rope_s": (1088, 1600),
       "mla_c": (1600, 1856), "mla_s": (1856, 2112)}
NCB1 = 2112
CB2 = {"rope_c": (0, 512), "rope_s": (512, 1024), "causal": (1024, 1536), "window": (1536, 2048),
       "upto": (2048, 2560), "upto64": (2560, 2688), "level": (2688, 2688 + 7 * 128)}
NCB2 = 2688 + 7 * 128
NROW2 = 2 * 16 + 16 + 256
WORK = 10560


def build(nc, wts, ada, ada_b, x_in, c_col, rel_bias, col1, row1, gain_mix, gain_ffn, col2, row2,
          gate_w, gate_b, final_gain, ident_in, cst1, cst2, out, n2=DEPTH2):
    f32, f32r = mybir.dt.float32, mybir.dt.float32r
    ALU, ACT, AX = mybir.AluOpType, mybir.ActivationFunctionType, mybir.AxisListType
    ctx = ExitStack()
    with ctx:
        def sb(name, shape, dt=f32):
            return ctx.enter_context(nc.sbuf_tensor(name, shape, dt))

        def sem(name):
            return ctx.enter_context(nc.semaphore(name))

        raw = sb("raw", [P, RAW, UNIT])
        whi = sb("whi", [P, SPLIT, UNIT], f32r)
        wlo = sb("wlo", [P, SPLIT, UNIT], f32r)
        ada_raw = sb("ada_raw", [P, 2, UNIT])
        ada_acc = sb("ada_acc", [P, 2, ADA])
        h32 = sb("h32", [P, 2, SEQ])
        hhi = sb("hhi", [P, KT, SEQ], f32r)
        hlo = sb("hlo", [P, KT, SEQ], f32r)
        x = sb("x", [P, NT, D])
        rows = sb("rows", [P, NT, D])
        gain = sb("gain", [P, D])
        cb = sb("cb", [P, max(NCB1, NCB2)])
        ident = sb("ident", [P, P])
        ones = sb("ones", [P, P])
        pcol = sb("pcol", [P, NCOL1])
        prow = sb("prow", [P, NROW1])
        pcol2 = sb("pcol2", [P, DEPTH2 * 16])
        prow2 = sb("prow2", [P, NROW2])
        ccol = sb("ccol", [P, KT])
        nsink = sb("nsink", [P, 32])
        kr_tmp = sb("kr_tmp", [P, 2, 64])
        mod = sb("mod", [P, ADA_LAYERS, 48])
        acol = sb("acol", [P, 16])
        zcol = sb("zcol", [P, 1])
        epsc = sb("epsc", [P, 1])
        ss = sb("ss", [P, 4])
        sd = sb("sd", [P, 4])
        rs = sb("rs", [P, 4])
        gs = sb("gs", [P, 3, 16])
        lamt = sb("lamt", [P, 8])
        nmax = sb("nmax", [P, 4, NT])
        psum_ = sb("psum_", [P, 4, NT])
        esink = sb("esink", [P, 4, NT])
        rsum = sb("rsum", [P, 4, NT])
        work = sb("work", [P, WORK])
        ahi = sb("ahi", [P, 4, SEQ], f32r)
        alo = sb("alo", [P, 4, SEQ], f32r)
        zeros = sb("zeros", [P, P], mybir.dt.bfloat16)

        def w(at, n):
            return work[:, at:at + n]

        def fold(ap, *shape):
            names = "abcde"[:len(shape)]
            spec = " ".join(names)
            return ap.rearrange(f"p ({spec}) -> p {spec}", **dict(zip(names, shape)))

        dense_bias = nc.dram_tensor("dense_bias", (DEPTH1, P, UNIT), f32, kind="Internal").ap()

        psu = ctx.enter_context(nc.psum_tensor("psu", [P, 2, 512], f32))
        pso = ctx.enter_context(nc.psum_tensor("pso", [P, 512], f32))
        psm = ctx.enter_context(nc.psum_tensor("psm", [P, 512], f32))
        psy = ctx.enter_context(nc.psum_tensor("psy", [P, 4, 512], f32))
        banks_o = [pso, psm]
        ps8 = psy[:].rearrange("p b (c n) -> p (b c) n", c=2)
        psy2 = psy[:].rearrange("p (t b) n -> p t (b n)", t=NT)

        naq, nak, nav, dfq, dfk, dfv, gqr = (w(512 * i, 512) for i in range(7))
        gkr, gv, mcq, mckv = w(3584, 256), w(3840, 256), w(4096, 512), w(4608, 320)
        kvr, qcT, kcT = w(4928, 1024), w(5952, 1024), w(6976, 1024)
        prob, probT = fold(w(8000, 1024), 2, 512), fold(w(9024, 1024), 2, 512)
        gqT, gkT = w(10048, 512), gkr
        hw = fold(w(1024, KT * SEQ), KT, SEQ)
        sg, a32 = fold(w(0, 512), 2, SEQ), fold(w(512, 512), 2, SEQ)
        scratch = rows[:].rearrange("p t n -> p (t n)")
        qf, kcat = scratch[:, 0:768], scratch[:, 768:1536]
        wgu, bgate = work[0:16, 9216:9728], work[0:1, 9728:10240]
        

        COLS1 = (0, 1, 3, 4)
        bank0 = [DEPTH1 * 32]
        for kind in KINDS2:
            bank0.append(bank0[-1] + len(IN2[kind]) + NF)
        item0 = [DEPTH1 * 20 + 16 * i for i in (0, 1, 1, 2)]

        start_loads = sem("start_loads")
        c_loaded = sem("c_loaded")
        cb1_loaded = sem("cb1_loaded")
        pool_loads = sem("pool_loads")
        filled = sem("filled")
        cb2_loaded = sem("cb2_loaded")
        raw_loaded = [sem(f"raw_loaded{i}") for i in range(RAW)]
        ada_loaded = [sem(f"ada_loaded{i}") for i in range(2)]
        ada_used = [sem(f"ada_used{i}") for i in range(2)]
        ada_mm = sem("ada_mm")
        ada_evac = sem("ada_evac")
        hi_done = sem("hi_done")
        lo_done = sem("lo_done")
        unit_mm = sem("unit_mm")
        bank_free = sem("bank_free")
        x_ready = sem("x_ready")
        std_ready = sem("std_ready")
        y_ready = sem("y_ready")
        xn_ready = sem("xn_ready")
        tr_done = sem("tr_done")
        hhi_done = sem("hhi_done")
        h_ready = sem("h_ready")
        ystd_ready = sem("ystd_ready")
        par_loaded = sem("par_loaded")
        gain_loaded = sem("gain_loaded")
        bias_spread = sem("bias_spread")
        na_loaded = sem("na_loaded")
        na_ready = sem("na_ready")
        silu_done = sem("silu_done")
        a_ready = sem("a_ready")
        s_done = sem("s_done")
        max_ready = sem("max_ready")
        p_ready = sem("p_ready")
        t_done = sem("t_done")
        pt_ready = sem("pt_ready")
        o_done = sem("o_done")
        o_evac = sem("o_evac")
        mix_ready = sem("mix_ready")
        gq_evac = sem("gq_evac")
        gq_sum = sem("gq_sum")
        gq_std = sem("gq_std")
        gq_rope = sem("gq_rope")
        gq_tr = sem("gq_tr")
        ml_std = sem("ml_std")
        ml_norm = sem("ml_norm")
        ml_tr = sem("ml_tr")
        ml_hi = sem("ml_hi")
        ml_h = sem("ml_h")
        ml_evac = sem("ml_evac")
        ml_rope = sem("ml_rope")
        ml_ctr = sem("ml_ctr")
        qk_ready = sem("qk_ready")
        sub_sum = sem("sub_sum")
        sub_std = sem("sub_std")
        swa_rope = sem("swa_rope")
        swa_tr = sem("swa_tr")
        swa_evac = sem("swa_evac")
        gate_mm = sem("gate_mm")
        gate_bcast = sem("gate_bcast")
        fox_l = sem("fox_l")
        fox_lf = sem("fox_lf")
        fox_c = sem("fox_c")
        fox_ce = sem("fox_ce")
        fox_row = sem("fox_row")
        g_logit = sem("g_logit")
        g_ln = sem("g_ln")
        g_la = sem("g_la")
        g_cum = sem("g_cum")
        g_b = sem("g_b")
        g_e = sem("g_e")
        g_x = sem("g_x")
        g_qk = sem("g_qk")
        g_s = sem("g_s")
        g_acc = sem("g_acc")
        g_dec = sem("g_dec")
        g_dex = sem("g_dex")
        g_kd = sem("g_kd")
        g_kt = sem("g_kt")
        g_kr = sem("g_kr")
        g_ds = sem("g_ds")
        g_st = sem("g_st")
        g_o = sem("g_o")
        g_std = sem("g_std")
        g_r = sem("g_r")
        gate_loaded = sem("gate_loaded")
        start_act = sem("start_act")
        acol_ready = sem("acol_ready")
        stored = sem("stored")
        out_ready = sem("out_ready")

        def unit_no(l, c, i=0):
            return l * PER1 + c + i * RAW

        def size_of(l, c):
            if isinstance(l, int) and l == DEPTH1:
                return SIZES2[c]
            return SIZES1[c % PER1] if c >= 0 else 0

        def last_unit(l, c):
            return isinstance(l, int) and l == DEPTH1 and c >= BASE2[n2 - 1] + (
                len(IN2[KINDS2[n2 - 1]]) + 4 + FFN_UNITS)

        def turns(engine, turn, last):
            with engine.Fori(0, 4 if last else 5) as i:
                turn(i)
            if last:
                turn(4)

        def slot_of(c):
            return c % RAW

        def part_of(c):
            return c % SPLIT

        def load_unit(sp, l, c, i=0, first=False):
            if last_unit(l, c + RAW * i if isinstance(i, int) else c):
                return
            n = size_of(l, c)
            if not first:
                sp.wait_ge(lo_done, unit_no(l, c, i) - RAW + 1)
            u = unit_no(l, c, i)
            src = wts[u] if isinstance(u, int) else wts[bass.ds(u, 1)][0]
            sp.dma_start(raw[:, slot_of(c), 0:n], src[:, 0:n]).then_inc(raw_loaded[slot_of(c)], 16)

        def load_ada(sp, a, s):
            first = isinstance(s, int) and s == 0
            no = a * STEPS + s
            for half in range(2):
                if not first or (isinstance(a, int) and a > 0):
                    sp.wait_ge(ada_used[half], no)
                at = (a * STEPS + s) * 2 + half
                src = ada[at] if isinstance(at, int) else ada[bass.ds(at, 1)][0]
                sp.dma_start(ada_raw[:, half], src).then_inc(ada_loaded[half], 16)

        def sp_ffn(sp, l, c0, a):
            for c in (c0, c0 + 1):
                load_unit(sp, l, c + RAW)
            def turn(i):
                for k in range(2):
                    if a is not None:
                        load_ada(sp, a, 2 + 2 * i + k)
                    for j in range(3):
                        load_unit(sp, l, c0 + 2 + 3 * k + j + RAW, i)

            turns(nc.sync, turn, last_unit(l, c0 + 33))
            load_unit(sp, l, c0 + 32 + RAW)

        block = ctx.enter_context(nc.Block())

        @block.sync
        def _(sp):
            sp.dma_start(x[:], x_in).then_inc(start_loads, 16)
            sp.dma_start(ident[:], ident_in).then_inc(start_loads, 16)
            for c in range(RAW):
                load_unit(sp, 0, c, first=True)
            sp.dma_start(cb[:, 0:NCB1], cst1).then_inc(cb1_loaded, 16)
            with nc.sync.Fori(0, DEPTH1) as l:
                for c in range(RAW, C1_FFN + RAW):
                    load_unit(sp, l, c)
                    if c == C1_SMALL:
                        sp.wait_ge(x_ready, 4 * l + 2)
                        sp.wait_ge(bias_spread, 16 * 16 * DEPTH1)
                        sp.dma_start(ada_raw[:, 0, :], dense_bias[bass.ds(l, 1)][0]).then_inc(na_loaded, 16)
                    if c == C1_O + 1 + RAW:
                        sp.wait_ge(max_ready, l * 20 + 4)
                        load_ada(sp, l, 0)
                        load_ada(sp, l, 1)
                sp_ffn(sp, l, C1_FFN, l)
            for n in range(n2):
                c0 = BASE2[n]
                nin = len(IN2[KINDS2[n]]) + 4
                for c in range(c0, c0 + nin):
                    load_unit(sp, DEPTH1, c + RAW)
                    if n == 0 and c == c0 + 1:
                        load_ada(sp, 2, 0)
                        load_ada(sp, 2, 1)
                if n == 1:
                    sp.wait_ge(mix_ready, DEPTH1 + 1)
                    load_ada(sp, 3, 0)
                    load_ada(sp, 3, 1)
                sp_ffn(sp, DEPTH1, c0 + nin, 2 + n if n < 2 else None)
            sp.wait_ge(out_ready, NT)
            sp.dma_start(out, rows[:]).then_inc(stored, 16)
            sp.wait_ge(stored, 16)

        def pool_weigh(pool, a, s, slot):
            no = a * STEPS + s
            if not isinstance(no, int) or no >= 2:
                pool.wait_ge(ada_mm, no - 1)
            acc = ada_acc[:, slot]
            tt = nc.gpsimd.tensor_tensor
            for half in range(2):
                pool.wait_ge(ada_loaded[half], 16 * (no + 1))
                tiles = fold(ada_raw[:, half], 4, ADA)
                c = ccol[:, 4 * half:4 * half + 4].unsqueeze(2).to_broadcast([P, 4, ADA])
                tt(tiles, tiles, c, ALU.mult)
                nc.gpsimd.drain()
                tt(tiles[:, 0:2], tiles[:, 0:2], tiles[:, 2:4], ALU.add)
                if half == 1:
                    nc.gpsimd.drain()
                    tt(tiles[:, 0], tiles[:, 0], acc, ALU.add)
                nc.gpsimd.drain()
                tt(acc, tiles[:, 0], tiles[:, 1], ALU.add).then_inc(ada_used[half], 1)

        def pool_ada(pool, a):
            with nc.gpsimd.Fori(0, 5) as i:
                pool_weigh(pool, a, 2 + 2 * i, 0)
                pool_weigh(pool, a, 3 + 2 * i, 1)

        def spread_biases(pool):
            for l in range(DEPTH1):
                for t in range(NT):
                    for r in range(2):
                        for h in range(4):
                            at = (l * 4 + h) * 465 + (7 - 2 * t - r) * 31 + 15
                            src = bass.AP(rel_bias.tensor, at, [[31, 4], [-1, 64], [1, 64]])
                            dst = fold(dense_bias[l, 64 * r:64 * r + 64, :], NT, 4, 4, 64)[:, t, h]
                            dst = dst.rearrange("q r c -> r q c")
                            pool.dma_start(dst, src).then_inc(bias_spread, 16)

        @block.gpsimd
        def _(pool):
            nc.gpsimd.memset(ones[:], 1.0).then_inc(filled, 1)
            nc.gpsimd.memset(epsc[:], EPS).then_inc(filled, 1)
            nc.gpsimd.memset(zcol[:], 0.0).then_inc(filled, 1)
            nc.gpsimd.memset(zeros[:], 0.0).then_inc(filled, 1)
            pool.dma_start(ccol[:], c_col).then_inc(c_loaded, 16)
            for l in range(DEPTH1):
                if l > 0:
                    pool.wait_ge(h_ready, 24 * l)
                pool.dma_start(pcol[:], col1[l]).then_inc(par_loaded, 16)
                pool.dma_start(prow[:], row1[l].partition_broadcast(P)).then_inc(par_loaded, 16)
                if l == 0:
                    spread_biases(pool)
                    pool.dma_start(mod[:], ada_b).then_inc(pool_loads, 16)
                    pool.dma_start(pcol2[:], col2).then_inc(pool_loads, 16)
                    pool.dma_start(prow2[:], row2.partition_broadcast(P)).then_inc(pool_loads, 16)
                pool.wait_ge(x_ready, 2 + 4 * l)
                pool.dma_start(gain[:], gain_mix[l].partition_broadcast(P)).then_inc(gain_loaded, 16)
                pool.wait_ge(na_loaded, 16 * (l + 1))
                pool.wait_ge(cb1_loaded, 16)
                nb = fold(ada_raw[:, 0, :], 32, 64)
                mask = cb[:, CB1["na"][0]:CB1["na"][1]]
                nc.gpsimd.tensor_tensor(nb, nb, mask.unsqueeze(1).to_broadcast([P, 32, 64]), ALU.add).then_inc(na_ready, 1)
                if l == 0:
                    pool.wait_ge(start_act, 1)
                pool_weigh(pool, l, 0, 0)
                pool_weigh(pool, l, 1, 1)
                pool.wait_ge(x_ready, 2 + 4 * l + 2)
                pool.dma_start(gain[:], gain_ffn[l].partition_broadcast(P)).then_inc(gain_loaded, 16)
                pool_ada(pool, l)
            pool.dma_start(cb[:, 0:NCB2], cst2).then_inc(cb2_loaded, 16)
            if n2 >= 2:
                pool.wait_ge(o_evac, item0[0] + 16)
                pool.dma_start(wgu, gate_w).then_inc(gate_loaded, 16)
                pool.dma_start(bgate, gate_b).then_inc(gate_loaded, 16)
            for n in range(min(n2, 2)):
                pool_weigh(pool, DEPTH1 + n, 0, 0)
                pool_weigh(pool, DEPTH1 + n, 1, 1)
                pool_ada(pool, DEPTH1 + n)
            if n2 == DEPTH2:
                pool.wait_ge(x_ready, 2 + 4 * (DEPTH1 + n2))
                pool.dma_start(gain[:], final_gain[0].partition_broadcast(P)).then_inc(gain_loaded, 16)

        mm = nc.tensor.matmul

        def pe_unit_cols(pe, c, bank, n=2, q=None):
            k = part_of(c)
            width = n * P
            last = None

            def product(kt, cc, start):
                cols = slice(kt * width + cc * P, kt * width + cc * P + P)
                for j, (a, h) in enumerate(((whi, hhi), (whi, hlo), (wlo, hhi))):
                    m = mm(psu[:, bank, cc * SEQ:(cc + 1) * SEQ], a[:, k, cols], h[:, kt, :],
                           start=(start and j == 0), stop=(kt == KT - 1 and j == 2), skip_group_check=q is not None)
                return m

            if q is not None:
                for kt in range(KT):
                    if kt % 2 == 0:
                        pe.wait_ge(h_ready, 8 * q + kt + 2)
                    for cc in range(n):
                        last = product(kt, cc, kt == 0 and cc == 0)
            else:
                for cc in range(n):
                    for kt in range(KT):
                        last = product(kt, cc, kt == 0)
            return last

        def pe_unit_rows(pe, c, width, outs, q=None, y_after=False):
            k = part_of(c)
            last = None
            for t in range(NT):
                for kt in range(KT):
                    if q is not None and t == 0 and kt % 2 == 0:
                        pe.wait_ge(h_ready, 8 * q + kt + 2)
                    toks = slice(t * P, t * P + P)
                    for j, (h, a) in enumerate(((hhi, whi), (hlo, whi), (hhi, wlo))):
                        last = mm(outs[t], h[:, kt, toks], a[:, k, kt * width:(kt + 1) * width],
                                  start=(kt == 0 and j == 0), stop=(kt == KT - 1 and j == 2))
                if y_after and t == 0:
                    last.then_inc(y_ready, 1)
            return last

        def pe_in_unit(pe, l, c, j, bank, kind, q, width=256):
            pe.wait_ge(lo_done, unit_no(l, c) + 1)
            if j >= 2:
                pe.wait_ge(bank_free, bank - 1)
            b = (bank if isinstance(bank, int) else j) % 2
            if kind == "cols":
                last = pe_unit_cols(pe, c, b, width // P, q if j == 0 else None)
            else:
                last = pe_unit_rows(pe, c, width, [psu[:, b, t * width:(t + 1) * width] for t in range(NT)],
                                    q if j == 0 else None)
            last.then_inc(unit_mm, 1)

        def pe_transpose(pe, q):
            for kt in range(KT):
                for t in range(NT):
                    last = nc.tensor.transpose(ps8[:, kt, t * P:(t + 1) * P],
                                               rows[:, t, kt * P:(kt + 1) * P], ident[:])
                last.then_inc(tr_done, 1)

        def pe_norm(pe, m, q):
            def turned(kt, t):
                return mm(ps8[:, kt, t * P:(t + 1) * P], x[:, t, kt * P:(kt + 1) * P], rows[:, t, 0:P],
                          start=True, stop=True)

            pe.wait_ge(xn_ready, NT * m + 1)
            for kt in range(4):
                turned(kt, 0)
            pe.wait_ge(xn_ready, NT * m + 2)
            for kt in range(KT):
                if kt >= 4:
                    turned(kt, 0)
                turned(kt, 1).then_inc(tr_done, 1)

        def pe_out(pe, l, c0, n, ready):
            pe.wait_ge(*ready)
            pe_transpose(pe, 3 * n + 1)
            for j in range(4):
                pe.wait_ge(lo_done, unit_no(l, c0 + j) + 1)
                last = pe_unit_rows(pe, c0 + j, 256, [psy2[:, t, j * 256:(j + 1) * 256] for t in range(NT)],
                                    3 * n + 1 if j == 0 else None, y_after=(j == 3))
                last.then_inc(unit_mm, 1)

        def pe_ada(pe, a, s, slot):
            no = a * STEPS + s
            pe.wait_ge(ada_used[1], no + 1)
            if not isinstance(s, int) or s > 0:
                pe.wait_ge(ada_evac, no)
            for j in range(4):
                last = mm(psm[:, j:j + 1], ada_acc[:, slot, j * P:(j + 1) * P], ones[:, 0:1], start=True, stop=True)
            last.then_inc(ada_mm, 1)

        def pe_ffn(pe, l, c0, n, bo, par, a, gated=False):
            def gu(c, i, f, bank, q=None):
                pe.wait_ge(lo_done, unit_no(l, c, i) + 1)
                pe.wait_ge(bank_free, bo + f - 1)
                pe_unit_cols(pe, c, bank, q=q).then_inc(unit_mm, 1)

            def dn(c, i, s, aslot, last_step=False):
                pe.wait_ge(lo_done, unit_no(l, c, i) + 1)
                pe.wait_ge(a_ready, n * NF + 2 * s + 2)
                k = part_of(c)
                for t in range(NT):
                    toks = slice(t * P, t * P + P)
                    for ff in range(2):
                        for half in range(2):
                            cols = slice(ff * 1024 + half * 512, ff * 1024 + half * 512 + 512)
                            for j, (h, b) in enumerate(((ahi, whi), (alo, whi), (ahi, wlo))):
                                last = mm(psy[:, 2 * t + half, :], h[:, aslot + ff, toks], b[:, k, cols],
                                          start=False, stop=(last_step and ff == 1 and j == 2),
                                          skip_group_check=True)
                    if last_step and t == 0:
                        last.then_inc(y_ready, 1)
                return last

            gu(c0, 0, 0, par, 3 * n + 2)
            gu(c0 + 1, 0, 1, 1 - par)
            for b in range(4):
                mm(fold(psy[:, b, :], 4, P), zeros[:], zeros[:].unsqueeze(1).to_broadcast([P, 4, P]),
                   start=True, stop=False, skip_group_check=True)
            if gated and a is not None:
                pe.wait_ge(gate_bcast, 2 * (n - DEPTH1) + 2)
            if a is not None:
                pe_ada(pe, a, 0, 0)
            with nc.tensor.Fori(0, 5) as i:
                for k in range(2):
                    c = c0 + 2 + 3 * k
                    gu(c, i, 2 + 4 * i + 2 * k, par)
                    gu(c + 1, i, 3 + 4 * i + 2 * k, 1 - par)
                    dn(c + 2, i, 2 * i + k, 2 * k).then_inc(unit_mm, 1)
                    if a is not None:
                        pe_ada(pe, a, 1 + 2 * i + k, 1 - k)
            dn(c0 + 32, 0, 10, 0, last_step=True).then_inc(unit_mm, 1)
            if a is not None:
                pe_ada(pe, a, 11, 1)

        def pe_items(pe, I0, items):
            def scores(k):
                it = items[k]
                if k >= 2:
                    pe.wait_ge(p_ready, I0 + k - 1)
                if it["pre"] is not None:
                    pe.wait_ge(*it["pre"])
                for t in range(NT):
                    o = psy[:, k % 2, t * SEQ:(t + 1) * SEQ]
                    last = mm(o, it["q"][:, t * P:(t + 1) * P], it["k"], start=True, stop=it["add"] is None)
                    if it["add"] is not None:
                        last = mm(o, ones[0:1, 0:P], it["add"], start=False, stop=True)
                last.then_inc(s_done, 1)

            def transposes(k):
                pe.wait_ge(p_ready, I0 + k + 1)
                if k >= 2:
                    pe.wait_ge(pt_ready, I0 + k - 1)
                for kc in range(2):
                    for t in range(NT):
                        at = (kc * NT + t) * P
                        last = nc.tensor.transpose(psy[:, 2 + k % 2, at:at + P],
                                                   prob[:, k % 2, t * SEQ + kc * P:t * SEQ + kc * P + P], ident[:])
                last.then_inc(t_done, 1)

            def values(k):
                pe.wait_ge(pt_ready, I0 + k + 1)
                if k >= 2:
                    pe.wait_ge(o_evac, I0 + k - 1)
                for t in range(NT):
                    for kc in range(2):
                        at = (kc * NT + t) * P
                        last = mm(banks_o[k % 2][:, t * HD:(t + 1) * HD],
                                  probT[:, k % 2, at:at + P], items[k]["v"][kc],
                                  start=(kc == 0), stop=(kc == 1))
                last.then_inc(o_done, 1)

            n = len(items)
            scores(0)
            for k in range(n):
                if k + 1 < n:
                    scores(k + 1)
                transposes(k)
                if k >= 1:
                    values(k - 1)
            values(n - 1)

        def act_items(act, I0, items):
            def copy(k):
                act.wait_ge(t_done, I0 + k + 1)
                if k >= 2:
                    act.wait_ge(o_done, I0 + k - 1)
                nc.scalar.copy(probT[:, k % 2], psy[:, 2 + k % 2, :]).then_inc(pt_ready, 1)

            n = len(items)
            for k in range(n):
                it = items[k]
                act.wait_ge(max_ready, I0 + k + 1)
                if it["bias"] is None and k >= 2:
                    act.wait_ge(t_done, I0 + k - 1)
                src = psy[:, k % 2] if it["bias"] is None else prob[:, k % 2]
                if it["sink"] is not None:
                    nc.scalar.activation(esink[:, k % 4], nmax[:, k % 4], ACT.Exp, bias=it["sink"])
                for t in range(NT):
                    last = nc.scalar.activation(prob[:, k % 2, t * SEQ:(t + 1) * SEQ], src[:, t * SEQ:(t + 1) * SEQ],
                                                ACT.Exp, bias=nmax[:, k % 4, t:t + 1],
                                                accum_out=psum_[:, k % 4, t:t + 1])
                last.then_inc(p_ready, 1)
                if k >= 1:
                    copy(k - 1)
            copy(n - 1)

        def dve_items(dve, I0, items):
            def maxima(k):
                it = items[k]
                dve.wait_ge(s_done, I0 + k + 1)
                src = psy[:, k % 2]
                if it["bias"] is not None:
                    if k >= 2:
                        dve.wait_ge(t_done, I0 + k - 1)
                    it["bias"](prob[:, k % 2], src)
                    nc.vector.drain()
                    src = prob[:, k % 2]
                last = nc.vector.tensor_reduce(out=nmax[:, k % 4], in_=fold(src, NT, SEQ), op=ALU.max,
                                               axis=AX.X, negate=True)
                if it["sink"] is not None:
                    nc.vector.drain()
                    last = nc.vector.tensor_scalar(nmax[:, k % 4], nmax[:, k % 4], it["nsink"], None, ALU.min)
                last.then_inc(max_ready, 1)

            def divide(k):
                it = items[k]
                dve.wait_ge(o_done, I0 + k + 1)
                if it["sink"] is not None:
                    nc.vector.tensor_tensor(psum_[:, k % 4], psum_[:, k % 4], esink[:, k % 4], ALU.add)
                    nc.vector.drain()
                nc.vector.reciprocal(rsum[:, k % 4], psum_[:, k % 4])
                nc.vector.drain()

                def over(k, o):
                    src = fold(banks_o[k % 2][:, 0:P], NT, HD)
                    return nc.vector.tensor_tensor(o, src, rsum[:, k % 4].unsqueeze(2).to_broadcast([P, NT, HD]), ALU.mult)

                o = rows[:, :, it["col"]:it["col"] + HD]
                if it["pair"] is None:
                    over(k, o).then_inc(o_evac, 1)
                elif it["pair"] == 1:
                    nc.vector.tensor_scalar(rsum[:, k % 4], rsum[:, k % 4], lamt[:, 4:5], None, ALU.mult)
                    nc.vector.drain()
                    over(k - 1, o)
                    tmp = fold(h32[:, 0, 0:P], NT, HD)
                    over(k, tmp)
                    nc.vector.drain()
                    nc.vector.tensor_tensor(o, o, tmp, ALU.subtract).then_inc(o_evac, 2)

            n = len(items)
            for k in range(n + 2):
                if k < n:
                    maxima(k)
                if k >= 2:
                    divide(k - 2)

        def act_hi(act, l, c, i=0, first=False):
            if last_unit(l, c + RAW * i if isinstance(i, int) else c):
                return
            n = size_of(l, c)
            u = unit_no(l, c, i)
            turn = (l * (PER1 // RAW) + i + c // RAW + 1) * 16
            act.wait_ge(raw_loaded[slot_of(c)], turn)
            if not first:
                act.wait_ge(unit_mm, u - SPLIT + 1)
            nc.scalar.copy(whi[:, part_of(c), 0:n], raw[:, slot_of(c), 0:n]).then_inc(hi_done, 1)

        def dve_lo(dve, l, c, i=0):
            if last_unit(l, c + RAW * i if isinstance(i, int) else c):
                return
            n = size_of(l, c)
            dve.wait_ge(hi_done, unit_no(l, c, i) + 1)
            nc.vector.tensor_tensor(wlo[:, part_of(c), 0:n], raw[:, slot_of(c), 0:n],
                                    whi[:, part_of(c), 0:n].bitcast(f32), ALU.subtract).then_inc(lo_done, 1)

        def act_rms(t):
            nc.scalar.drain()
            return nc.scalar.activation(sd[:, t:t + 1], ss[:, t:t + 1], ACT.Sqrt, bias=epsc[:], scale=1.0 / D)

        def act_norm(act, m, q, scale, bias):
            for t in range(NT):
                act.wait_ge(x_ready, 2 * m + t + 1)
                nc.scalar.activation(rows[:, t], x[:, t], ACT.Square, accum_out=ss[:, t:t + 1])
                act_rms(t).then_inc(std_ready, 1)
            if q is None:
                return
            for kt in range(0, KT, 2):
                act.wait_ge(tr_done, 8 * q + kt + 2)
                for k in (kt, kt + 1):
                    nc.scalar.activation(hw[:, k], ps8[:, k], ACT.Identity, scale=scale[:, k:k + 1],
                                         bias=zcol[:] if bias is None else bias[:, k:k + 1])
                nc.scalar.drain()
                nc.scalar.copy(hhi[:, kt:kt + 2], hw[:, kt:kt + 2]).then_inc(hhi_done, 2)

        def act_split(act, q):
            for kt in range(0, KT, 2):
                act.wait_ge(tr_done, 8 * q + kt + 2)
                nc.scalar.copy(hhi[:, kt:kt + 2], ps8[:, kt:kt + 2]).then_inc(hhi_done, 2)

        def dve_split(dve, q, src):
            for kt in range(0, KT, 2):
                dve.wait_ge(hhi_done, 8 * q + kt + 2)
                nc.vector.tensor_tensor(hlo[:, kt:kt + 2], src[:, kt:kt + 2], hhi[:, kt:kt + 2].bitcast(f32),
                                        ALU.subtract).then_inc(h_ready, 2)

        def dve_norm(dve, m, q):
            for t in range(NT):
                dve.wait_ge(std_ready, NT * m + t + 1)
                nc.vector.reciprocal(rs[:, t:t + 1], sd[:, t:t + 1])
                nc.vector.drain()
                nc.vector.tensor_scalar(rows[:, t, 0:P], ident[:], rs[:, t:t + 1], None, ALU.mult).then_inc(xn_ready, 1)
            dve_split(dve, q, hw)

        def wait_y(engine, m, t, l, c):
            if t == 0:
                engine.wait_ge(y_ready, m + 1)
            else:
                engine.wait_ge(unit_mm, unit_no(l, c) + 1)

        def act_post(act, m, l, c):
            for t in range(NT):
                wait_y(act, m, t, l, c)
                nc.scalar.activation(rows[:, t], psy2[:, t], ACT.Square, accum_out=ss[:, 2 + t:3 + t])
                act_rms(2 + t).then_inc(ystd_ready, 1)

        def dve_post(dve, m):
            dve.wait_ge(gain_loaded, 16 * (m + 1))
            for t in range(NT):
                dve.wait_ge(ystd_ready, NT * m + t + 1)
                nc.vector.reciprocal(rs[:, 2 + t:3 + t], sd[:, 2 + t:3 + t])
                nc.vector.drain()
                nc.vector.scalar_tensor_tensor(out=rows[:, t], in0=psy2[:, t], scalar=rs[:, 2 + t:3 + t],
                                               in1=gain[:], op0=ALU.mult, op1=ALU.mult)
                nc.vector.drain()
                nc.vector.tensor_tensor(x[:, t], x[:, t], rows[:, t], ALU.add).then_inc(x_ready, 1)

        def act_ffn(act, l, c0, n, par):
            def silu(c, i, f, bank):
                act.wait_ge(unit_mm, unit_no(l, c, i) + 1)
                act_hi(act, l, c + 2, i)
                if not (isinstance(f, int) and f < 2):
                    act.wait_ge(a_ready, n * NF + f - 1)
                nc.scalar.activation(sg[:, bank], psu[:, bank, 0:SEQ], ACT.Silu).then_inc(silu_done, 1)

            silu(c0, 0, 0, par)
            silu(c0 + 1, 0, 1, 1 - par)

            def turn(i):
                for k in range(2):
                    c = c0 + 2 + 3 * k
                    silu(c, i, 2 + 4 * i + 2 * k, par)
                    silu(c + 1, i, 3 + 4 * i + 2 * k, 1 - par)
                    act_hi(act, l, c + 4, i)

            turns(nc.scalar, turn, last_unit(l, c0 + 33))
            act_hi(act, l, c0 + 34)

        def dve_ffn(dve, l, c0, n, par, a):
            def activations(c, i, f, bank, aslot):
                dve_lo(dve, l, c + 2, i)
                dve.wait_ge(silu_done, n * NF + f + 1)
                nc.vector.tensor_tensor(a32[:, bank], sg[:, bank], psu[:, bank, SEQ:2 * SEQ], ALU.mult).then_inc(bank_free, 1)
                nc.vector.drain()
                nc.vector.tensor_copy(ahi[:, aslot], a32[:, bank])
                nc.vector.drain()
                nc.vector.tensor_tensor(alo[:, aslot], a32[:, bank], ahi[:, aslot].bitcast(f32), ALU.subtract).then_inc(a_ready, 1)

            def add_out(s):
                dve.wait_ge(ada_mm, a * STEPS + s + 1)
                if isinstance(s, int) and isinstance(a, int):
                    o = mod[:, a, 4 * s:4 * s + 4]
                else:
                    o = mod[:].rearrange("p a c -> p (a c)")[:, bass.ds(a * 48 + 4 * s, 4)]
                nc.vector.tensor_tensor(o, o, psm[:, 0:4], ALU.add).then_inc(ada_evac, 1)

            activations(c0, 0, 0, par, 0)
            activations(c0 + 1, 0, 1, 1 - par, 1)
            def turn(i):
                for k in range(2):
                    c = c0 + 2 + 3 * k
                    activations(c, i, 2 + 4 * i + 2 * k, par, 2 - 2 * k)
                    if a is not None:
                        add_out(2 * i + k)
                    activations(c + 1, i, 3 + 4 * i + 2 * k, 1 - par, 3 - 2 * k)
                    dve_lo(dve, l, c + 4, i)

            turns(nc.vector, turn, last_unit(l, c0 + 33))
            dve_lo(dve, l, c0 + 34)
            if a is not None:
                add_out(10)
                add_out(11)

        def pe_gate(pe, n, which):
            if which == 0:
                pe.wait_ge(ada_evac, STEPS * min(n + 2, ADA_LAYERS))
            for j in range(KT):
                o = (pso if j < 4 else psm)[:, (j % 4) * P:(j % 4 + 1) * P]
                col = 16 + 24 * which + j
                last = mm(o, mod[:, n, col:col + 1].to_broadcast([P, P]), ident[:], start=True, stop=True)
            last.then_inc(gate_mm, 1)

        def act_gate(act, n, which):
            act.wait_ge(gate_mm, 2 * n + which + 1)
            act.wait_ge(x_ready, 2 + 2 * (2 * (DEPTH1 + n) + which))
            nc.scalar.copy(gain[:, 0:512], pso[:])
            nc.scalar.copy(gain[:, 512:1024], psm[:]).then_inc(gate_bcast, 1)

        def dve_gated(dve, n, which, c):
            dve.wait_ge(gate_bcast, 2 * n + which + 1)
            for t in range(NT):
                wait_y(dve, 2 * (DEPTH1 + n) + which, t, DEPTH1, c)
                nc.vector.tensor_tensor(rows[:, t], psy2[:, t], gain[:], ALU.mult)
                nc.vector.drain()
                nc.vector.tensor_tensor(x[:, t], x[:, t], rows[:, t], ALU.add).then_inc(x_ready, 1)

        def item(q, k, v, col, add=None, bias=None, sink=None, nsink=None, pair=None):
            return dict(q=q, k=k, v=v, col=col, add=add, bias=bias, sink=sink, nsink=nsink, pair=pair, pre=None)

        def na_bias(h):
            def bias(dst, src):
                b = fold(ada_raw[:, 0, :], NT, 4, SEQ)[:, :, h]
                return nc.vector.tensor_tensor(fold(dst, NT, SEQ), fold(src, NT, SEQ), b, ALU.add)
            return bias

        def distance_bias(h):
            def bias(dst, src):
                slope = 2.0 ** (-8.0 * (h + 1) / 4)
                return nc.vector.scalar_tensor_tensor(out=dst, in0=cb[:, 0:512], scalar=slope, in1=src,
                                                      op0=ALU.mult, op1=ALU.add)
            return bias

        def window_bias(dst, src):
            lo, hi = CB2["window"]
            return nc.vector.tensor_tensor(dst, src, cb[:, lo:hi], ALU.add)

        def forget_bias(h):
            def bias(dst, src):
                lo = CB2["causal"][0]
                for t in range(NT):
                    s = slice(t * SEQ, (t + 1) * SEQ)
                    last = nc.vector.scalar_tensor_tensor(
                        out=dst[:, s], in0=src[:, s], scalar=lcq[:, t * 16 + h:t * 16 + h + 1],
                        in1=cb[:, lo + t * SEQ:lo + (t + 1) * SEQ], op0=ALU.add, op1=ALU.add)
                return last
            return bias

        def heads1():
            out = []
            for h in range(4):
                ps, c = slice(64 * (h % 2), 64 * (h % 2) + 64), (h // 2) * SEQ
                out.append(item(naq[ps, c:c + SEQ], nak[ps, c:c + SEQ],
                                [nav[:, kc * 256 + h * HD:kc * 256 + (h + 1) * HD] for kc in range(2)],
                                h * HD, bias=na_bias(h)))
            for h in range(4):
                for which in range(2):
                    p0, c = 64 * (h % 2) + 32 * which, (h // 2) * SEQ
                    ps = slice(p0, p0 + 32)
                    out.append(item(dfq[ps, c:c + SEQ], dfk[ps, c:c + SEQ],
                                    [dfv[:, kc * 256 + h * HD:kc * 256 + (h + 1) * HD] for kc in range(2)],
                                    256 + h * HD, bias=distance_bias(h), pair=which))
            for c in range(2):
                for kv in range(2):
                    ps = slice(64 * kv, 64 * kv + 64)
                    out.append(item(gqT[ps, c * SEQ:(c + 1) * SEQ], gkT[ps, :],
                                    [gv[:, kc * P + kv * HD:kc * P + (kv + 1) * HD] for kc in range(2)],
                                    512 + (2 * kv + c) * HD))
            for h in range(4):
                out.append(item(qcT[0:96, h * SEQ:(h + 1) * SEQ], kcT[0:96, h * SEQ:(h + 1) * SEQ],
                                [kvr[:, kc * 512 + h * P + HD:kc * 512 + (h + 1) * P] for kc in range(2)],
                                768 + h * HD))
            return out

        s_raw, s_roped = fold(w(0, 1024), 2, 512), fold(w(1024, 1024), 2, 512)
        s_u, s_v = w(2048, 512), w(2560, 512)
        s_qT, s_kT, s_vv = w(3072, 2048), w(5120, 512), w(5632, 512)

        def heads_swa(sidx):
            out = []
            for ch in range(8):
                for half in range(2):
                    kvh = 2 * (ch // 4) + half
                    h = kvh * 4 + ch % 4
                    ps = slice(64 * half, 64 * half + 64)
                    at = sidx * 16 + h
                    out.append(item(s_qT[ps, ch * SEQ:(ch + 1) * SEQ],
                                    s_kT[ps, (ch // 4) * SEQ:(ch // 4 + 1) * SEQ],
                                    [s_vv[:, kc * 256 + kvh * HD:kc * 256 + (kvh + 1) * HD] for kc in range(2)],
                                    h * HD, bias=window_bias, sink=prow2[:, at:at + 1], nsink=nsink[:, at:at + 1]))
            return out

        f_qT, f_kT, f_v = w(0, 2048), w(2048, 2048), w(4096, 2048)
        f_x, f_l, f_lf, lcq, f_row = w(6144, 32), w(6176, 32), w(6208, 32), w(6240, 32), w(6272, 256)

        def heads_fox():
            out = []
            for h in range(16):
                ps, c = slice(64 * (h % 2), 64 * (h % 2) + 64), (h // 2) * SEQ
                out.append(item(f_qT[ps, c:c + SEQ], f_kT[ps, c:c + SEQ],
                                [f_v[:, kc * D + h * HD:kc * D + (h + 1) * HD] for kc in range(2)], h * HD,
                                add=ada_raw[0:1, h // 8, (h % 8) * SEQ:(h % 8 + 1) * SEQ], bias=forget_bias(h)))
            return out

        g_qT, g_kT, g_bT = w(0, 1024), w(1024, 1024), w(2048, 1024)
        g_Q, g_K, g_E, g_S = w(3072, 1024), w(4096, 1024), w(5120, 1024), w(3072, 3072)
        g_lag, g_v = w(6144, 1024), w(7168, 2048)
        g_att, g_krow = scratch[:, 0:1024], scratch[:, 1024:2048]
        g_low, g_tmp = h32[0:16, 0], h32[:].rearrange("p a n -> p (a n)")
        g_ret = ada_raw[:].rearrange("p a n -> p (a n)")[:, 0:2048]
        eb = gs[:, 2]

        def rope(src, dst, c, s, u, v, d):
            def halves(ap):
                return ap.rearrange("p t (n two d) -> p t n two d", two=2, d=d)
            nc.vector.tensor_tensor(u, src, c, ALU.mult)
            for i in range(2):
                nc.vector.tensor_tensor(halves(v)[:, :, :, i], halves(src)[:, :, :, 1 - i], halves(s)[:, :, :, i], ALU.mult)
            nc.vector.drain()
            return nc.vector.tensor_tensor(dst, u, v, ALU.add)

        def tabs(lo, hi, n):
            return fold(cb[:, lo:hi], NT, n)

        def pe_swa(pe, n, c0, b0):
            s5 = 5 * (n // 3)

            def heads(j):
                pe.wait_ge(swa_rope, s5 + j + 1)
                if j >= 2:
                    pe.wait_ge(swa_evac, s5 + j - 1)
                else:
                    pe.wait_ge(gate_bcast, 2 * n + 1)
                o = pso if j % 2 == 0 else psm
                for c in range(2):
                    for t in range(NT):
                        last = nc.tensor.transpose(o[:, c * SEQ + t * P:c * SEQ + (t + 1) * P],
                                                   s_roped[:, j % 2, t * 256 + c * P:t * 256 + (c + 1) * P], ident[:])
                last.then_inc(swa_tr, 1)

            for j in range(6):
                pe_in_unit(pe, DEPTH1, c0 + j, j, b0 + j, "rows", 3 * (DEPTH1 + n))
                if j >= 1:
                    heads(j - 1)
            pe.wait_ge(swa_evac, s5 + 5)
            pe.wait_ge(bank_free, b0 + 6)
            pe_items(pe, item0[n], heads_swa(n // 3))

        def pe_fox(pe, n, c0, b0):
            for j in range(13):
                pe_in_unit(pe, DEPTH1, c0 + j, j, b0 + j, "cols" if j < 8 else "rows", 3 * (DEPTH1 + n), 16 if j == 12 else 256)
            pe.wait_ge(fox_lf, 1)
            lo = CB2["upto"][0]
            for t in range(NT):
                for kt in range(t + 1):
                    mm(psm[:, t * 16:(t + 1) * 16], cb[:, lo + kt * SEQ + t * P:lo + kt * SEQ + (t + 1) * P],
                       f_lf[:, kt * 16:(kt + 1) * 16], start=(kt == 0), stop=(kt == t))
            for kt in range(2):
                last = mm(pso[0:16, 0:SEQ], f_lf[:, kt * 16:(kt + 1) * 16], cb[:, lo + kt * SEQ:lo + (kt + 1) * SEQ],
                          start=(kt == 0), stop=(kt == 1))
            last.then_inc(fox_c, 1)
            pe.wait_ge(fox_row, 32)
            pe_items(pe, item0[n], heads_fox())

        def pe_gla(pe, n, c0, b0):
            for j in range(13):
                pe_in_unit(pe, DEPTH1, c0 + j, j, b0 + j, "cols" if j < 5 else "rows", 3 * (DEPTH1 + n), P if j == 4 else 256)
                if j == 6:
                    pe.wait_ge(bank_free, b0 + 5)
                    pe.wait_ge(gate_loaded, 32)
                    for t in range(NT):
                        mm(psy[:, t, :], g_low[:, t * P:(t + 1) * P], wgu, start=True, stop=False)
                        last = mm(psy[:, t, :], ones[0:1, 0:P], bgate, start=False, stop=True)
                    last.then_inc(g_logit, 1)
                if j == 8:
                    pe.wait_ge(g_la, 1)
                    lo = CB2["upto64"][0]
                    for t in range(NT):
                        for h in range(4):
                            last = mm(psy[:, 2 + t, h * P:(h + 1) * P], g_lag[:, t * 512 + h * P:t * 512 + (h + 1) * P],
                                      cb[:, lo:lo + P], start=True, stop=True)
                    last.then_inc(g_cum, 1)
            pe.wait_ge(bank_free, b0 + 13)
            pe.wait_ge(g_b, 1)
            for lv in range(7):
                if lv >= 1:
                    pe.wait_ge(g_qk, lv)
                if lv >= 2:
                    pe.wait_ge(g_acc, lv - 1)
                q, k = (g_qT, g_kT) if lv == 0 else (g_Q, g_K)
                for t in range(NT):
                    for h in range(4):
                        at = h * SEQ + t * P
                        last = mm(psy[:, (lv % 2) * 2 + t, h * P:(h + 1) * P], k[:, at:at + P], q[:, at:at + P],
                                  start=True, stop=True)
                last.then_inc(g_s, 1)
            pe.wait_ge(g_kd, 1)
            for t in range(NT):
                for h in range(4):
                    last = nc.tensor.transpose(psu[:, t, h * P:(h + 1) * P],
                                               g_E[:, h * SEQ + t * P:h * SEQ + (t + 1) * P], ident[:])
            last.then_inc(g_kt, 1)
            pe.wait_ge(g_kr, 1)
            pe.wait_ge(g_acc, 7)
            for c in range(3):
                t, ps = c // 2, slice(64 * (c % 2), 64 * (c % 2) + 64)
                for h in range(4):
                    o = (psy[:, 2 * c + h // 2] if c < 2 else psu[:, h // 2])[:, (h % 2) * 256:(h % 2 + 1) * 256]
                    last = mm(o, g_krow[ps, t * 512 + h * P:t * 512 + (h + 1) * P],
                              g_v[ps, t * D + h * 256:t * D + (h + 1) * 256], start=True, stop=True)
            last.then_inc(g_ds, 1)
            pe.wait_ge(g_st, 1)
            for t in range(NT):
                for h in range(4):
                    o = psy2[:, t, h * 256:(h + 1) * 256]
                    mm(o, g_att[:, t * 512 + h * P:t * 512 + (h + 1) * P], g_v[:, t * D + h * 256:t * D + (h + 1) * 256],
                       start=True, stop=False, skip_group_check=True)
                    for c in (2 * t, 2 * t + 1):
                        if c == 0:
                            continue
                        ps = slice(64 * (c % 2), 64 * (c % 2) + 64)
                        last = mm(o[ps], g_lag[:, h * SEQ + c * 64:h * SEQ + c * 64 + 64],
                                  g_S[:, (c - 1) * 1024 + h * 256:(c - 1) * 1024 + (h + 1) * 256],
                                  start=False, stop=(c % 2 == 1), skip_group_check=True)
            last.then_inc(g_o, 1)

        def act_swa(act, n, c0, b0):
            s5 = 5 * (n // 3)

            def evac(j):
                act.wait_ge(swa_tr, s5 + j + 1)
                o = pso if j % 2 == 0 else psm
                dst = s_qT[:, j * 512:(j + 1) * 512] if j < 4 else s_kT
                nc.scalar.copy(dst, o[:]).then_inc(swa_evac, 1)

            for j in range(6):
                act.wait_ge(unit_mm, unit_no(DEPTH1, c0 + j) + 1)
                act_hi(act, DEPTH1, c0 + j + SPLIT)
                src = psu[:, (b0 + j) % 2]
                if j < 5:
                    if j >= 2:
                        act.wait_ge(swa_rope, s5 + j - 1)
                    nc.scalar.activation(s_raw[:, j % 2], src, ACT.Copy, scale=HD ** -0.5 if j < 4 else 1.0).then_inc(bank_free, 1)
                else:
                    nc.scalar.copy(s_vv, src).then_inc(bank_free, 1)
                if j >= 1:
                    evac(j - 1)
            act_items(act, item0[n], heads_swa(n // 3))

        def act_fox(act, n, c0, b0):
            for j in range(13):
                act.wait_ge(unit_mm, unit_no(DEPTH1, c0 + j) + 1)
                act_hi(act, DEPTH1, c0 + j + SPLIT)
                src = psu[:, (b0 + j) % 2]
                if j < 4:
                    nc.scalar.activation(f_qT[:, j * 512:(j + 1) * 512], src, ACT.Copy, scale=HD ** -0.5).then_inc(bank_free, 1)
                elif j < 8:
                    nc.scalar.copy(f_kT[:, (j - 4) * 512:(j - 3) * 512], src).then_inc(bank_free, 1)
                elif j < 12:
                    dst = fold(f_v, NT, D)[:, :, (j - 8) * 256:(j - 7) * 256]
                    nc.scalar.copy(dst, fold(src, NT, 256)).then_inc(bank_free, 1)
            act.wait_ge(bank_free, b0 + 13)
            nc.scalar.activation(f_l, f_x, ACT.Abs)
            nc.scalar.drain()
            nc.scalar.activation(f_l, f_l, ACT.Exp, scale=-1.0)
            nc.scalar.drain()
            nc.scalar.activation(f_l, f_l, ACT.Ln, bias=1.0).then_inc(fox_l, 1)
            act.wait_ge(fox_c, 1)
            nc.scalar.copy(lcq, psm[:, 0:32])
            nc.scalar.activation(f_row[0:16, :], pso[0:16, 0:SEQ], ACT.Copy, scale=-1.0).then_inc(fox_ce, 1)
            act.wait_ge(fox_ce, 1)
            for i in range(2):
                act.dma_start(ada_raw[0:1, i, :].rearrange("o (h n) -> o h n", h=8), f_row[8 * i:8 * i + 8, :]).then_inc(fox_row, 16)
            act_items(act, item0[n], heads_fox())

        def act_gla(act, n, c0, b0):
            def log_parts():
                act.wait_ge(g_logit, 1)
                for t in range(NT):
                    nc.scalar.activation(g_Q[:, t * 512:(t + 1) * 512], psy[:, t, :], ACT.Abs)
                nc.scalar.drain()
                nc.scalar.activation(g_Q, g_Q, ACT.Exp, scale=-1.0)
                nc.scalar.drain()
                nc.scalar.activation(g_Q, g_Q, ACT.Ln, bias=1.0).then_inc(g_ln, 1)

            for j in range(13):
                act.wait_ge(unit_mm, unit_no(DEPTH1, c0 + j) + 1)
                act_hi(act, DEPTH1, c0 + j + SPLIT)
                src = psu[:, (b0 + j) % 2]
                if j < 2:
                    nc.scalar.activation(g_qT[:, j * 512:(j + 1) * 512], src, ACT.Copy, scale=P ** -0.5).then_inc(bank_free, 1)
                elif j < 4:
                    nc.scalar.copy(g_kT[:, (j - 2) * 512:(j - 1) * 512], src).then_inc(bank_free, 1)
                elif j == 4:
                    nc.scalar.copy(g_low, src[0:16, 0:SEQ]).then_inc(bank_free, 1)
                elif j < 9:
                    dst = fold(g_v, NT, D)[:, :, (j - 5) * 256:(j - 4) * 256]
                    nc.scalar.copy(dst, fold(src, NT, 256)).then_inc(bank_free, 1)
                else:
                    dst = fold(g_ret, NT, D)[:, :, (j - 9) * 256:(j - 8) * 256]
                    nc.scalar.copy(dst, fold(src, NT, 256)).then_inc(bank_free, 1)
                if j == 7:
                    log_parts()
            act.wait_ge(g_cum, 1)
            for t in range(NT):
                dst = fold(g_bT, 4, SEQ)[:, :, t * P:(t + 1) * P]
                last = nc.scalar.activation(dst, fold(psy[:, 2 + t], 4, P), ACT.Copy, scale=1.0 / 16)
            last.then_inc(g_b, 1)
            for lv in range(1, 7):
                act.wait_ge(g_e, lv)
                nc.scalar.activation(g_E, g_E, ACT.Exp).then_inc(g_x, 1)
            act.wait_ge(g_dec, 1)
            nc.scalar.activation(g_E, g_E, ACT.Exp)
            nc.scalar.activation(g_lag, g_bT, ACT.Exp)
            nc.scalar.activation(eb, fold(g_bT, 16, 64)[:, :, 63], ACT.Exp).then_inc(g_dex, 1)
            act.wait_ge(g_kt, 1)
            nc.scalar.copy(fold(g_krow, 2, 512), psu[:]).then_inc(g_kr, 1)
            act.wait_ge(g_o, 1)
            for t in range(NT):
                for h in range(4):
                    nc.scalar.activation(w((t * 4 + h) * 256, 256), psy2[:, t, h * 256:(h + 1) * 256], ACT.Square,
                                         accum_out=gs[:, 0, t * 4 + h:t * 4 + h + 1])
            nc.scalar.drain()
            nc.scalar.activation(gs[:, 1, 0:8], gs[:, 0, 0:8], ACT.Sqrt, bias=epsc[:], scale=1.0 / 256)
            nc.scalar.activation(g_ret, g_ret, ACT.Silu).then_inc(g_std, 1)

        def dve_swa(dve, n, c0, b0):
            s5 = 5 * (n // 3)
            rc, rsn = tabs(*CB2["rope_c"], 256), tabs(*CB2["rope_s"], 256)
            for j in range(6):
                nc.vector.drain()
                dve_lo(dve, DEPTH1, c0 + j + SPLIT)
                if j < 5:
                    dve.wait_ge(bank_free, b0 + j + 1)
                    if j >= 2:
                        dve.wait_ge(swa_tr, s5 + j - 1)
                    rope(fold(s_raw[:, j % 2], NT, 256), fold(s_roped[:, j % 2], NT, 256), rc, rsn,
                         fold(s_u, NT, 256), fold(s_v, NT, 256), 32).then_inc(swa_rope, 1)
            dve_items(dve, item0[n], heads_swa(n // 3))

        def dve_fox(dve, n, c0, b0):
            for j in range(13):
                dve_lo(dve, DEPTH1, c0 + j + SPLIT)
            dve.wait_ge(unit_mm, unit_no(DEPTH1, c0 + 12) + 1)
            dve.wait_ge(bank_free, b0 + 12)
            nc.vector.tensor_tensor(fold(f_x, NT, 16), fold(psu[:, (b0 + 12) % 2, 0:32], NT, 16),
                                    prow2[:, 32:48].unsqueeze(1).to_broadcast([P, NT, 16]), ALU.add).then_inc(bank_free, 1)
            dve.wait_ge(fox_l, 1)
            nc.vector.scalar_tensor_tensor(out=f_lf, in0=f_x, scalar=0.0, in1=f_l, op0=ALU.min, op1=ALU.subtract).then_inc(fox_lf, 1)
            dve.wait_ge(fox_ce, 1)
            dve_items(dve, item0[n], heads_fox())

        def dve_gla(dve, n, c0, b0):
            for j in range(13):
                dve_lo(dve, DEPTH1, c0 + j + SPLIT)
                if j == 7:
                    dve.wait_ge(g_ln, 1)
                    for t in range(NT):
                        last = nc.vector.scalar_tensor_tensor(out=g_lag[:, t * 512:(t + 1) * 512], in0=psy[:, t, :], scalar=0.0,
                                                              in1=g_Q[:, t * 512:(t + 1) * 512], op0=ALU.min, op1=ALU.subtract)
                    last.then_inc(g_la, 1)
            nc.vector.drain()
            nc.vector.memset(g_Q, 0.0)
            nc.vector.memset(g_K, 0.0)
            nc.vector.drain()
            dve.wait_ge(g_b, 1)
            lo = CB2["level"][0]

            def add_level(lv):
                dve.wait_ge(g_s, lv + 1)
                mask = cb[:, lo + lv * P:lo + (lv + 1) * P].unsqueeze(1).to_broadcast([P, 4, P])
                for t in range(NT):
                    src = fold(psy[:, (lv % 2) * 2 + t], 4, P)
                    acc = g_att[:, t * 512:(t + 1) * 512]
                    if lv == 0:
                        last = nc.vector.tensor_tensor(fold(acc, 4, P), src, mask, ALU.mult)
                    else:
                        nc.vector.tensor_tensor(fold(g_tmp, 4, P), src, mask, ALU.mult)
                        nc.vector.drain()
                        last = nc.vector.tensor_tensor(acc, acc, g_tmp, ALU.add)
                        if t == 0:
                            nc.vector.drain()
                last.then_inc(g_acc, 1)

            for lv in range(1, 7):
                m = 64 >> lv
                nb = 1024 // (2 * m)

                def parts(ap):
                    return ap.rearrange("p (n two m) -> p n two m", two=2, m=m)
                b4 = parts(g_bT)
                ref = b4[:, :, 0, m - 1:m].to_broadcast([P, nb, m])
                Eu, El = fold(g_E[:, 0:512], nb, m), fold(g_E[:, 512:1024], nb, m)
                if lv > 1:
                    nc.vector.drain()
                nc.vector.tensor_tensor(Eu, b4[:, :, 1, :], ref, ALU.subtract)
                nc.vector.tensor_tensor(El, ref, b4[:, :, 0, :], ALU.subtract).then_inc(g_e, 1)
                add_level(lv - 1)
                dve.wait_ge(g_x, lv)
                nc.vector.tensor_tensor(parts(g_Q)[:, :, 1, :], parts(g_qT)[:, :, 1, :], Eu, ALU.mult)
                nc.vector.tensor_tensor(parts(g_K)[:, :, 0, :], parts(g_kT)[:, :, 0, :], El, ALU.mult).then_inc(g_qk, 1)
            nc.vector.drain()
            b3 = fold(g_bT, 16, 64)
            nc.vector.tensor_tensor(fold(g_E, 16, 64), b3[:, :, 63:64].to_broadcast([P, 16, 64]), b3, ALU.subtract).then_inc(g_dec, 1)
            add_level(6)
            dve.wait_ge(g_dex, 1)
            nc.vector.tensor_tensor(g_E, g_E, g_kT, ALU.mult)
            nc.vector.tensor_tensor(g_lag, g_lag, g_qT, ALU.mult).then_inc(g_kd, 1)
            dve.wait_ge(g_ds, 1)
            nc.vector.tensor_copy(fold(g_S[:, 0:1024], 2, 512), psy[:, 0:2])
            nc.vector.drain()
            for c in (1, 2):
                for h in range(4):
                    src = (psy[:, 2 + h // 2] if c == 1 else psu[:, h // 2])[:, (h % 2) * 256:(h % 2 + 1) * 256]
                    at = (c - 1) * 1024 + h * 256
                    last = nc.vector.scalar_tensor_tensor(out=g_S[:, at + 1024:at + 1280], in0=g_S[:, at:at + 256],
                                                          scalar=eb[:, h * 4 + c:h * 4 + c + 1], in1=src,
                                                          op0=ALU.mult, op1=ALU.add)
                if c == 1:
                    nc.vector.drain()
            last.then_inc(g_st, 1)
            dve.wait_ge(g_std, 1)
            nc.vector.reciprocal(gs[:, 2, 0:8], gs[:, 1, 0:8])
            nc.vector.drain()
            for t in range(NT):
                r4 = rows[:, t].rearrange("p (h d) -> p h d", h=4)
                nc.vector.tensor_tensor(r4, psy2[:, t].rearrange("p (h d) -> p h d", h=4),
                                        gs[:, 2, t * 4:t * 4 + 4].unsqueeze(2).to_broadcast([P, 4, 256]), ALU.mult)
                nc.vector.drain()
                nc.vector.tensor_tensor(r4, r4, prow2[:, 48:304].unsqueeze(1).to_broadcast([P, 4, 256]), ALU.mult)
                nc.vector.drain()
                last = nc.vector.tensor_tensor(rows[:, t], rows[:, t], g_ret[:, t * D:(t + 1) * D], ALU.mult)
            last.then_inc(mix_ready, 1)

        @block.tensor
        def _(pe):
            pe.wait_ge(start_loads, 16 * 2)
            pe.wait_ge(filled, 4)
            with nc.tensor.Fori(0, DEPTH1) as l:
                pe_norm(pe, 2 * l, 3 * l)
                for j in range(10):
                    pe_in_unit(pe, l, j, j, l * 32 + j, "cols" if j in COLS1 else "rows", 3 * l, 160 if j == 9 else 256)
                pe.wait_ge(gq_rope, l + 1)
                for t in range(NT):
                    for c in range(2):
                        nc.tensor.transpose(pso[:, c * SEQ + t * P:c * SEQ + (t + 1) * P],
                                            gqr[:, t * 256 + c * P:t * 256 + (c + 1) * P], ident[:])
                    last = nc.tensor.transpose(psm[:, t * P:(t + 1) * P], gkr[:, t * P:(t + 1) * P], ident[:])
                last.then_inc(gq_tr, 1)
                pe.wait_ge(ml_norm, l + 1)
                for t in range(NT):
                    for c in range(2):
                        nc.tensor.transpose(ps8[:, c, t * P:(t + 1) * P],
                                            mcq[:, t * 256 + c * P:t * 256 + (c + 1) * P], ident[:])
                    last = nc.tensor.transpose(ps8[:, 2, t * P:(t + 1) * P], mckv[:, t * 160:t * 160 + P], ident[:])
                last.then_inc(ml_tr, 1)
                pe.wait_ge(ml_h, 3 * l + 3)
                pe.wait_ge(lo_done, unit_no(l, C1_SMALL) + 1)
                ks = part_of(C1_SMALL)
                for t in range(NT):
                    toks = slice(t * P, t * P + P)
                    for o, kts, base, width in ((psy[:, t, 0:384], (0, 1), 0, 384), (psy[:, 2 + t, :], (2,), 768, 512)):
                        for kt in kts:
                            cols = slice(base + (kt % 2) * width, base + (kt % 2) * width + width)
                            for j, (h, a) in enumerate(((hhi, whi), (hlo, whi), (hhi, wlo))):
                                last = mm(o, h[:, kt, toks], a[:, ks, cols],
                                          start=(kt == kts[0] and j == 0), stop=(kt == kts[-1] and j == 2))
                last.then_inc(unit_mm, 1)
                pe.wait_ge(ml_rope, l + 1)
                for h in range(4):
                    for t in range(NT):
                        nc.tensor.transpose(ps8[0:96, h, t * P:(t + 1) * P],
                                            qf[:, t * 384 + h * 96:t * 384 + (h + 1) * 96], ident[:])
                        last = nc.tensor.transpose(ps8[0:96, 4 + h, t * P:(t + 1) * P],
                                                   kcat[:, t * 384 + h * 96:t * 384 + (h + 1) * 96], ident[:])
                last.then_inc(ml_ctr, 1)
                pe.wait_ge(qk_ready, l + 1)
                pe_items(pe, l * 20, heads1())
                pe_out(pe, l, C1_O, l, (mix_ready, l + 1))
                pe_norm(pe, 2 * l + 1, 3 * l + 2)
                pe_ffn(pe, l, C1_FFN, l, l * 32 + 10, 0, l)
            for n in range(n2):
                kind, c0, b0, g = KINDS2[n], BASE2[n], bank0[n], DEPTH1 + n
                nin = len(IN2[kind])
                pe_norm(pe, 2 * g, 3 * g)
                pe_gate(pe, n, 0)
                {"swa": pe_swa, "gla": pe_gla, "fox": pe_fox}[kind](pe, n, c0, b0)
                pe_out(pe, DEPTH1, c0 + nin, g, (mix_ready, DEPTH1 + 1) if kind == "gla" else (o_evac, item0[n] + 16))
                pe_norm(pe, 2 * g + 1, 3 * g + 2)
                pe_gate(pe, n, 1)
                pe_ffn(pe, DEPTH1, c0 + nin + 4, g, b0 + nin, (b0 + nin) % 2, g if g < ADA_LAYERS else None, gated=True)

        @block.scalar
        def _(act):
            act.wait_ge(start_loads, 16 * 2)
            act.wait_ge(filled, 4)
            act.wait_ge(c_loaded, 16)
            nc.scalar.activation(ccol[:], ccol[:], ACT.Silu).then_inc(start_act, 1)
            for c in range(SPLIT):
                act_hi(act, 0, c, first=True)
            with nc.scalar.Fori(0, DEPTH1) as l:
                act.wait_ge(par_loaded, 32 * (l + 1))
                act_norm(act, 2 * l, 3 * l, pcol[:, 0:8], None)
                dst = {0: (naq, HD ** -0.5), 1: (nak, 1.0), 2: (nav, 1.0), 3: (dfq, 32 ** -0.5), 4: (dfk, 1.0),
                       5: (dfv, 1.0), 6: (gqr, 1.0), 8: (mcq, 1.0)}
                for j in range(10):
                    act.wait_ge(unit_mm, unit_no(l, j) + 1)
                    act_hi(act, l, j + SPLIT)
                    src = psu[:, j % 2]
                    if j in dst:
                        nc.scalar.activation(dst[j][0], src, ACT.Copy, scale=dst[j][1]).then_inc(bank_free, 1)
                    elif j == 7:
                        nc.scalar.copy(fold(gkr, NT, P), fold(src, NT, 256)[:, :, 0:P])
                        nc.scalar.copy(fold(gv, NT, P), fold(src, NT, 256)[:, :, P:256]).then_inc(bank_free, 1)
                    else:
                        nc.scalar.copy(mckv, src[:, 0:320]).then_inc(bank_free, 1)
                nc.scalar.drain()
                for t in range(NT):
                    nc.scalar.activation(prob[:, t, 0:256], mcq[:, t * 256:(t + 1) * 256], ACT.Square, accum_out=ss[:, t:t + 1])
                    nc.scalar.activation(prob[:, t, 256:256 + P], mckv[:, t * 160:t * 160 + P], ACT.Square, accum_out=ss[:, 2 + t:3 + t])
                nc.scalar.drain()
                nc.scalar.activation(sd[:, 0:2], ss[:, 0:2], ACT.Sqrt, bias=epsc[:], scale=1.0 / 256)
                nc.scalar.activation(sd[:, 2:4], ss[:, 2:4], ACT.Sqrt, bias=epsc[:], scale=1.0 / 128).then_inc(ml_std, 1)
                act.wait_ge(gq_sum, l + 1)
                nc.scalar.activation(gs[:, 1, 0:12], gs[:, 0, 0:12], ACT.Sqrt, bias=epsc[:], scale=1.0 / HD)
                nc.scalar.activation(lamt[:, 2:4], lamt[:, 0:2], ACT.Exp).then_inc(gq_std, 1)
                act.wait_ge(gq_tr, l + 1)
                nc.scalar.activation(gqT, pso[:], ACT.Copy, scale=HD ** -0.5)
                nc.scalar.copy(gkT, psm[:, 0:SEQ])
                act.wait_ge(ml_tr, l + 1)
                for c in range(3):
                    if c == 2:
                        act.wait_ge(ml_h, 3 * l + 1)
                    nc.scalar.activation(h32[:, c % 2], ps8[:, c], ACT.Identity, scale=pcol[:, 16 + c:17 + c], bias=zcol[:])
                    nc.scalar.drain()
                    nc.scalar.copy(hhi[:, c], h32[:, c % 2]).then_inc(ml_hi, 1)
                act.wait_ge(unit_mm, unit_no(l, C1_SMALL) + 1)
                act_hi(act, l, C1_SMALL + SPLIT)
                for t in range(NT):
                    nc.scalar.activation(qf[:, t * 384:(t + 1) * 384], psy[:, t, 0:384], ACT.Copy, scale=96 ** -0.5)
                    last = nc.scalar.copy(kvr[:, t * 512:(t + 1) * 512], psy[:, 2 + t, :])
                last.then_inc(ml_evac, 1)
                act.wait_ge(ml_ctr, l + 1)
                for i in range(2):
                    nc.scalar.copy(qcT[0:96, i * 512:(i + 1) * 512], psy[0:96, i, :])
                    last = nc.scalar.copy(kcT[0:96, i * 512:(i + 1) * 512], psy[0:96, 2 + i, :])
                last.then_inc(qk_ready, 1)
                act_items(act, l * 20, heads1())
                act.wait_ge(sub_sum, l + 1)
                nc.scalar.activation(gs[:, 1, 0:8], gs[:, 0, 0:8], ACT.Sqrt, bias=epsc[:], scale=1.0 / HD).then_inc(sub_std, 1)
                act_split(act, 3 * l + 1)
                for j in range(4):
                    act_hi(act, l, C1_O + j + SPLIT)
                act_post(act, 2 * l, l, C1_O + 3)
                act_norm(act, 2 * l + 1, 3 * l + 2, pcol[:, 8:16], None)
                act_ffn(act, l, C1_FFN, l, 0)
                act_post(act, 2 * l + 1, l, PER1 - 1)
            for n in range(n2):
                kind, c0, b0, g = KINDS2[n], BASE2[n], bank0[n], DEPTH1 + n
                nin = len(IN2[kind])
                act.wait_ge(acol_ready, n + 1)
                act_norm(act, 2 * g, 3 * g, acol[:, 0:8], mod[:, n, 0:8])
                act_gate(act, n, 0)
                {"swa": act_swa, "gla": act_gla, "fox": act_fox}[kind](act, n, c0, b0)
                act_split(act, 3 * g + 1)
                for j in range(4):
                    act_hi(act, DEPTH1, c0 + nin + j + SPLIT)
                act_norm(act, 2 * g + 1, 3 * g + 2, acol[:, 8:16], mod[:, n, 24:32])
                act_gate(act, n, 1)
                act_ffn(act, DEPTH1, c0 + nin + 4, g, (b0 + nin) % 2)
            act_norm(act, 2 * (DEPTH1 + n2), None, None, None)

        @block.vector
        def _(dve):
            dve.wait_ge(start_loads, 16 * 2)
            nc.vector.memset(esink[:], 0.0).then_inc(x_ready, 2)
            for c in range(SPLIT):
                dve_lo(dve, 0, c)
            with nc.vector.Fori(0, DEPTH1) as l:
                dve_norm(dve, 2 * l, 3 * l)
                for j in range(10):
                    dve_lo(dve, l, j + SPLIT)
                dve.wait_ge(bank_free, l * 32 + 8)
                dve.wait_ge(par_loaded, 32 * (l + 1))
                dve.wait_ge(cb1_loaded, 16)
                dve.wait_ge(pool_loads, 16 * 3)
                dve.wait_ge(start_act, 1)
                qs, ks = scratch[:, 0:512], scratch[:, 1024:1280]
                nc.vector.tensor_tensor(qs, gqr, gqr, ALU.mult)
                nc.vector.tensor_tensor(ks, gkr, gkr, ALU.mult)
                nc.vector.tensor_tensor(scratch[:, 1536:1600], prow[:, 192:256], prow[:, 256:320], ALU.mult)
                nc.vector.drain()
                nc.vector.tensor_reduce(out=gs[:, 0, 0:8], in_=fold(qs, 8, HD), op=ALU.add, axis=AX.X)
                nc.vector.tensor_reduce(out=gs[:, 0, 8:12], in_=fold(ks, 4, HD), op=ALU.add, axis=AX.X)
                nc.vector.tensor_reduce(out=lamt[:, 0:2], in_=fold(scratch[:, 1536:1600], 2, 32), op=ALU.add,
                                        axis=AX.X).then_inc(gq_sum, 1)
                dve.wait_ge(gq_std, l + 1)
                nc.vector.reciprocal(gs[:, 2, 0:12], gs[:, 1, 0:12])
                nc.vector.tensor_tensor(lamt[:, 5:6], lamt[:, 2:3], lamt[:, 3:4], ALU.subtract)
                nc.vector.drain()
                nc.vector.tensor_tensor(lamt[:, 4:5], lamt[:, 5:6], prow[:, 320:321], ALU.add)
                for src, n, at, gn in ((gqr, 8, 0, "gq"), (gkr, 4, 8, "gk")):
                    v = fold(src, n, HD)
                    nc.vector.tensor_tensor(v, v, gs[:, 2, at:at + n].unsqueeze(2).to_broadcast([P, n, HD]), ALU.mult)
                nc.vector.drain()
                for src, n, at, gn in ((gqr, 8, 0, "gq"), (gkr, 4, 8, "gk")):
                    v = fold(src, n, HD)
                    nc.vector.tensor_tensor(v, v, prow[:, ROW1[gn][0]:ROW1[gn][1]].unsqueeze(1).to_broadcast([P, n, HD]), ALU.mult)
                nc.vector.drain()
                rc, rsn = tabs(*CB1["rope_c"], 256), tabs(*CB1["rope_s"], 256)
                rope(fold(gkr, NT, P), fold(gkr, NT, P), rc[:, :, 0:P], rsn[:, :, 0:P],
                     fold(scratch[:, 1024:1280], NT, P), fold(scratch[:, 1280:1536], NT, P), 16)
                rope(fold(gqr, NT, 256), fold(gqr, NT, 256), rc, rsn,
                     fold(scratch[:, 0:512], NT, 256), fold(scratch[:, 512:1024], NT, 256), 16).then_inc(gq_rope, 1)
                dve.wait_ge(ml_std, l + 1)
                nc.vector.reciprocal(rs[:, 0:4], sd[:, 0:4])
                nc.vector.drain()
                for t in range(NT):
                    a, b = mcq[:, t * 256:(t + 1) * 256], mckv[:, t * 160:t * 160 + P]
                    nc.vector.tensor_scalar(a, a, rs[:, t:t + 1], None, ALU.mult)
                    last = nc.vector.tensor_scalar(b, b, rs[:, 2 + t:3 + t], None, ALU.mult)
                last.then_inc(ml_norm, 1)
                for c in range(3):
                    dve.wait_ge(ml_hi, 3 * l + c + 1)
                    nc.vector.tensor_tensor(hlo[:, c], h32[:, c % 2], hhi[:, c].bitcast(f32), ALU.subtract).then_inc(ml_h, 1)
                dve_lo(dve, l, C1_SMALL + SPLIT)
                dve.wait_ge(ml_evac, l + 1)
                mc, ms = tabs(*CB1["mla_c"], P), tabs(*CB1["mla_s"], P)
                qr = fold(qf, NT, 4, 96)[:, :, :, 64:96]
                u, v = fold(scratch[:, 1536:1792], NT, 4, 32), fold(scratch[:, 1792:2048], NT, 4, 32)
                c4, s4 = (m.rearrange("p t (h d) -> p t h d", h=4) for m in (mc, ms))
                nc.vector.tensor_tensor(u, qr, c4, ALU.mult)
                for i in range(2):
                    a, b = slice(16 * i, 16 * i + 16), slice(16 - 16 * i, 32 - 16 * i)
                    nc.vector.tensor_tensor(v[:, :, :, a], qr[:, :, :, b], s4[:, :, :, a], ALU.mult)
                kr = fold(mckv, NT, 160)[:, :, P:160]
                ku, kv_ = fold(kr_tmp[:, 0], NT, 32), fold(kr_tmp[:, 1], NT, 32)
                nc.vector.tensor_tensor(ku, kr, mc[:, :, 0:32], ALU.mult)
                for i in range(2):
                    a, b = slice(16 * i, 16 * i + 16), slice(16 - 16 * i, 32 - 16 * i)
                    nc.vector.tensor_tensor(kv_[:, :, a], kr[:, :, b], ms[:, :, a], ALU.mult)
                nc.vector.drain()
                nc.vector.tensor_tensor(qr, u, v, ALU.add)
                nc.vector.tensor_tensor(kr, ku, kv_, ALU.add)
                nc.vector.tensor_copy(fold(kcat, NT, 4, 96)[:, :, :, 0:64], fold(kvr, NT, 4, P)[:, :, :, 0:64])
                nc.vector.drain()
                nc.vector.tensor_copy(fold(kcat, NT, 4, 96)[:, :, :, 64:96],
                                      kr.unsqueeze(2).to_broadcast([P, NT, 4, 32])).then_inc(ml_rope, 1)
                dve.wait_ge(na_ready, l + 1)
                dve_items(dve, l * 20, heads1())
                dh = rows[:, :, 256:512]
                dh4 = dh.rearrange("p t (h d) -> p t h d", h=4)
                nc.vector.drain()
                nc.vector.tensor_tensor(fold(naq, NT, 256), dh, dh, ALU.mult)
                nc.vector.tensor_scalar(nak[:, 0:HD], prow[:, 0:64], prow[:, 321:322], None, ALU.mult)
                nc.vector.drain()
                nc.vector.tensor_reduce(out=gs[:, 0, 0:8], in_=fold(naq, 8, HD), op=ALU.add, axis=AX.X).then_inc(sub_sum, 1)
                dve.wait_ge(sub_std, l + 1)
                nc.vector.reciprocal(gs[:, 2, 0:8], gs[:, 1, 0:8])
                nc.vector.drain()
                nc.vector.tensor_tensor(dh4, dh4, fold(gs[:, 2, 0:8], NT, 4).unsqueeze(3).to_broadcast([P, NT, 4, HD]), ALU.mult)
                nc.vector.drain()
                nc.vector.tensor_tensor(dh4, dh4, nak[:, 0:HD].unsqueeze(1).unsqueeze(1).to_broadcast([P, NT, 4, HD]),
                                        ALU.mult).then_inc(mix_ready, 1)
                dve_split(dve, 3 * l + 1, ps8)
                for j in range(4):
                    dve_lo(dve, l, C1_O + j + SPLIT)
                dve_post(dve, 2 * l)
                dve_norm(dve, 2 * l + 1, 3 * l + 2)
                dve_ffn(dve, l, C1_FFN, l, 0, l)
                dve_post(dve, 2 * l + 1)
            nc.vector.tensor_scalar(nsink[:], prow2[:, 0:32], -1.0, None, ALU.mult)
            for n in range(n2):
                kind, c0, b0, g = KINDS2[n], BASE2[n], bank0[n], DEPTH1 + n
                nin = len(IN2[kind])
                nc.vector.scalar_tensor_tensor(out=acol[:, 0:8], in0=mod[:, n, 8:16], scalar=1.0,
                                               in1=pcol2[:, 16 * n:16 * n + 8], op0=ALU.add, op1=ALU.mult)
                nc.vector.scalar_tensor_tensor(out=acol[:, 8:16], in0=mod[:, n, 32:40], scalar=1.0,
                                               in1=pcol2[:, 16 * n + 8:16 * n + 16], op0=ALU.add, op1=ALU.mult).then_inc(acol_ready, 1)
                dve_norm(dve, 2 * g, 3 * g)
                dve.wait_ge(cb2_loaded, 16)
                {"swa": dve_swa, "gla": dve_gla, "fox": dve_fox}[kind](dve, n, c0, b0)
                dve_split(dve, 3 * g + 1, ps8)
                for j in range(4):
                    dve_lo(dve, DEPTH1, c0 + nin + j + SPLIT)
                dve_gated(dve, n, 0, c0 + nin + 3)
                dve_norm(dve, 2 * g + 1, 3 * g + 2)
                dve_ffn(dve, DEPTH1, c0 + nin + 4, g, (b0 + nin) % 2, g if g < ADA_LAYERS else None)
                dve_gated(dve, n, 1, c0 + nin + 4 + FFN_UNITS - 1)
            m = 2 * (DEPTH1 + n2)
            if n2 == DEPTH2:
                dve.wait_ge(gain_loaded, 16 * 5)
            for t in range(NT):
                dve.wait_ge(std_ready, NT * m + t + 1)
                nc.vector.reciprocal(rs[:, t:t + 1], sd[:, t:t + 1])
                nc.vector.drain()
                if n2 == DEPTH2:
                    last = nc.vector.scalar_tensor_tensor(out=rows[:, t], in0=x[:, t], scalar=rs[:, t:t + 1], in1=gain[:],
                                                          op0=ALU.mult, op1=ALU.mult)
                else:
                    last = nc.vector.tensor_copy(rows[:, t], x[:, t])
                last.then_inc(out_ready, 1)

def _unit(a):
    k, n = a.shape[0] // P, a.shape[1]
    u = np.zeros((P, UNIT), np.float32)
    u[:, :k * n] = a.reshape(k, P, n).transpose(1, 0, 2).reshape(P, k * n)
    return u


def _cols(v):
    return v.reshape(-1, P).T


def _ffn_units(gu, down):
    out = []

    def f_unit(f):
        c = slice(f * P, (f + 1) * P)
        return _unit(np.concatenate([gu[:, :DFF][:, c], gu[:, DFF:][:, c]], 1))

    out += [f_unit(0), f_unit(1)]
    for s in range(1, NF // 2):
        out += [f_unit(2 * s), f_unit(2 * s + 1), _unit(down[(s - 1) * 256:s * 256])]
    return out + [_unit(down[-256:])]


def _column_units(a, n=None):
    return [_unit(a[:, i:i + 256]) for i in range(0, a.shape[1], 256)][:n]


def _weights(a):
    units = []
    for l in range(DEPTH1):
        win = a["w_in"][l]
        q = win[:, 1536:1792].reshape(D, 4, HD)[:, [0, 2, 1, 3]].reshape(D, 256)
        win = np.concatenate([win[:, :1536], q, win[:, 1792:]], 1)
        units += _column_units(win)
        small = np.zeros((P, UNIT), np.float32)
        small[:, :768] = a["mla_w_uq"][l].reshape(2, P, 384).transpose(1, 0, 2).reshape(P, 768)
        small[:, 768:1280] = a["mla_w_ukv"][l]
        units.append(small)
        units += _column_units(a["w_o"][l]) + _ffn_units(a["ffn_w_gate_up"][l], a["ffn_w_down"][l])
    seen = {"swa": 0, "gla": 0, "fox": 0}
    for n, kind in enumerate(KINDS2):
        i = seen[kind]
        seen[kind] += 1
        win = a[f"{kind}_w_in_2"][i]
        if kind == "swa":
            order = [(2 * (c // 4) + half) * 4 + c % 4 for c in range(8) for half in range(2)]
            q = win[:, :D].reshape(D, 16, HD)[:, order].reshape(D, D)
            units += _column_units(np.concatenate([q, win[:, D:]], 1))
        elif kind == "gla":
            low = np.zeros((D, P), np.float32)
            low[:, :16] = win[:, 3072:]
            units += _column_units(win[:, :1024]) + [_unit(low)] + _column_units(win[:, 1024:3072])
        else:
            units += _column_units(win)
        units += _column_units(a[f"{kind}_w_o_2"][i]) + _ffn_units(a["ffn_w_gu_2"][n], a["ffn_w_down_2"][n])
    return np.stack(units)


def _constants():
    tok = np.arange(SEQ)

    def by_tile(t):
        return t.reshape(NT, P, -1).transpose(1, 0, 2).reshape(P, -1).astype(np.float32)

    def turn(pos, d, theta, old=True):
        inv = (np.float32(theta) ** (-np.arange(0, d, 2, dtype=np.float32) / np.float32(d))).astype(np.float32)
        ang = (pos.astype(np.float32)[:, None] * inv[None]).astype(np.float32).astype(np.float64)
        return np.concatenate([np.cos(ang)] * 2, 1), np.concatenate([-np.sin(ang), np.sin(ang)], 1)

    rc, rs_ = turn(tok // GRID, 32, 10000.0)
    cc, cs = turn(tok % GRID, 32, 10000.0)
    ax_c, ax_s = np.tile(np.concatenate([rc, cc], 1), (1, 4)), np.tile(np.concatenate([rs_, cs], 1), (1, 4))
    mc, ms = (np.tile(v, (1, 4)) for v in turn(tok, 32, 10000.0))
    dist = -np.abs(tok[:, None] - tok[None])
    cq, ck = (np.arange(P) % GRID)[:, None], np.arange(GRID)[None]
    start = np.clip(cq - 8, 0, GRID - 16)
    na = np.where((ck >= start) & (ck < start + 16), 0.0, NEG)
    c1 = np.concatenate([by_tile(dist), na, by_tile(ax_c), by_tile(ax_s), by_tile(mc), by_tile(ms)], 1)
    sc, ss_ = (np.tile(v, (1, 4)) for v in turn(tok, HD, 150000.0))
    q, k = tok[:, None], tok[None]
    causal = np.where(k <= q, 0.0, NEG)
    window = np.where((k <= q) & (k > q - P), 0.0, NEG)
    upto = (q <= k).astype(np.float32)
    s, t = np.arange(P)[:, None], np.arange(P)[None]
    same = s // 64 == t // 64
    levels = [(s == t)]
    for lv in range(1, 7):
        m = 64 >> lv
        levels.append((s // (2 * m) == t // (2 * m)) & (s % (2 * m) < m) & (t % (2 * m) >= m))
    c2 = np.concatenate([by_tile(sc), by_tile(ss_), by_tile(causal), by_tile(window), by_tile(upto), same & (s <= t),
                         *levels], 1)
    assert c1.shape[1] == NCB1 and c2.shape[1] == NCB2
    return np.ascontiguousarray(c1, np.float32), np.ascontiguousarray(c2, np.float32)


def layout(a):
    c1, c2 = _constants()
    ada = a["ada_w_2"].reshape(4, 2, 4, P, 12, ADA).transpose(0, 4, 1, 3, 2, 5).reshape(96, P, UNIT)
    lam = [0.8 - 0.6 * math.exp(-0.3 * l) for l in range(DEPTH1)]
    row1 = np.stack([np.concatenate([a["diff_subln"][l], a["gqa_q_norm"][l], a["gqa_k_norm"][l],
                                     a["diff_lambda_q1"][l], a["diff_lambda_q2"][l], a["diff_lambda_k1"][l],
                                     a["diff_lambda_k2"][l], np.float32([lam[l], 1.0 - lam[l]])]) for l in range(DEPTH1)])
    col1 = np.stack([np.concatenate([_cols(a["pre_mix_norm"][l]), _cols(a["pre_ffn_norm"][l]),
                                     _cols(a["mla_q_norm"][l]), _cols(a["mla_kv_norm"][l])], 1) for l in range(DEPTH1)])
    col2 = np.concatenate([_cols(a["norm_gain_2"][n, i]) for n in range(DEPTH2) for i in range(2)], 1)
    row2 = np.concatenate([a["swa_sinks_2"].reshape(-1), a["fox_b_f_2"].reshape(-1), a["gla_head_norm_2"].reshape(-1)])
    x = a["x"][0].reshape(NT, P, D).transpose(1, 0, 2)
    return {
        "wts": _weights(a), "ada": ada, "ada_b": _cols(a["ada_b_2"]).reshape(P, 4, 48), "x_in": x, "c_col": _cols(a["c_2"][0]),
        "rel_bias": a["na_rel_bias"], "col1": col1, "row1": row1, "gain_mix": a["post_mix_norm"],
        "gain_ffn": a["post_ffn_norm"], "col2": col2, "row2": row2, "gate_w": a["gla_w_gate_up_2"][0],
        "gate_b": a["gla_b_gate_2"], "final_gain": a["final_norm_2"].reshape(1, D), "ident_in": np.eye(P, dtype=np.float32),
        "cst1": c1, "cst2": c2,
    }


def kernel(**inputs):
    import concourse.bacc as bacc
    from concourse.bass_utils import run_bass_kernel_spmd

    arrays = {k: np.ascontiguousarray(v, np.float32) for k, v in layout({k: np.asarray(v) for k, v in inputs.items()}).items()}
    nc = bacc.Bacc("TRN2", target_bir_lowering=False, num_devices=1)
    args = {k: nc.dram_tensor(k, v.shape, mybir.dt.float32, kind="ExternalInput").ap() for k, v in arrays.items()}
    out = nc.dram_tensor("out", (P, NT, D), mybir.dt.float32, kind="ExternalOutput").ap()
    build(nc, **args, out=out)
    r = run_bass_kernel_spmd(nc, [arrays], core_ids=[0])
    return r.results[0]["out"].transpose(1, 0, 2).reshape(1, SEQ, D)
```

```python
import math
from contextlib import ExitStack

import numpy as np
import concourse.bass as bass
from concourse import mybir

P = 128
D = 1024
SEQ = 256
NT = SEQ // P
KT = D // P
HD = 64
DFF = 2816
NF = DFF // P
GRID = 64
DEPTH1, DEPTH2 = 2, 4
EPS = 1e-6
NEG = -1.0e30

UNIT = 2048
RAW = 6
SPLIT = 2
C1_SMALL, C1_O, C1_FFN = 7, 11, 15
W_IN1 = (8, 9, 6, 7, 0, 1, 2, None, 3, 4, 5)
FFN_UNITS = NF + NF // 2
PER1 = C1_FFN + FFN_UNITS
SIZES1 = [{9: KT * 160, None: 2 * 384 + 512}.get(u, UNIT) for u in W_IN1] + [UNIT] * (4 + FFN_UNITS)
IN2 = {"swa": [UNIT] * 6, "gla": [UNIT] * 4 + [KT * P] + [UNIT] * 8, "fox": [KT * 16] + [UNIT] * 12}
KINDS2 = ["swa", "gla", "fox", "swa"]
BASE2, SIZES2 = [], []
for _kind in KINDS2:
    BASE2.append(len(SIZES2))
    SIZES2 += IN2[_kind] + [UNIT] * (4 + FFN_UNITS)
UNITS = DEPTH1 * PER1 + len(SIZES2)
STEPS = NF // 2 + 1
ADA = UNIT // 4
ADA_LAYERS = 4

ROW1 = {"subln": (0, 64), "gq": (64, 128), "gk": (128, 192), "lq": (192, 256), "lk": (256, 320), "lam": (320, 322)}
NROW1 = 322
COL1 = {"pre_mix": 0, "pre_ffn": 8, "mla_q": 16, "mla_kv": 18}
NCOL1 = 19
CB1 = {"dist": (0, 512), "na": (512, 576), "rope_c": (576, 1088), "rope_s": (1088, 1600),
       "mla_c": (1600, 1856), "mla_s": (1856, 2112)}
NCB1 = 2112
CB2 = {"rope_c": (0, 512), "rope_s": (512, 1024), "causal": (1024, 1408), "window": (1408, 1792),
       "upto": (1792, 2304), "upto64": (2304, 2432), "level": (2432, 2432 + 7 * 128)}
NCB2 = 2432 + 7 * 128
NROW2 = 2 * 16 + 16 + 256
WORK = 10560


def build(nc, wts, ada, ada_b, x_in, c_col, rel_bias, col1, row1, gain_mix, gain_ffn, col2, row2,
          gate_w, gate_b, final_gain, ident_in, cst1, cst2, out):
    f32, f32r = mybir.dt.float32, mybir.dt.float32r
    ALU, ACT, AX = mybir.AluOpType, mybir.ActivationFunctionType, mybir.AxisListType
    ctx = ExitStack()
    with ctx:
        def sb(name, shape, dt=f32):
            return ctx.enter_context(nc.sbuf_tensor(name, shape, dt))

        def sem(name):
            return ctx.enter_context(nc.semaphore(name))

        raw = sb("raw", [P, RAW, UNIT])
        whi = sb("whi", [P, SPLIT, UNIT], f32r)
        wlo = sb("wlo", [P, SPLIT, UNIT], f32r)
        ada_raw = sb("ada_raw", [P, 2, UNIT])
        ada_acc = sb("ada_acc", [P, 2, ADA])
        h32 = sb("h32", [P, 2, SEQ])
        hhi = sb("hhi", [P, KT, SEQ], f32r)
        hlo = sb("hlo", [P, KT, SEQ], f32r)
        x = sb("x", [P, NT, D])
        rows = sb("rows", [P, NT, D])
        gain = sb("gain", [P, D])
        cb = sb("cb", [P, max(NCB1, NCB2)])
        ident = sb("ident", [P, P])
        ones = sb("ones", [P, P])
        spare = sb("spare", [P, 1])
        pcol = sb("pcol", [P, NCOL1])
        prow = sb("prow", [P, NROW1])
        pcol2 = sb("pcol2", [P, DEPTH2 * 16])
        prow2 = sb("prow2", [P, NROW2])
        ccol = sb("ccol", [P, KT])
        nsink = sb("nsink", [P, 32])
        kr_tmp = sb("kr_tmp", [P, 2, 64])
        mod = sb("mod", [P, ADA_LAYERS, 48])
        acol = sb("acol", [P, 16])
        zcol = sb("zcol", [P, 1])
        epsc = sb("epsc", [P, 1])
        ss = sb("ss", [P, 4])
        sd = sb("sd", [P, 4])
        rs = sb("rs", [P, 4])
        gs = sb("gs", [P, 3, 16])
        lamt = sb("lamt", [P, 8])
        nmax = sb("nmax", [P, 4, NT])
        psum_ = sb("psum_", [P, 4, NT])
        esink = sb("esink", [P, 4, NT])
        rsum = sb("rsum", [P, 4, NT])
        work = sb("work", [P, WORK])
        ahi = sb("ahi", [P, 4, SEQ], f32r)
        alo = sb("alo", [P, 4, SEQ], f32r)
        zeros = sb("zeros", [P, P], mybir.dt.bfloat16)

        def w(at, n):
            return work[:, at:at + n]

        def fold(ap, *shape):
            names = "abcde"[:len(shape)]
            spec = " ".join(names)
            return ap.rearrange(f"p ({spec}) -> p {spec}", **dict(zip(names, shape)))

        dense_bias = nc.dram_tensor("dense_bias", (DEPTH1, P, UNIT), f32, kind="Internal").ap()

        psu = ctx.enter_context(nc.psum_tensor("psu", [P, 2, 512], f32))
        pso = ctx.enter_context(nc.psum_tensor("pso", [P, 512], f32))
        psm = ctx.enter_context(nc.psum_tensor("psm", [P, 512], f32))
        psy = ctx.enter_context(nc.psum_tensor("psy", [P, 4, 512], f32))
        banks_o = [pso, psm]
        ps8 = psy[:].rearrange("p b (c n) -> p (b c) n", c=2)
        psy2 = psy[:].rearrange("p (t b) n -> p t (b n)", t=NT)

        naq, nak, nav, dfq, dfk, dfv, gqr = (w(512 * i, 512) for i in range(7))
        gkr, gv, mcq, mckv = w(3584, 256), w(3840, 256), w(4096, 512), w(4608, 320)
        kvr, qcT, kcT = w(4928, 1024), w(5952, 1024), w(6976, 1024)
        prob, probT = fold(w(8000, 1024), 2, 512), fold(w(9024, 1024), 2, 512)
        gqT, gkT = w(10048, 512), gkr
        hw = fold(w(1024, KT * SEQ), KT, SEQ)
        sg, a32 = fold(w(0, 512), 2, SEQ), fold(w(512, 512), 2, SEQ)
        scratch = rows[:].rearrange("p t n -> p (t n)")
        qf, kcat = scratch[:, 0:768], scratch[:, 768:1536]
        wgu, bgate = work[0:16, 9216:9728], work[0:1, 9728:10240]
        

        COLS1 = (0, 1, 3, 4)
        bank0 = [DEPTH1 * 32]
        for kind in KINDS2:
            bank0.append(bank0[-1] + len(IN2[kind]) + NF)
        item0 = [DEPTH1 * 20 + 16 * i for i in (0, 1, 1, 2)]

        start_loads = sem("start_loads")
        c_loaded = sem("c_loaded")
        cb1_loaded = sem("cb1_loaded")
        pool_loads = sem("pool_loads")
        filled = sem("filled")
        cb2_loaded = sem("cb2_loaded")
        raw_loaded = [sem(f"raw_loaded{i}") for i in range(RAW)]
        ada_loaded = [sem(f"ada_loaded{i}") for i in range(2)]
        ada_used = [sem(f"ada_used{i}") for i in range(2)]
        ada_mm = sem("ada_mm")
        ada_evac = sem("ada_evac")
        hi_done = sem("hi_done")
        lo_done = sem("lo_done")
        unit_mm = sem("unit_mm")
        bank_free = sem("bank_free")
        x_ready = sem("x_ready")
        std_ready = sem("std_ready")
        y_ready = sem("y_ready")
        xn_ready = sem("xn_ready")
        tr_done = sem("tr_done")
        hhi_done = sem("hhi_done")
        h_ready = sem("h_ready")
        ystd_ready = sem("ystd_ready")
        par_loaded = sem("par_loaded")
        gain_loaded = sem("gain_loaded")
        bias_spread = sem("bias_spread")
        na_loaded = sem("na_loaded")
        na_ready = sem("na_ready")
        silu_done = sem("silu_done")
        a_ready = sem("a_ready")
        s_done = sem("s_done")
        max_ready = sem("max_ready")
        p_ready = sem("p_ready")
        t_done = sem("t_done")
        pt_ready = sem("pt_ready")
        o_done = sem("o_done")
        o_evac = sem("o_evac")
        mix_ready = sem("mix_ready")
        gq_evac = sem("gq_evac")
        gq_sum = sem("gq_sum")
        gq_std = sem("gq_std")
        gq_rope = sem("gq_rope")
        gq_tr = sem("gq_tr")
        ml_std = sem("ml_std")
        ml_norm = sem("ml_norm")
        ml_tr = sem("ml_tr")
        ml_hi = sem("ml_hi")
        ml_h = sem("ml_h")
        ml_evac = sem("ml_evac")
        ml_rope = sem("ml_rope")
        ml_ctr = sem("ml_ctr")
        qk_ready = sem("qk_ready")
        sub_sum = sem("sub_sum")
        sub_std = sem("sub_std")
        swa_rope = sem("swa_rope")
        swa_tr = sem("swa_tr")
        swa_evac = sem("swa_evac")
        gate_mm = sem("gate_mm")
        gate_bcast = sem("gate_bcast")
        fox_l = sem("fox_l")
        fox_lf = sem("fox_lf")
        fox_c = sem("fox_c")
        fox_ce = sem("fox_ce")
        fox_row = sem("fox_row")
        g_logit = sem("g_logit")
        g_ln = sem("g_ln")
        g_la = sem("g_la")
        g_cum = sem("g_cum")
        g_b = sem("g_b")
        g_e = sem("g_e")
        g_x = sem("g_x")
        g_qk = sem("g_qk")
        g_s = sem("g_s")
        g_acc = sem("g_acc")
        g_sum = sem("g_sum")
        g_dec = sem("g_dec")
        g_dex = sem("g_dex")
        g_kd = sem("g_kd")
        g_kt = sem("g_kt")
        g_kr = sem("g_kr")
        g_ds = sem("g_ds")
        g_st = sem("g_st")
        g_o = sem("g_o")
        g_std = sem("g_std")
        g_silu = sem("g_silu")
        g_r = sem("g_r")
        gate_loaded = sem("gate_loaded")
        start_act = sem("start_act")
        acol_ready = sem("acol_ready")
        stored = sem("stored")
        out_ready = sem("out_ready")

        def unit_no(l, c, i=0):
            return l * PER1 + c + i * RAW

        def size_of(l, c):
            if isinstance(l, int) and l == DEPTH1:
                return SIZES2[c]
            return SIZES1[c % PER1] if c >= 0 else 0

        def past_end(l, c):
            return isinstance(l, int) and l == DEPTH1 and c >= len(SIZES2)

        def turns(engine, turn, last):
            with engine.Fori(0, 4 if last else 5) as i:
                turn(i)
            if last:
                turn(4)

        def slot_of(c):
            return c % RAW

        def part_of(c):
            return c % SPLIT

        def load_unit(sp, l, c, i=0, first=False):
            if past_end(l, c + RAW * i if isinstance(i, int) else c):
                return
            n = size_of(l, c)
            if not first:
                sp.wait_ge(lo_done, unit_no(l, c, i) - RAW + 1)
            u = unit_no(l, c, i)
            src = wts[u] if isinstance(u, int) else wts[bass.ds(u, 1)][0]
            sp.dma_start(raw[:, slot_of(c), 0:n], src[:, 0:n]).then_inc(raw_loaded[slot_of(c)], 16)

        def load_ada(sp, a, s):
            first = isinstance(s, int) and s == 0
            no = a * STEPS + s
            for half in range(2):
                if not first or (isinstance(a, int) and a > 0):
                    sp.wait_ge(ada_used[half], no)
                at = (a * STEPS + s) * 2 + half
                src = ada[at] if isinstance(at, int) else ada[bass.ds(at, 1)][0]
                sp.dma_start(ada_raw[:, half], src).then_inc(ada_loaded[half], 16)

        def sp_ffn(sp, l, c0, a):
            for c in (c0, c0 + 1):
                load_unit(sp, l, c + RAW)
            def turn(i):
                for k in range(2):
                    if a is not None:
                        load_ada(sp, a, 2 + 2 * i + k)
                    for j in range(3):
                        load_unit(sp, l, c0 + 2 + 3 * k + j + RAW, i)

            turns(nc.sync, turn, past_end(l, c0 + 33))
            load_unit(sp, l, c0 + 32 + RAW)

        block = ctx.enter_context(nc.Block())

        @block.sync
        def _(sp):
            sp.dma_start(x[:], x_in).then_inc(start_loads, 16)
            sp.dma_start(ident[:], ident_in).then_inc(start_loads, 16)
            load_unit(sp, 0, 0, first=True)
            sp.wait_ge(par_loaded, 32)
            for c in range(1, RAW):
                load_unit(sp, 0, c, first=True)
            sp.dma_start(cb[:, 0:NCB1], cst1).then_inc(cb1_loaded, 16)
            with nc.sync.Fori(0, DEPTH1) as l:
                for c in range(RAW, C1_FFN + RAW):
                    load_unit(sp, l, c)
                    if c == C1_O:
                        sp.wait_ge(x_ready, 4 * l + 2)
                        sp.wait_ge(bias_spread, 16 * 16 * DEPTH1)
                        sp.dma_start(ada_raw[:, 0, :], dense_bias[bass.ds(l, 1)][0]).then_inc(na_loaded, 16)
                    if c == C1_O + 1 + RAW:
                        sp.wait_ge(max_ready, l * 20 + 4)
                        load_ada(sp, l, 0)
                        load_ada(sp, l, 1)
                sp_ffn(sp, l, C1_FFN, l)
            for n in range(DEPTH2):
                c0 = BASE2[n]
                nin = len(IN2[KINDS2[n]]) + 4
                for c in range(c0, c0 + nin):
                    load_unit(sp, DEPTH1, c + RAW)
                    if n == 0 and c == c0 + 1:
                        load_ada(sp, 2, 0)
                        load_ada(sp, 2, 1)
                if n == 1:
                    sp.wait_ge(mix_ready, DEPTH1 + 1)
                    load_ada(sp, 3, 0)
                    load_ada(sp, 3, 1)
                sp_ffn(sp, DEPTH1, c0 + nin, 2 + n if n < 2 else None)
            for t in range(NT):
                sp.wait_ge(out_ready, t + 1)
                sp.dma_start(out[:, t], rows[:, t]).then_inc(stored, 16)
            sp.wait_ge(stored, 16 * NT)

        def pool_weigh(pool, a, s, slot):
            no = a * STEPS + s
            if not isinstance(no, int) or no >= 2:
                pool.wait_ge(ada_mm, no - 1)
            acc = ada_acc[:, slot]
            tt = nc.gpsimd.tensor_tensor
            for half in range(2):
                pool.wait_ge(ada_loaded[half], 16 * (no + 1))
                tiles = fold(ada_raw[:, half], 4, ADA)
                c = ccol[:, 4 * half:4 * half + 4].unsqueeze(2).to_broadcast([P, 4, ADA])
                tt(tiles, tiles, c, ALU.mult)
                nc.gpsimd.drain()
                tt(tiles[:, 0:2], tiles[:, 0:2], tiles[:, 2:4], ALU.add)
                if half == 1:
                    nc.gpsimd.drain()
                    tt(tiles[:, 0], tiles[:, 0], acc, ALU.add)
                nc.gpsimd.drain()
                tt(acc, tiles[:, 0], tiles[:, 1], ALU.add).then_inc(ada_used[half], 1)

        def pool_ada(pool, a):
            with nc.gpsimd.Fori(0, 5) as i:
                pool_weigh(pool, a, 2 + 2 * i, 0)
                pool_weigh(pool, a, 3 + 2 * i, 1)

        def spread_biases(pool):
            for l in range(DEPTH1):
                for t in range(NT):
                    for r in range(2):
                        for h in range(4):
                            at = (l * 4 + h) * 465 + (7 - 2 * t - r) * 31 + 15
                            src = bass.AP(rel_bias.tensor, at, [[31, 4], [-1, 64], [1, 64]])
                            dst = fold(dense_bias[l, 64 * r:64 * r + 64, :], NT, 4, 4, 64)[:, t, h]
                            dst = dst.rearrange("q r c -> r q c")
                            pool.dma_start(dst, src).then_inc(bias_spread, 16)

        @block.gpsimd
        def _(pool):
            nc.gpsimd.memset(ones[:], 1.0).then_inc(filled, 1)
            nc.gpsimd.memset(epsc[:], EPS).then_inc(filled, 1)
            nc.gpsimd.memset(zcol[:], 0.0).then_inc(filled, 1)
            nc.gpsimd.memset(zeros[:], 0.0).then_inc(filled, 1)
            pool.dma_start(ccol[:], c_col).then_inc(c_loaded, 16)
            for l in range(DEPTH1):
                if l > 0:
                    pool.wait_ge(h_ready, 24 * l)
                pool.dma_start(pcol[:], col1[l]).then_inc(par_loaded, 16)
                pool.dma_start(prow[:], row1[l].partition_broadcast(P)).then_inc(par_loaded, 16)
                if l == 0:
                    spread_biases(pool)
                    pool.dma_start(mod[:], ada_b).then_inc(pool_loads, 16)
                    pool.dma_start(pcol2[:], col2).then_inc(pool_loads, 16)
                    pool.dma_start(prow2[:], row2.partition_broadcast(P)).then_inc(pool_loads, 16)
                pool.wait_ge(x_ready, 2 + 4 * l)
                pool.dma_start(gain[:], gain_mix[l].partition_broadcast(P)).then_inc(gain_loaded, 16)
                pool.wait_ge(na_loaded, 16 * (l + 1))
                pool.wait_ge(cb1_loaded, 16)
                nb = fold(ada_raw[:, 0, :], 32, 64)
                mask = cb[:, CB1["na"][0]:CB1["na"][1]]
                nc.gpsimd.tensor_tensor(nb, nb, mask.unsqueeze(1).to_broadcast([P, 32, 64]), ALU.add).then_inc(na_ready, 1)
                if l == 0:
                    pool.wait_ge(start_act, 1)
                pool_weigh(pool, l, 0, 0)
                pool_weigh(pool, l, 1, 1)
                pool.wait_ge(x_ready, 2 + 4 * l + 2)
                pool.dma_start(gain[:], gain_ffn[l].partition_broadcast(P)).then_inc(gain_loaded, 16)
                pool_ada(pool, l)
            pool.dma_start(cb[:, 0:NCB2], cst2).then_inc(cb2_loaded, 16)
            pool_weigh(pool, DEPTH1, 0, 0)
            pool_weigh(pool, DEPTH1, 1, 1)
            pool.wait_ge(o_evac, item0[0] + 16)
            pool.dma_start(wgu, gate_w).then_inc(gate_loaded, 16)
            pool.dma_start(bgate, gate_b).then_inc(gate_loaded, 16)
            for n in range(2):
                if n == 1:
                    for lv in range(1, 7):
                        pool.wait_ge(g_acc, lv + 1)
                        nc.gpsimd.tensor_tensor(scratch[:, 0:1024], scratch[:, 0:1024], scratch[:, 1024:2048], ALU.add).then_inc(g_sum, 1)
                        nc.gpsimd.drain()
                if n > 0:
                    pool_weigh(pool, DEPTH1 + n, 0, 0)
                    pool_weigh(pool, DEPTH1 + n, 1, 1)
                pool_ada(pool, DEPTH1 + n)
            pool.wait_ge(x_ready, 2 + 4 * (DEPTH1 + DEPTH2))
            pool.dma_start(gain[:], final_gain[0].partition_broadcast(P)).then_inc(gain_loaded, 16)

        mm = nc.tensor.matmul

        def pe_unit_cols(pe, c, bank, n=2, q=None):
            k = part_of(c)
            width = n * P
            last = None

            def product(kt, cc, start):
                cols = slice(kt * width + cc * P, kt * width + cc * P + P)
                for j, (a, h) in enumerate(((whi, hhi), (whi, hlo), (wlo, hhi))):
                    m = mm(psu[:, bank, cc * SEQ:(cc + 1) * SEQ], a[:, k, cols], h[:, kt, :],
                           start=(start and j == 0), stop=(kt == KT - 1 and j == 2), skip_group_check=q is not None)
                return m

            if q is not None:
                for kt in range(KT):
                    if kt % 2 == 0:
                        pe.wait_ge(h_ready, 8 * q + kt + 2)
                    for cc in range(n):
                        last = product(kt, cc, kt == 0 and cc == 0)
            else:
                for cc in range(n):
                    for kt in range(KT):
                        last = product(kt, cc, kt == 0)
            return last

        def pe_unit_rows(pe, c, width, outs, q=None, y_after=False):
            k = part_of(c)
            last = None
            for t in range(NT):
                for kt in range(KT):
                    if q is not None and t == 0 and kt % 2 == 0:
                        pe.wait_ge(h_ready, 8 * q + kt + 2)
                    toks = slice(t * P, t * P + P)
                    for j, (h, a) in enumerate(((hhi, whi), (hlo, whi), (hhi, wlo))):
                        last = mm(outs[t], h[:, kt, toks], a[:, k, kt * width:(kt + 1) * width],
                                  start=(kt == 0 and j == 0), stop=(kt == KT - 1 and j == 2))
                if y_after and t == 0:
                    last.then_inc(y_ready, 1)
            return last

        def pe_in_unit(pe, l, c, j, bank, kind, q, width=256):
            pe.wait_ge(lo_done, unit_no(l, c) + 1)
            if j >= 2:
                pe.wait_ge(bank_free, bank - 1)
            b = (bank if isinstance(bank, int) else j) % 2
            if kind == "cols":
                last = pe_unit_cols(pe, c, b, width // P, q if j == 0 else None)
            else:
                last = pe_unit_rows(pe, c, width, [psu[:, b, t * width:(t + 1) * width] for t in range(NT)],
                                    q if j == 0 else None)
            last.then_inc(unit_mm, 1)

        def pe_transpose(pe, q):
            for kt in range(KT):
                for t in range(NT):
                    last = nc.tensor.transpose(ps8[:, kt, t * P:(t + 1) * P],
                                               rows[:, t, kt * P:(kt + 1) * P], ident[:])
                last.then_inc(tr_done, 1)

        def pe_norm(pe, m, q):
            def turned(kt, t):
                return mm(ps8[:, kt, t * P:(t + 1) * P], x[:, t, kt * P:(kt + 1) * P], rows[:, t, 0:P],
                          start=True, stop=True)

            pe.wait_ge(xn_ready, NT * m + 1)
            for kt in range(4):
                turned(kt, 0)
            pe.wait_ge(xn_ready, NT * m + 2)
            for kt in range(KT):
                if kt >= 4:
                    turned(kt, 0)
                turned(kt, 1).then_inc(tr_done, 1)

        def pe_out(pe, l, c0, n, ready):
            pe.wait_ge(*ready)
            pe_transpose(pe, 3 * n + 1)
            for j in range(4):
                pe.wait_ge(lo_done, unit_no(l, c0 + j) + 1)
                last = pe_unit_rows(pe, c0 + j, 256, [psy2[:, t, j * 256:(j + 1) * 256] for t in range(NT)],
                                    3 * n + 1 if j == 0 else None, y_after=(j == 3))
                last.then_inc(unit_mm, 1)

        def pe_ada(pe, a, s, slot):
            no = a * STEPS + s
            pe.wait_ge(ada_used[1], no + 1)
            if not isinstance(s, int) or s > 0:
                pe.wait_ge(ada_evac, no)
            for j in range(4):
                last = mm(psm[:, j:j + 1], ada_acc[:, slot, j * P:(j + 1) * P], ones[:, 0:1], start=True, stop=True)
            last.then_inc(ada_mm, 1)

        def pe_ffn(pe, l, c0, n, bo, par, a, gated=False):
            def gu(c, i, f, bank, q=None):
                pe.wait_ge(lo_done, unit_no(l, c, i) + 1)
                pe.wait_ge(bank_free, bo + f - 1)
                pe_unit_cols(pe, c, bank, q=q).then_inc(unit_mm, 1)

            def dn(c, i, s, aslot, last_step=False):
                pe.wait_ge(lo_done, unit_no(l, c, i) + 1)
                pe.wait_ge(a_ready, n * NF + 2 * s + 2)
                k = part_of(c)
                for t in range(NT):
                    toks = slice(t * P, t * P + P)
                    for ff in range(2):
                        for half in range(2):
                            cols = slice(ff * 1024 + half * 512, ff * 1024 + half * 512 + 512)
                            for j, (h, b) in enumerate(((ahi, whi), (alo, whi), (ahi, wlo))):
                                last = mm(psy[:, 2 * t + half, :], h[:, aslot + ff, toks], b[:, k, cols],
                                          start=False, stop=(last_step and ff == 1 and j == 2),
                                          skip_group_check=True)
                    if last_step and t == 0:
                        last.then_inc(y_ready, 1)
                return last

            gu(c0, 0, 0, par, 3 * n + 2)
            gu(c0 + 1, 0, 1, 1 - par)
            for b in range(4):
                mm(fold(psy[:, b, :], 4, P), zeros[:], zeros[:].unsqueeze(1).to_broadcast([P, 4, P]),
                   start=True, stop=False, skip_group_check=True)
            if gated and a is not None:
                pe.wait_ge(gate_bcast, 2 * (n - DEPTH1) + 2)
            if a is not None:
                pe_ada(pe, a, 0, 0)
            with nc.tensor.Fori(0, 5) as i:
                for k in range(2):
                    c = c0 + 2 + 3 * k
                    gu(c, i, 2 + 4 * i + 2 * k, par)
                    gu(c + 1, i, 3 + 4 * i + 2 * k, 1 - par)
                    dn(c + 2, i, 2 * i + k, 2 * k).then_inc(unit_mm, 1)
                    if a is not None:
                        pe_ada(pe, a, 1 + 2 * i + k, 1 - k)
            dn(c0 + 32, 0, 10, 0, last_step=True).then_inc(unit_mm, 1)
            if a is not None:
                pe_ada(pe, a, 11, 1)

        def spans(it):
            return (slice(P if it["causal"] else 0, SEQ), slice(SEQ, 2 * SEQ))

        def blocks(it):
            return [(0, 0, P)] + [(1, kc, SEQ + kc * P) for kc in range(2)] if it["causal"] else [
                (t, kc, t * SEQ + kc * P) for t in range(NT) for kc in range(2)]

        def pe_items(pe, I0, items):
            def scores(k):
                it = items[k]
                if k >= 2:
                    pe.wait_ge(p_ready, I0 + k - 1)
                for t in range(NT):
                    span = spans(it)[t]
                    keys = slice(0, span.stop - span.start)
                    o = psy[:, k % 2, span]
                    last = mm(o, it["q"][:, t * P:(t + 1) * P], it["k"][:, keys], start=True, stop=it["add"] is None)
                    if it["add"] is not None:
                        last = mm(o, ones[0:1, 0:P], it["add"][:, keys], start=False, stop=True)
                last.then_inc(s_done, 1)

            def transposes(k):
                pe.wait_ge(p_ready, I0 + k + 1)
                if k >= 2:
                    pe.wait_ge(pt_ready, I0 + k - 1)
                for _, _, at in blocks(items[k]):
                    last = nc.tensor.transpose(psy[:, 2 + k % 2, at:at + P], prob[:, k % 2, at:at + P], ident[:])
                last.then_inc(t_done, 1)

            def values(k):
                pe.wait_ge(pt_ready, I0 + k + 1)
                if k >= 2:
                    pe.wait_ge(o_evac, I0 + k - 1)
                for t, kc, at in blocks(items[k]):
                    last = mm(banks_o[k % 2][:, t * HD:(t + 1) * HD], probT[:, k % 2, at:at + P],
                              items[k]["v"][kc], start=(kc == 0), stop=(kc == 1 or at == P))
                last.then_inc(o_done, 1)

            n = len(items)
            scores(0)
            for k in range(n):
                if k + 1 < n:
                    scores(k + 1)
                transposes(k)
                if k >= 1:
                    values(k - 1)
            values(n - 1)

        def act_items(act, I0, items):
            def copy(k):
                act.wait_ge(t_done, I0 + k + 1)
                if k >= 2:
                    act.wait_ge(o_done, I0 + k - 1)
                lo = spans(items[k])[0].start
                nc.scalar.copy(probT[:, k % 2, lo:], psy[:, 2 + k % 2, lo:]).then_inc(pt_ready, 1)

            n = len(items)
            act_table(ACT.Exp)
            for k in range(n):
                it = items[k]
                act.wait_ge(max_ready, I0 + k + 1)
                if it["bias"] is None and k >= 2:
                    act.wait_ge(t_done, I0 + k - 1)
                src = psy[:, k % 2] if it["bias"] is None else prob[:, k % 2]
                if it["sink"] is not None:
                    nc.scalar.activation(esink[:, k % 4], nmax[:, k % 4], ACT.Exp, bias=it["sink"])
                for t, span in enumerate(spans(it)):
                    last = nc.scalar.activation(prob[:, k % 2, span], src[:, span], ACT.Exp, bias=nmax[:, k % 4, t:t + 1],
                                                accum_out=psum_[:, k % 4, t:t + 1])
                last.then_inc(p_ready, 1)
                if k >= 1:
                    copy(k - 1)
            copy(n - 1)

        def dve_items(dve, I0, items):
            def maxima(k):
                it = items[k]
                dve.wait_ge(s_done, I0 + k + 1)
                src = psy[:, k % 2]
                if it["bias"] is not None:
                    if k >= 2:
                        dve.wait_ge(t_done, I0 + k - 1)
                    it["bias"](prob[:, k % 2], src)
                    nc.vector.drain()
                    src = prob[:, k % 2]
                if it["causal"]:
                    for t, span in enumerate(spans(it)):
                        last = nc.vector.tensor_reduce(out=nmax[:, k % 4, t:t + 1], in_=src[:, span], op=ALU.max,
                                                       axis=AX.X, negate=True)
                else:
                    last = nc.vector.tensor_reduce(out=nmax[:, k % 4], in_=fold(src, NT, SEQ), op=ALU.max,
                                                   axis=AX.X, negate=True)
                if it["sink"] is not None:
                    nc.vector.drain()
                    last = nc.vector.tensor_scalar(nmax[:, k % 4], nmax[:, k % 4], it["nsink"], None, ALU.min)
                last.then_inc(max_ready, 1)

            def divide(k):
                it = items[k]
                dve.wait_ge(o_done, I0 + k + 1)
                if it["sink"] is not None:
                    nc.vector.tensor_tensor(psum_[:, k % 4], psum_[:, k % 4], esink[:, k % 4], ALU.add)
                    nc.vector.drain()
                nc.vector.reciprocal(rsum[:, k % 4], psum_[:, k % 4])
                nc.vector.drain()

                def over(k, o):
                    src = fold(banks_o[k % 2][:, 0:P], NT, HD)
                    return nc.vector.tensor_tensor(o, src, rsum[:, k % 4].unsqueeze(2).to_broadcast([P, NT, HD]), ALU.mult)

                o = rows[:, :, it["col"]:it["col"] + HD]
                if it["pair"] is None:
                    over(k, o).then_inc(o_evac, 1)
                elif it["pair"] == 1:
                    nc.vector.tensor_scalar(rsum[:, k % 4], rsum[:, k % 4], lamt[:, 4:5], None, ALU.mult)
                    nc.vector.drain()
                    over(k - 1, o)
                    tmp = fold(h32[:, 0, 0:P], NT, HD)
                    over(k, tmp)
                    nc.vector.drain()
                    nc.vector.tensor_tensor(o, o, tmp, ALU.subtract).then_inc(o_evac, 2)

            n = len(items)
            for k in range(n + 2):
                if k < n:
                    maxima(k)
                if k >= 2:
                    divide(k - 2)

        def act_hi(act, l, c, i=0, first=False):
            if past_end(l, c + RAW * i if isinstance(i, int) else c):
                return
            n = size_of(l, c)
            u = unit_no(l, c, i)
            turn = (l * (PER1 // RAW) + i + c // RAW + 1) * 16
            act.wait_ge(raw_loaded[slot_of(c)], turn)
            if not first:
                act.wait_ge(unit_mm, u - SPLIT + 1)
            nc.scalar.copy(whi[:, part_of(c), 0:n], raw[:, slot_of(c), 0:n]).then_inc(hi_done, 1)

        def dve_lo(dve, l, c, i=0):
            if past_end(l, c + RAW * i if isinstance(i, int) else c):
                return
            n = size_of(l, c)
            dve.wait_ge(hi_done, unit_no(l, c, i) + 1)
            nc.vector.tensor_tensor(wlo[:, part_of(c), 0:n], raw[:, slot_of(c), 0:n],
                                    whi[:, part_of(c), 0:n].bitcast(f32), ALU.subtract).then_inc(lo_done, 1)

        def act_table(func):
            nc.scalar.activation(spare[:], epsc[:], func)

        def act_rms(t):
            nc.scalar.drain()
            return nc.scalar.activation(sd[:, t:t + 1], ss[:, t:t + 1], ACT.Sqrt, bias=epsc[:], scale=1.0 / D)

        def act_norm(act, m, q, scale, bias, l=None, c=None):
            for t in range(NT):
                act.wait_ge(x_ready, 2 * m + t + 1)
                nc.scalar.activation(rows[:, t], x[:, t], ACT.Square, accum_out=ss[:, t:t + 1])
                act_rms(t).then_inc(std_ready, 1)
            if q is None:
                return
            act_hi(act, l, c, first=True)
            for kt in range(0, KT, 2):
                act.wait_ge(tr_done, 8 * q + kt + 2)
                for k in (kt, kt + 1):
                    nc.scalar.activation(hw[:, k], ps8[:, k], ACT.Identity, scale=scale[:, k:k + 1],
                                         bias=zcol[:] if bias is None else bias[:, k:k + 1])
                nc.scalar.drain()
                nc.scalar.copy(hhi[:, kt:kt + 2], hw[:, kt:kt + 2]).then_inc(hhi_done, 2)

        def act_split(act, q):
            for kt in range(0, KT, 2):
                act.wait_ge(tr_done, 8 * q + kt + 2)
                nc.scalar.copy(hhi[:, kt:kt + 2], ps8[:, kt:kt + 2]).then_inc(hhi_done, 2)

        def dve_split(dve, q, src):
            for kt in range(0, KT, 2):
                dve.wait_ge(hhi_done, 8 * q + kt + 2)
                nc.vector.tensor_tensor(hlo[:, kt:kt + 2], src[:, kt:kt + 2], hhi[:, kt:kt + 2].bitcast(f32),
                                        ALU.subtract).then_inc(h_ready, 2)

        def dve_norm(dve, m, q, l, c):
            for t in range(NT):
                dve.wait_ge(std_ready, NT * m + t + 1)
                nc.vector.reciprocal(rs[:, t:t + 1], sd[:, t:t + 1])
                nc.vector.drain()
                nc.vector.tensor_scalar(rows[:, t, 0:P], ident[:], rs[:, t:t + 1], None, ALU.mult).then_inc(xn_ready, 1)
            dve_lo(dve, l, c)
            dve_split(dve, q, hw)

        def wait_y(engine, m, t, l, c):
            if t == 0:
                engine.wait_ge(y_ready, m + 1)
            else:
                engine.wait_ge(unit_mm, unit_no(l, c) + 1)

        def act_post(act, m, l, c):
            act_table(ACT.Sqrt)
            for t in range(NT):
                wait_y(act, m, t, l, c)
                nc.scalar.activation(rows[:, t], psy2[:, t], ACT.Square, accum_out=ss[:, 2 + t:3 + t])
                act_rms(2 + t).then_inc(ystd_ready, 1)

        def dve_post(dve, m):
            dve.wait_ge(gain_loaded, 16 * (m + 1))
            for t in range(NT):
                dve.wait_ge(ystd_ready, NT * m + t + 1)
                nc.vector.reciprocal(rs[:, 2 + t:3 + t], sd[:, 2 + t:3 + t])
                nc.vector.drain()
                nc.vector.scalar_tensor_tensor(out=rows[:, t], in0=psy2[:, t], scalar=rs[:, 2 + t:3 + t],
                                               in1=gain[:], op0=ALU.mult, op1=ALU.mult)
                nc.vector.drain()
                nc.vector.tensor_tensor(x[:, t], x[:, t], rows[:, t], ALU.add).then_inc(x_ready, 1)

        def act_ffn(act, l, c0, n, par):
            def silu(c, i, f, bank):
                act.wait_ge(unit_mm, unit_no(l, c, i) + 1)
                act_hi(act, l, c + 2, i)
                if not (isinstance(f, int) and f < 2):
                    act.wait_ge(a_ready, n * NF + f - 1)
                nc.scalar.activation(sg[:, bank], psu[:, bank, 0:SEQ], ACT.Silu).then_inc(silu_done, 1)

            act_table(ACT.Silu)
            silu(c0, 0, 0, par)
            silu(c0 + 1, 0, 1, 1 - par)

            def turn(i):
                for k in range(2):
                    c = c0 + 2 + 3 * k
                    silu(c, i, 2 + 4 * i + 2 * k, par)
                    silu(c + 1, i, 3 + 4 * i + 2 * k, 1 - par)
                    act_hi(act, l, c + 4, i)

            turns(nc.scalar, turn, past_end(l, c0 + 33))

        def add_out(dve, a, s):
            dve.wait_ge(ada_mm, a * STEPS + s + 1)
            if isinstance(s, int) and isinstance(a, int):
                o = mod[:, a, 4 * s:4 * s + 4]
            else:
                o = mod[:].rearrange("p a c -> p (a c)")[:, bass.ds(a * 48 + 4 * s, 4)]
            nc.vector.tensor_tensor(o, o, psm[:, 0:4], ALU.add).then_inc(ada_evac, 1)

        def dve_ffn(dve, l, c0, n, par, a):
            def activations(c, i, f, bank, aslot):
                dve_lo(dve, l, c + 2, i)
                dve.wait_ge(silu_done, n * NF + f + 1)
                nc.vector.tensor_tensor(a32[:, bank], sg[:, bank], psu[:, bank, SEQ:2 * SEQ], ALU.mult).then_inc(bank_free, 1)
                nc.vector.drain()
                nc.vector.tensor_copy(ahi[:, aslot], a32[:, bank])
                nc.vector.drain()
                nc.vector.tensor_tensor(alo[:, aslot], a32[:, bank], ahi[:, aslot].bitcast(f32), ALU.subtract).then_inc(a_ready, 1)

            activations(c0, 0, 0, par, 0)
            activations(c0 + 1, 0, 1, 1 - par, 1)
            def turn(i):
                for k in range(2):
                    c = c0 + 2 + 3 * k
                    activations(c, i, 2 + 4 * i + 2 * k, par, 2 - 2 * k)
                    if a is not None:
                        add_out(dve, a, 2 * i + k)
                    activations(c + 1, i, 3 + 4 * i + 2 * k, 1 - par, 3 - 2 * k)
                    dve_lo(dve, l, c + 4, i)

            turns(nc.vector, turn, past_end(l, c0 + 33))
            if a is not None:
                add_out(dve, a, 10)

        def pe_gate(pe, n, which):
            if which == 0:
                pe.wait_ge(ada_evac, STEPS * min(n + 2, ADA_LAYERS))
            for j in range(KT):
                o = (pso if j < 4 else psm)[:, (j % 4) * P:(j % 4 + 1) * P]
                col = 16 + 24 * which + j
                last = mm(o, mod[:, n, col:col + 1].to_broadcast([P, P]), ident[:], start=True, stop=True)
            last.then_inc(gate_mm, 1)

        def act_gate(act, n, which):
            act.wait_ge(gate_mm, 2 * n + which + 1)
            act.wait_ge(x_ready, 2 + 2 * (2 * (DEPTH1 + n) + which))
            nc.scalar.copy(gain[:, 0:512], pso[:])
            nc.scalar.copy(gain[:, 512:1024], psm[:]).then_inc(gate_bcast, 1)

        def dve_gated(dve, n, which, c):
            dve.wait_ge(gate_bcast, 2 * n + which + 1)
            for t in range(NT):
                wait_y(dve, 2 * (DEPTH1 + n) + which, t, DEPTH1, c)
                nc.vector.tensor_tensor(rows[:, t], psy2[:, t], gain[:], ALU.mult)
                nc.vector.drain()
                nc.vector.tensor_tensor(x[:, t], x[:, t], rows[:, t], ALU.add).then_inc(x_ready, 1)

        def item(q, k, v, col, add=None, bias=None, sink=None, nsink=None, pair=None, causal=False):
            return dict(q=q, k=k, v=v, col=col, add=add, bias=bias, sink=sink, nsink=nsink, pair=pair, causal=causal)

        def na_bias(h):
            def bias(dst, src):
                b = fold(ada_raw[:, 0, :], NT, 4, SEQ)[:, :, h]
                return nc.vector.tensor_tensor(fold(dst, NT, SEQ), fold(src, NT, SEQ), b, ALU.add)
            return bias

        def distance_bias(h):
            def bias(dst, src):
                slope = 2.0 ** (-8.0 * (h + 1) / 4)
                return nc.vector.scalar_tensor_tensor(out=dst, in0=cb[:, 0:512], scalar=slope, in1=src,
                                                      op0=ALU.mult, op1=ALU.add)
            return bias

        def window_bias(dst, src):
            lo, hi = CB2["window"]
            return nc.vector.tensor_tensor(dst[:, P:], src[:, P:], cb[:, lo:hi], ALU.add)

        def forget_bias(h):
            def bias(dst, src):
                lo = CB2["causal"][0]
                for t, s in enumerate((slice(P, SEQ), slice(SEQ, 2 * SEQ))):
                    last = nc.vector.scalar_tensor_tensor(
                        out=dst[:, s], in0=src[:, s], scalar=lcq[:, t * 16 + h:t * 16 + h + 1],
                        in1=cb[:, lo + s.start - P:lo + s.stop - P], op0=ALU.add, op1=ALU.add)
                return last
            return bias

        def heads1():
            out = []
            for h in range(4):
                ps, c = slice(64 * (h % 2), 64 * (h % 2) + 64), (h // 2) * SEQ
                out.append(item(naq[ps, c:c + SEQ], nak[ps, c:c + SEQ],
                                [nav[:, kc * 256 + h * HD:kc * 256 + (h + 1) * HD] for kc in range(2)],
                                h * HD, bias=na_bias(h)))
            for h in range(4):
                for which in range(2):
                    p0, c = 64 * (h % 2) + 32 * which, (h // 2) * SEQ
                    ps = slice(p0, p0 + 32)
                    out.append(item(dfq[ps, c:c + SEQ], dfk[ps, c:c + SEQ],
                                    [dfv[:, kc * 256 + h * HD:kc * 256 + (h + 1) * HD] for kc in range(2)],
                                    256 + h * HD, bias=distance_bias(h), pair=which))
            for c in range(2):
                for kv in range(2):
                    ps = slice(64 * kv, 64 * kv + 64)
                    out.append(item(gqT[ps, c * SEQ:(c + 1) * SEQ], gkT[ps, :],
                                    [gv[:, kc * P + kv * HD:kc * P + (kv + 1) * HD] for kc in range(2)],
                                    512 + (2 * kv + c) * HD))
            for h in range(4):
                out.append(item(qcT[0:96, h * SEQ:(h + 1) * SEQ], kcT[0:96, h * SEQ:(h + 1) * SEQ],
                                [kvr[:, kc * 512 + h * P + HD:kc * 512 + (h + 1) * P] for kc in range(2)],
                                768 + h * HD))
            return out

        s_raw, s_roped = fold(w(0, 1024), 2, 512), fold(w(1024, 1024), 2, 512)
        s_u, s_v = w(2048, 512), w(2560, 512)
        s_qT, s_kT, s_vv = w(3072, 2048), w(5120, 512), w(5632, 512)

        def heads_swa(sidx):
            out = []
            for ch in range(8):
                for half in range(2):
                    kvh = 2 * (ch // 4) + half
                    h = kvh * 4 + ch % 4
                    ps = slice(64 * half, 64 * half + 64)
                    at = sidx * 16 + h
                    out.append(item(s_qT[ps, ch * SEQ:(ch + 1) * SEQ],
                                    s_kT[ps, (ch // 4) * SEQ:(ch // 4 + 1) * SEQ],
                                    [s_vv[:, kc * 256 + kvh * HD:kc * 256 + (kvh + 1) * HD] for kc in range(2)],
                                    h * HD, bias=window_bias, sink=prow2[:, at:at + 1], nsink=nsink[:, at:at + 1],
                                    causal=True))
            return out

        f_qT, f_kT, f_v = w(0, 2048), w(2048, 2048), w(4096, 2048)
        f_x, f_l, f_lf, lcq, f_row = w(6144, 32), w(6176, 32), w(6208, 32), w(6240, 32), w(6272, 256)

        def heads_fox():
            out = []
            for h in range(16):
                ps, c = slice(64 * (h % 2), 64 * (h % 2) + 64), (h // 2) * SEQ
                out.append(item(f_qT[ps, c:c + SEQ], f_kT[ps, c:c + SEQ],
                                [f_v[:, kc * D + h * HD:kc * D + (h + 1) * HD] for kc in range(2)], h * HD,
                                add=ada_raw[0:1, h // 8, (h % 8) * SEQ:(h % 8 + 1) * SEQ], bias=forget_bias(h), causal=True))
            return out

        g_qT, g_kT, g_bT = w(0, 1024), w(1024, 1024), w(2048, 1024)
        g_Q, g_K, g_E, g_S = w(3072, 1024), w(4096, 1024), w(5120, 1024), w(3072, 3072)
        g_lag, g_v = w(6144, 1024), w(7168, 2048)
        g_att, g_krow = scratch[:, 0:1024], scratch[:, 1024:2048]
        g_low = h32[0:16, 0]
        g_ret = ada_raw[:].rearrange("p a n -> p (a n)")[:, 0:2048]
        eb = gs[:, 2]

        def rope(src, dst, c, s, u, v, d):
            def halves(ap):
                return ap.rearrange("p t (n two d) -> p t n two d", two=2, d=d)
            nc.vector.tensor_tensor(u, src, c, ALU.mult)
            for i in range(2):
                nc.vector.tensor_tensor(halves(v)[:, :, :, i], halves(src)[:, :, :, 1 - i], halves(s)[:, :, :, i], ALU.mult)
            nc.vector.drain()
            return nc.vector.tensor_tensor(dst, u, v, ALU.add)

        def tabs(lo, hi, n):
            return fold(cb[:, lo:hi], NT, n)

        def pe_swa(pe, n, c0, b0):
            s5 = 5 * (n // 3)

            def heads(j):
                pe.wait_ge(swa_rope, s5 + j + 1)
                if j >= 2:
                    pe.wait_ge(swa_evac, s5 + j - 1)
                else:
                    pe.wait_ge(gate_bcast, 2 * n + 1)
                o = pso if j % 2 == 0 else psm
                for c in range(2):
                    for t in range(NT):
                        last = nc.tensor.transpose(o[:, c * SEQ + t * P:c * SEQ + (t + 1) * P],
                                                   s_roped[:, j % 2, t * 256 + c * P:t * 256 + (c + 1) * P], ident[:])
                last.then_inc(swa_tr, 1)

            for j in range(6):
                pe_in_unit(pe, DEPTH1, c0 + j, j, b0 + j, "rows", 3 * (DEPTH1 + n))
                if j >= 1:
                    heads(j - 1)
            pe.wait_ge(swa_evac, s5 + 5)
            pe.wait_ge(bank_free, b0 + 6)
            pe_items(pe, item0[n], heads_swa(n // 3))

        def pe_fox(pe, n, c0, b0):
            for j in range(13):
                pe_in_unit(pe, DEPTH1, c0 + j, j, b0 + j, "cols" if 1 <= j < 9 else "rows", 3 * (DEPTH1 + n),
                           16 if j == 0 else 256)
                if j == 5:
                    pe.wait_ge(fox_lf, 1)
                    pe.wait_ge(gate_bcast, 2 * n + 1)
                    lo = CB2["upto"][0]
                    for t in range(NT):
                        for kt in range(t + 1):
                            mm(psm[:, t * 16:(t + 1) * 16], cb[:, lo + kt * SEQ + t * P:lo + kt * SEQ + (t + 1) * P],
                               f_lf[:, kt * 16:(kt + 1) * 16], start=(kt == 0), stop=(kt == t))
                    for kt in range(2):
                        last = mm(pso[0:16, 0:SEQ], f_lf[:, kt * 16:(kt + 1) * 16], cb[:, lo + kt * SEQ:lo + (kt + 1) * SEQ],
                                  start=(kt == 0), stop=(kt == 1))
                    last.then_inc(fox_c, 1)
            pe.wait_ge(bank_free, b0 + 13)
            pe.wait_ge(fox_row, 32)
            pe_items(pe, item0[n], heads_fox())

        def pe_gla(pe, n, c0, b0):
            for j in range(13):
                pe_in_unit(pe, DEPTH1, c0 + j, j, b0 + j, "cols" if j < 5 else "rows", 3 * (DEPTH1 + n), P if j == 4 else 256)
                if j == 6:
                    pe.wait_ge(bank_free, b0 + 5)
                    pe.wait_ge(gate_loaded, 32)
                    for t in range(NT):
                        mm(psy[:, t, :], g_low[:, t * P:(t + 1) * P], wgu, start=True, stop=False)
                        last = mm(psy[:, t, :], ones[0:1, 0:P], bgate, start=False, stop=True)
                    last.then_inc(g_logit, 1)
                if j == 8:
                    pe.wait_ge(g_la, 1)
                    lo = CB2["upto64"][0]
                    for t in range(NT):
                        for h in range(4):
                            last = mm(psy[:, 2 + t, h * P:(h + 1) * P], g_lag[:, t * 512 + h * P:t * 512 + (h + 1) * P],
                                      cb[:, lo:lo + P], start=True, stop=True)
                    last.then_inc(g_cum, 1)
            pe.wait_ge(bank_free, b0 + 13)
            pe.wait_ge(g_b, 1)
            for lv in range(7):
                if lv >= 1:
                    pe.wait_ge(g_qk, lv)
                if lv >= 2:
                    pe.wait_ge(g_acc, lv - 1)
                q, k = (g_qT, g_kT) if lv == 0 else (g_Q, g_K)
                for t in range(NT):
                    for h in range(4):
                        at = h * SEQ + t * P
                        last = mm(psy[:, (lv % 2) * 2 + t, h * P:(h + 1) * P], k[:, at:at + P], q[:, at:at + P],
                                  start=True, stop=True)
                last.then_inc(g_s, 1)
            pe.wait_ge(g_kd, 1)
            for t in range(NT):
                for h in range(4):
                    last = nc.tensor.transpose(psu[:, t, h * P:(h + 1) * P],
                                               g_E[:, h * SEQ + t * P:h * SEQ + (t + 1) * P], ident[:])
            last.then_inc(g_kt, 1)
            pe.wait_ge(g_kr, 1)
            pe.wait_ge(g_acc, 7)
            for c in range(3):
                t, ps = c // 2, slice(64 * (c % 2), 64 * (c % 2) + 64)
                for h in range(4):
                    o = (psy[:, 2 * c + h // 2] if c < 2 else psu[:, h // 2])[:, (h % 2) * 256:(h % 2 + 1) * 256]
                    last = mm(o, g_krow[ps, t * 512 + h * P:t * 512 + (h + 1) * P],
                              g_v[ps, t * D + h * 256:t * D + (h + 1) * 256], start=True, stop=True)
            last.then_inc(g_ds, 1)
            pe.wait_ge(g_st, 1)
            pe.wait_ge(g_sum, 6)
            for t in range(NT):
                for h in range(4):
                    o = psy2[:, t, h * 256:(h + 1) * 256]
                    mm(o, g_att[:, t * 512 + h * P:t * 512 + (h + 1) * P], g_v[:, t * D + h * 256:t * D + (h + 1) * 256],
                       start=True, stop=False, skip_group_check=True)
                    for c in (2 * t, 2 * t + 1):
                        if c == 0:
                            continue
                        ps = slice(64 * (c % 2), 64 * (c % 2) + 64)
                        last = mm(o[ps], g_lag[:, h * SEQ + c * 64:h * SEQ + c * 64 + 64],
                                  g_S[:, (c - 1) * 1024 + h * 256:(c - 1) * 1024 + (h + 1) * 256],
                                  start=False, stop=(c % 2 == 1), skip_group_check=True)
            last.then_inc(g_o, 1)

        def act_swa(act, n, c0, b0):
            s5 = 5 * (n // 3)

            def evac(j):
                act.wait_ge(swa_tr, s5 + j + 1)
                o = pso if j % 2 == 0 else psm
                dst = s_qT[:, j * 512:(j + 1) * 512] if j < 4 else s_kT
                nc.scalar.copy(dst, o[:]).then_inc(swa_evac, 1)

            for j in range(6):
                act.wait_ge(unit_mm, unit_no(DEPTH1, c0 + j) + 1)
                act_hi(act, DEPTH1, c0 + j + SPLIT)
                src = psu[:, (b0 + j) % 2]
                if j < 5:
                    if j >= 2:
                        act.wait_ge(swa_rope, s5 + j - 1)
                    nc.scalar.activation(s_raw[:, j % 2], src, ACT.Copy, scale=HD ** -0.5 if j < 4 else 1.0).then_inc(bank_free, 1)
                else:
                    nc.scalar.copy(s_vv, src).then_inc(bank_free, 1)
                if j >= 1:
                    evac(j - 1)
            act_items(act, item0[n], heads_swa(n // 3))

        def act_fox(act, n, c0, b0):
            for j in range(13):
                act.wait_ge(unit_mm, unit_no(DEPTH1, c0 + j) + 1)
                act_hi(act, DEPTH1, c0 + j + SPLIT)
                src = psu[:, (b0 + j) % 2]
                if j == 1:
                    act.wait_ge(bank_free, b0 + 1)
                if 1 <= j < 5:
                    nc.scalar.activation(f_qT[:, (j - 1) * 512:j * 512], src, ACT.Copy, scale=HD ** -0.5).then_inc(bank_free, 1)
                elif 5 <= j < 9:
                    nc.scalar.copy(f_kT[:, (j - 5) * 512:(j - 4) * 512], src).then_inc(bank_free, 1)
                elif j >= 9:
                    dst = fold(f_v, NT, D)[:, :, (j - 9) * 256:(j - 8) * 256]
                    nc.scalar.copy(dst, fold(src, NT, 256)).then_inc(bank_free, 1)
                if j == 2:
                    nc.scalar.activation(f_l, f_x, ACT.Abs)
                    nc.scalar.drain()
                    nc.scalar.activation(f_l, f_l, ACT.Exp, scale=-1.0)
                    nc.scalar.drain()
                    nc.scalar.activation(f_l, f_l, ACT.Ln, bias=1.0).then_inc(fox_l, 1)
                if j == 6:
                    act.wait_ge(fox_c, 1)
                    nc.scalar.copy(lcq, psm[:, 0:32])
                    nc.scalar.activation(f_row[0:16, :], pso[0:16, 0:SEQ], ACT.Copy, scale=-1.0).then_inc(fox_ce, 1)
                    act.wait_ge(fox_ce, 1)
                    for i in range(2):
                        act.dma_start(ada_raw[0:1, i, :].rearrange("o (h n) -> o h n", h=8),
                                      f_row[8 * i:8 * i + 8, :]).then_inc(fox_row, 16)
            act_items(act, item0[n], heads_fox())

        def act_gla(act, n, c0, b0):
            def log_parts():
                act.wait_ge(g_logit, 1)
                for t in range(NT):
                    nc.scalar.activation(g_Q[:, t * 512:(t + 1) * 512], psy[:, t, :], ACT.Abs)
                nc.scalar.drain()
                nc.scalar.activation(g_Q, g_Q, ACT.Exp, scale=-1.0)
                nc.scalar.drain()
                nc.scalar.activation(g_Q, g_Q, ACT.Ln, bias=1.0).then_inc(g_ln, 1)

            for j in range(13):
                act.wait_ge(unit_mm, unit_no(DEPTH1, c0 + j) + 1)
                act_hi(act, DEPTH1, c0 + j + SPLIT)
                src = psu[:, (b0 + j) % 2]
                if j < 2:
                    nc.scalar.activation(g_qT[:, j * 512:(j + 1) * 512], src, ACT.Copy, scale=P ** -0.5).then_inc(bank_free, 1)
                elif j < 4:
                    nc.scalar.copy(g_kT[:, (j - 2) * 512:(j - 1) * 512], src).then_inc(bank_free, 1)
                elif j == 4:
                    nc.scalar.copy(g_low, src[0:16, 0:SEQ]).then_inc(bank_free, 1)
                elif j < 9:
                    dst = fold(g_v, NT, D)[:, :, (j - 5) * 256:(j - 4) * 256]
                    nc.scalar.copy(dst, fold(src, NT, 256)).then_inc(bank_free, 1)
                else:
                    dst = fold(g_ret, NT, D)[:, :, (j - 9) * 256:(j - 8) * 256]
                    nc.scalar.copy(dst, fold(src, NT, 256)).then_inc(bank_free, 1)
                if j == 7:
                    log_parts()
            act.wait_ge(g_cum, 1)
            for t in range(NT):
                dst = fold(g_bT, 4, SEQ)[:, :, t * P:(t + 1) * P]
                last = nc.scalar.activation(dst, fold(psy[:, 2 + t], 4, P), ACT.Copy, scale=1.0 / 16)
            last.then_inc(g_b, 1)
            for lv in range(1, 7):
                act.wait_ge(g_e, lv)
                nc.scalar.activation(g_E, g_E, ACT.Exp).then_inc(g_x, 1)
            act.wait_ge(g_dec, 1)
            nc.scalar.activation(g_E, g_E, ACT.Exp)
            nc.scalar.activation(g_lag, g_bT, ACT.Exp)
            nc.scalar.activation(eb, fold(g_bT, 16, 64)[:, :, 63], ACT.Exp).then_inc(g_dex, 1)
            act.wait_ge(g_kt, 1)
            act.wait_ge(g_sum, 6)
            nc.scalar.copy(fold(g_krow, 2, 512), psu[:]).then_inc(g_kr, 1)
            nc.scalar.activation(g_ret, g_ret, ACT.Silu).then_inc(g_silu, 1)
            act_table(ACT.Sqrt)
            act.wait_ge(g_o, 1)
            for t in range(NT):
                for h in range(4):
                    nc.scalar.activation(w((t * 4 + h) * 256, 256), psy2[:, t, h * 256:(h + 1) * 256], ACT.Square,
                                         accum_out=gs[:, 0, t * 4 + h:t * 4 + h + 1])
            nc.scalar.drain()
            nc.scalar.activation(gs[:, 1, 0:8], gs[:, 0, 0:8], ACT.Sqrt, bias=epsc[:], scale=1.0 / 256).then_inc(g_std, 1)

        def dve_swa(dve, n, c0, b0):
            s5 = 5 * (n // 3)
            rc, rsn = tabs(*CB2["rope_c"], 256), tabs(*CB2["rope_s"], 256)
            for j in range(6):
                nc.vector.drain()
                dve_lo(dve, DEPTH1, c0 + j + SPLIT)
                if j < 5:
                    dve.wait_ge(bank_free, b0 + j + 1)
                    if j >= 2:
                        dve.wait_ge(swa_tr, s5 + j - 1)
                    rope(fold(s_raw[:, j % 2], NT, 256), fold(s_roped[:, j % 2], NT, 256), rc, rsn,
                         fold(s_u, NT, 256), fold(s_v, NT, 256), 32).then_inc(swa_rope, 1)
            dve_items(dve, item0[n], heads_swa(n // 3))

        def dve_fox(dve, n, c0, b0):
            for j in range(13):
                dve_lo(dve, DEPTH1, c0 + j + SPLIT)
                if j == 0:
                    dve.wait_ge(unit_mm, unit_no(DEPTH1, c0) + 1)
                    nc.vector.tensor_tensor(fold(f_x, NT, 16), fold(psu[:, b0 % 2, 0:32], NT, 16),
                                            prow2[:, 32:48].unsqueeze(1).to_broadcast([P, NT, 16]), ALU.add).then_inc(bank_free, 1)
                if j == 3:
                    dve.wait_ge(fox_l, 1)
                    nc.vector.scalar_tensor_tensor(out=f_lf, in0=f_x, scalar=0.0, in1=f_l, op0=ALU.min,
                                                   op1=ALU.subtract).then_inc(fox_lf, 1)
            dve.wait_ge(fox_ce, 1)
            dve_items(dve, item0[n], heads_fox())

        def dve_gla(dve, n, c0, b0):
            for j in range(13):
                dve_lo(dve, DEPTH1, c0 + j + SPLIT)
                if j == 7:
                    dve.wait_ge(g_ln, 1)
                    for t in range(NT):
                        last = nc.vector.scalar_tensor_tensor(out=g_lag[:, t * 512:(t + 1) * 512], in0=psy[:, t, :], scalar=0.0,
                                                              in1=g_Q[:, t * 512:(t + 1) * 512], op0=ALU.min, op1=ALU.subtract)
                    last.then_inc(g_la, 1)
            nc.vector.drain()
            nc.vector.memset(g_Q, 0.0)
            nc.vector.memset(g_K, 0.0)
            nc.vector.drain()
            dve.wait_ge(g_b, 1)
            lo = CB2["level"][0]

            def add_level(lv):
                dve.wait_ge(g_s, lv + 1)
                mask = cb[:, lo + lv * P:lo + (lv + 1) * P].unsqueeze(1).to_broadcast([P, 4, P])
                for t in range(NT):
                    src = fold(psy[:, (lv % 2) * 2 + t], 4, P)
                    if lv >= 2 and t == 0:
                        dve.wait_ge(g_sum, lv - 1)
                    dst = (g_att if lv == 0 else g_krow)[:, t * 512:(t + 1) * 512]
                    last = nc.vector.tensor_tensor(fold(dst, 4, P), src, mask, ALU.mult)
                last.then_inc(g_acc, 1)

            for lv in range(1, 7):
                m = 64 >> lv
                nb = 1024 // (2 * m)

                def parts(ap):
                    return ap.rearrange("p (n two m) -> p n two m", two=2, m=m)
                b4 = parts(g_bT)
                ref = b4[:, :, 0, m - 1:m].to_broadcast([P, nb, m])
                Eu, El = fold(g_E[:, 0:512], nb, m), fold(g_E[:, 512:1024], nb, m)
                if lv > 1:
                    nc.vector.drain()
                nc.vector.tensor_tensor(Eu, b4[:, :, 1, :], ref, ALU.subtract)
                nc.vector.tensor_tensor(El, ref, b4[:, :, 0, :], ALU.subtract).then_inc(g_e, 1)
                add_level(lv - 1)
                dve.wait_ge(g_x, lv)
                nc.vector.tensor_tensor(parts(g_Q)[:, :, 1, :], parts(g_qT)[:, :, 1, :], Eu, ALU.mult)
                nc.vector.tensor_tensor(parts(g_K)[:, :, 0, :], parts(g_kT)[:, :, 0, :], El, ALU.mult).then_inc(g_qk, 1)
            nc.vector.drain()
            b3 = fold(g_bT, 16, 64)
            nc.vector.tensor_tensor(fold(g_E, 16, 64), b3[:, :, 63:64].to_broadcast([P, 16, 64]), b3, ALU.subtract).then_inc(g_dec, 1)
            add_level(6)
            dve.wait_ge(g_dex, 1)
            nc.vector.tensor_tensor(g_E, g_E, g_kT, ALU.mult)
            nc.vector.tensor_tensor(g_lag, g_lag, g_qT, ALU.mult).then_inc(g_kd, 1)
            dve.wait_ge(g_ds, 1)
            nc.vector.tensor_copy(fold(g_S[:, 0:1024], 2, 512), psy[:, 0:2])
            nc.vector.drain()
            for c in (1, 2):
                for h in range(4):
                    src = (psy[:, 2 + h // 2] if c == 1 else psu[:, h // 2])[:, (h % 2) * 256:(h % 2 + 1) * 256]
                    at = (c - 1) * 1024 + h * 256
                    last = nc.vector.scalar_tensor_tensor(out=g_S[:, at + 1024:at + 1280], in0=g_S[:, at:at + 256],
                                                          scalar=eb[:, h * 4 + c:h * 4 + c + 1], in1=src,
                                                          op0=ALU.mult, op1=ALU.add)
                if c == 1:
                    nc.vector.drain()
            last.then_inc(g_st, 1)
            dve.wait_ge(g_silu, 1)
            gr = g_ret.rearrange("p (h d) -> p h d", d=256)
            nc.vector.tensor_tensor(gr, gr, prow2[:, 48:304].unsqueeze(1).to_broadcast([P, 8, 256]), ALU.mult)
            dve.wait_ge(g_std, 1)
            nc.vector.reciprocal(gs[:, 2, 0:8], gs[:, 1, 0:8])
            nc.vector.drain()
            for t in range(NT):
                r4 = rows[:, t].rearrange("p (h d) -> p h d", h=4)
                nc.vector.tensor_tensor(r4, psy2[:, t].rearrange("p (h d) -> p h d", h=4),
                                        gs[:, 2, t * 4:t * 4 + 4].unsqueeze(2).to_broadcast([P, 4, 256]), ALU.mult)
                nc.vector.drain()
                last = nc.vector.tensor_tensor(rows[:, t], rows[:, t], g_ret[:, t * D:(t + 1) * D], ALU.mult)
            last.then_inc(mix_ready, 1)

        @block.tensor
        def _(pe):
            pe.wait_ge(start_loads, 16 * 2)
            pe.wait_ge(filled, 4)
            with nc.tensor.Fori(0, DEPTH1) as l:
                pe_norm(pe, 2 * l, 3 * l)
                for c, u in enumerate(W_IN1):
                    if c != C1_SMALL:
                        j = c - (c > C1_SMALL)
                        pe_in_unit(pe, l, c, j, l * 32 + j, "cols" if u in COLS1 else "rows", 3 * l, 160 if u == 9 else 256)
                    else:
                        pe.wait_ge(ml_h, 3 * l + 3)
                        pe.wait_ge(lo_done, unit_no(l, c) + 1)
                        ks = part_of(c)
                        for t in range(NT):
                            toks = slice(t * P, t * P + P)
                            for o, kts, base, width in ((psy[:, t, 0:384], (0, 1), 0, 384), (psy[:, 2 + t, :], (2,), 768, 512)):
                                for kt in kts:
                                    cols = slice(base + (kt % 2) * width, base + (kt % 2) * width + width)
                                    for p, (h, a) in enumerate(((ahi, whi), (alo, whi), (ahi, wlo))):
                                        last = mm(o, h[:, kt, toks], a[:, ks, cols],
                                                  start=(kt == kts[0] and p == 0), stop=(kt == kts[-1] and p == 2))
                        last.then_inc(unit_mm, 1)
                    if c == 3:
                        pe.wait_ge(ml_norm, l + 1)
                        for t in range(NT):
                            for k in range(2):
                                nc.tensor.transpose(ps8[:, k, t * P:(t + 1) * P],
                                                    mcq[:, t * 256 + k * P:t * 256 + (k + 1) * P], ident[:])
                            last = nc.tensor.transpose(ps8[:, 2, t * P:(t + 1) * P], mckv[:, t * 160:t * 160 + P], ident[:])
                        last.then_inc(ml_tr, 1)
                    if c == 9:
                        pe.wait_ge(gq_rope, l + 1)
                        for t in range(NT):
                            for k in range(2):
                                nc.tensor.transpose(pso[:, k * SEQ + t * P:k * SEQ + (t + 1) * P],
                                                    gqr[:, t * 256 + k * P:t * 256 + (k + 1) * P], ident[:])
                            last = nc.tensor.transpose(psm[:, t * P:(t + 1) * P], gkr[:, t * P:(t + 1) * P], ident[:])
                        last.then_inc(gq_tr, 1)
                pe.wait_ge(ml_rope, l + 1)
                for h in range(4):
                    for t in range(NT):
                        nc.tensor.transpose(ps8[0:96, h, t * P:(t + 1) * P],
                                            qf[:, t * 384 + h * 96:t * 384 + (h + 1) * 96], ident[:])
                        last = nc.tensor.transpose(ps8[0:96, 4 + h, t * P:(t + 1) * P],
                                                   kcat[:, t * 384 + h * 96:t * 384 + (h + 1) * 96], ident[:])
                last.then_inc(ml_ctr, 1)
                pe.wait_ge(qk_ready, l + 1)
                pe_items(pe, l * 20, heads1())
                pe_out(pe, l, C1_O, l, (mix_ready, l + 1))
                pe_norm(pe, 2 * l + 1, 3 * l + 2)
                pe_ffn(pe, l, C1_FFN, l, l * 32 + 10, 0, l)
            for n in range(DEPTH2):
                kind, c0, b0, g = KINDS2[n], BASE2[n], bank0[n], DEPTH1 + n
                nin = len(IN2[kind])
                pe_norm(pe, 2 * g, 3 * g)
                pe_gate(pe, n, 0)
                {"swa": pe_swa, "gla": pe_gla, "fox": pe_fox}[kind](pe, n, c0, b0)
                pe_out(pe, DEPTH1, c0 + nin, g, (mix_ready, DEPTH1 + 1) if kind == "gla" else (o_evac, item0[n] + 16))
                pe_norm(pe, 2 * g + 1, 3 * g + 2)
                pe_gate(pe, n, 1)
                pe_ffn(pe, DEPTH1, c0 + nin + 4, g, b0 + nin, (b0 + nin) % 2, g if g < ADA_LAYERS else None, gated=True)

        @block.scalar
        def _(act):
            act.wait_ge(start_loads, 16 * 2)
            act.wait_ge(filled, 4)
            act.wait_ge(c_loaded, 16)
            nc.scalar.activation(ccol[:], ccol[:], ACT.Silu).then_inc(start_act, 1)
            act_hi(act, 0, 0, first=True)
            with nc.scalar.Fori(0, DEPTH1) as l:
                act.wait_ge(par_loaded, 32 * (l + 1))
                act_norm(act, 2 * l, 3 * l, pcol[:, 0:8], None, l, 1)
                dst = {0: (naq, HD ** -0.5), 1: (nak, 1.0), 2: (nav, 1.0), 3: (dfq, 32 ** -0.5), 4: (dfk, 1.0),
                       5: (dfv, 1.0), 6: (gqr, 1.0), 8: (mcq, 1.0)}
                for c, u in enumerate(W_IN1):
                    act.wait_ge(unit_mm, unit_no(l, c) + 1)
                    act_hi(act, l, c + SPLIT)
                    src = psu[:, (c - (c > C1_SMALL)) % 2]
                    if c == C1_SMALL:
                        for t in range(NT):
                            nc.scalar.activation(qf[:, t * 384:(t + 1) * 384], psy[:, t, 0:384], ACT.Copy, scale=96 ** -0.5)
                            last = nc.scalar.copy(kvr[:, t * 512:(t + 1) * 512], psy[:, 2 + t, :])
                        last.then_inc(ml_evac, 1)
                    elif u in dst:
                        if u == 3:
                            act.wait_ge(gq_rope, l + 1)
                        nc.scalar.activation(dst[u][0], src, ACT.Copy, scale=dst[u][1]).then_inc(bank_free, 1)
                    elif u == 7:
                        nc.scalar.copy(fold(gkr, NT, P), fold(src, NT, 256)[:, :, 0:P])
                        nc.scalar.copy(fold(gv, NT, P), fold(src, NT, 256)[:, :, P:256]).then_inc(bank_free, 1)
                    else:
                        nc.scalar.copy(mckv, src[:, 0:320]).then_inc(bank_free, 1)
                    if c == 1:
                        nc.scalar.drain()
                        for t in range(NT):
                            nc.scalar.activation(prob[:, t, 0:256], mcq[:, t * 256:(t + 1) * 256], ACT.Square, accum_out=ss[:, t:t + 1])
                            nc.scalar.activation(prob[:, t, 256:256 + P], mckv[:, t * 160:t * 160 + P], ACT.Square,
                                                 accum_out=ss[:, 2 + t:3 + t])
                        nc.scalar.drain()
                        nc.scalar.activation(sd[:, 0:2], ss[:, 0:2], ACT.Sqrt, bias=epsc[:], scale=1.0 / 256)
                        nc.scalar.activation(sd[:, 2:4], ss[:, 2:4], ACT.Sqrt, bias=epsc[:], scale=1.0 / 128).then_inc(ml_std, 1)
                    if c == 4:
                        act.wait_ge(ml_tr, l + 1)
                        for k in range(3):
                            if k == 2:
                                act.wait_ge(ml_h, 3 * l + 1)
                            nc.scalar.activation(h32[:, k % 2], ps8[:, k], ACT.Identity, scale=pcol[:, 16 + k:17 + k], bias=zcol[:])
                            nc.scalar.drain()
                            nc.scalar.copy(ahi[:, k], h32[:, k % 2]).then_inc(ml_hi, 1)
                    if c == 5:
                        act.wait_ge(gq_sum, l + 1)
                        nc.scalar.activation(gs[:, 1, 0:12], gs[:, 0, 0:12], ACT.Sqrt, bias=epsc[:], scale=1.0 / HD)
                        nc.scalar.activation(lamt[:, 2:4], lamt[:, 0:2], ACT.Exp).then_inc(gq_std, 1)
                act.wait_ge(gq_tr, l + 1)
                nc.scalar.activation(gqT, pso[:], ACT.Copy, scale=HD ** -0.5)
                nc.scalar.copy(gkT, psm[:, 0:SEQ])
                act.wait_ge(ml_ctr, l + 1)
                for i in range(2):
                    nc.scalar.copy(qcT[0:96, i * 512:(i + 1) * 512], psy[0:96, i, :])
                    last = nc.scalar.copy(kcT[0:96, i * 512:(i + 1) * 512], psy[0:96, 2 + i, :])
                last.then_inc(qk_ready, 1)
                act_items(act, l * 20, heads1())
                act.wait_ge(sub_sum, l + 1)
                nc.scalar.activation(gs[:, 1, 0:8], gs[:, 0, 0:8], ACT.Sqrt, bias=epsc[:], scale=1.0 / HD).then_inc(sub_std, 1)
                act_split(act, 3 * l + 1)
                for j in range(3):
                    act_hi(act, l, C1_O + j + SPLIT)
                act_post(act, 2 * l, l, C1_O + 3)
                act_norm(act, 2 * l + 1, 3 * l + 2, pcol[:, 8:16], None, l, C1_FFN + 1)
                act_ffn(act, l, C1_FFN, l, 0)
                act_post(act, 2 * l + 1, l, PER1 - 1)
            for n in range(DEPTH2):
                kind, c0, b0, g = KINDS2[n], BASE2[n], bank0[n], DEPTH1 + n
                nin = len(IN2[kind])
                act_table(ACT.Sqrt)
                act.wait_ge(acol_ready, n + 1)
                act_norm(act, 2 * g, 3 * g, acol[:, 0:8], mod[:, n, 0:8], DEPTH1, c0 + 1)
                act_gate(act, n, 0)
                {"swa": act_swa, "gla": act_gla, "fox": act_fox}[kind](act, n, c0, b0)
                act_split(act, 3 * g + 1)
                for j in range(3):
                    act_hi(act, DEPTH1, c0 + nin + j + SPLIT)
                act_table(ACT.Sqrt)
                act_norm(act, 2 * g + 1, 3 * g + 2, acol[:, 8:16], mod[:, n, 24:32], DEPTH1, c0 + nin + 5)
                act_gate(act, n, 1)
                act_ffn(act, DEPTH1, c0 + nin + 4, g, (b0 + nin) % 2)
            act_table(ACT.Sqrt)
            act_norm(act, 2 * (DEPTH1 + DEPTH2), None, None, None)

        @block.vector
        def _(dve):
            dve.wait_ge(start_loads, 16 * 2)
            nc.vector.memset(esink[:], 0.0).then_inc(x_ready, 2)
            dve_lo(dve, 0, 0)
            with nc.vector.Fori(0, DEPTH1) as l:
                dve_norm(dve, 2 * l, 3 * l, l, 1)
                dve_lo(dve, l, 2)
                dve_lo(dve, l, 3)
                dve.wait_ge(ml_std, l + 1)
                nc.vector.reciprocal(rs[:, 0:4], sd[:, 0:4])
                nc.vector.drain()
                for t in range(NT):
                    a, b = mcq[:, t * 256:(t + 1) * 256], mckv[:, t * 160:t * 160 + P]
                    nc.vector.tensor_scalar(a, a, rs[:, t:t + 1], None, ALU.mult)
                    last = nc.vector.tensor_scalar(b, b, rs[:, 2 + t:3 + t], None, ALU.mult)
                last.then_inc(ml_norm, 1)
                dve_lo(dve, l, 4)
                dve_lo(dve, l, 5)
                dve.wait_ge(bank_free, l * 32 + 4)
                dve.wait_ge(par_loaded, 32 * (l + 1))
                dve.wait_ge(cb1_loaded, 16)
                dve.wait_ge(pool_loads, 16 * 3)
                dve.wait_ge(start_act, 1)
                qs, ks = scratch[:, 0:512], scratch[:, 1024:1280]
                nc.vector.tensor_tensor(qs, gqr, gqr, ALU.mult)
                nc.vector.tensor_tensor(ks, gkr, gkr, ALU.mult)
                nc.vector.tensor_tensor(scratch[:, 1536:1600], prow[:, 192:256], prow[:, 256:320], ALU.mult)
                nc.vector.drain()
                nc.vector.tensor_reduce(out=gs[:, 0, 0:8], in_=fold(qs, 8, HD), op=ALU.add, axis=AX.X)
                nc.vector.tensor_reduce(out=gs[:, 0, 8:12], in_=fold(ks, 4, HD), op=ALU.add, axis=AX.X)
                nc.vector.tensor_reduce(out=lamt[:, 0:2], in_=fold(scratch[:, 1536:1600], 2, 32), op=ALU.add,
                                        axis=AX.X).then_inc(gq_sum, 1)
                dve_lo(dve, l, 6)
                for c in range(3):
                    dve.wait_ge(ml_hi, 3 * l + c + 1)
                    nc.vector.tensor_tensor(alo[:, c], h32[:, c % 2], ahi[:, c].bitcast(f32), ALU.subtract).then_inc(ml_h, 1)
                dve_lo(dve, l, 7)
                dve.wait_ge(gq_std, l + 1)
                nc.vector.reciprocal(gs[:, 2, 0:12], gs[:, 1, 0:12])
                nc.vector.tensor_tensor(lamt[:, 5:6], lamt[:, 2:3], lamt[:, 3:4], ALU.subtract)
                nc.vector.drain()
                nc.vector.tensor_tensor(lamt[:, 4:5], lamt[:, 5:6], prow[:, 320:321], ALU.add)
                for src, n, at, gn in ((gqr, 8, 0, "gq"), (gkr, 4, 8, "gk")):
                    v = fold(src, n, HD)
                    nc.vector.tensor_tensor(v, v, gs[:, 2, at:at + n].unsqueeze(2).to_broadcast([P, n, HD]), ALU.mult)
                nc.vector.drain()
                for src, n, at, gn in ((gqr, 8, 0, "gq"), (gkr, 4, 8, "gk")):
                    v = fold(src, n, HD)
                    nc.vector.tensor_tensor(v, v, prow[:, ROW1[gn][0]:ROW1[gn][1]].unsqueeze(1).to_broadcast([P, n, HD]), ALU.mult)
                nc.vector.drain()
                dve_lo(dve, l, 8)
                rc, rsn = tabs(*CB1["rope_c"], 256), tabs(*CB1["rope_s"], 256)
                rope(fold(gkr, NT, P), fold(gkr, NT, P), rc[:, :, 0:P], rsn[:, :, 0:P],
                     fold(scratch[:, 1024:1280], NT, P), fold(scratch[:, 1280:1536], NT, P), 16)
                dve_lo(dve, l, 9)
                rope(fold(gqr, NT, 256), fold(gqr, NT, 256), rc, rsn,
                     fold(dfq, NT, 256), fold(dfk, NT, 256), 16).then_inc(gq_rope, 1)
                dve_lo(dve, l, 10)
                dve.wait_ge(ml_evac, l + 1)
                mc, ms = tabs(*CB1["mla_c"], P), tabs(*CB1["mla_s"], P)
                qr = fold(qf, NT, 4, 96)[:, :, :, 64:96]
                u, v = fold(scratch[:, 1536:1792], NT, 4, 32), fold(scratch[:, 1792:2048], NT, 4, 32)
                c4, s4 = (m.rearrange("p t (h d) -> p t h d", h=4) for m in (mc, ms))
                nc.vector.tensor_tensor(u, qr, c4, ALU.mult)
                for i in range(2):
                    a, b = slice(16 * i, 16 * i + 16), slice(16 - 16 * i, 32 - 16 * i)
                    nc.vector.tensor_tensor(v[:, :, :, a], qr[:, :, :, b], s4[:, :, :, a], ALU.mult)
                kr = fold(mckv, NT, 160)[:, :, P:160]
                ku, kv_ = fold(kr_tmp[:, 0], NT, 32), fold(kr_tmp[:, 1], NT, 32)
                nc.vector.tensor_tensor(ku, kr, mc[:, :, 0:32], ALU.mult)
                for i in range(2):
                    a, b = slice(16 * i, 16 * i + 16), slice(16 - 16 * i, 32 - 16 * i)
                    nc.vector.tensor_tensor(kv_[:, :, a], kr[:, :, b], ms[:, :, a], ALU.mult)
                nc.vector.drain()
                nc.vector.tensor_tensor(qr, u, v, ALU.add)
                nc.vector.tensor_tensor(kr, ku, kv_, ALU.add)
                nc.vector.tensor_copy(fold(kcat, NT, 4, 96)[:, :, :, 0:64], fold(kvr, NT, 4, P)[:, :, :, 0:64])
                nc.vector.drain()
                nc.vector.tensor_copy(fold(kcat, NT, 4, 96)[:, :, :, 64:96],
                                      kr.unsqueeze(2).to_broadcast([P, NT, 4, 32])).then_inc(ml_rope, 1)
                dve_lo(dve, l, 11)
                dve_lo(dve, l, 12)
                dve.wait_ge(na_ready, l + 1)
                dve_items(dve, l * 20, heads1())
                dh = rows[:, :, 256:512]
                dh4 = dh.rearrange("p t (h d) -> p t h d", h=4)
                nc.vector.drain()
                nc.vector.tensor_tensor(fold(naq, NT, 256), dh, dh, ALU.mult)
                nc.vector.tensor_scalar(nak[:, 0:HD], prow[:, 0:64], prow[:, 321:322], None, ALU.mult)
                nc.vector.drain()
                nc.vector.tensor_reduce(out=gs[:, 0, 0:8], in_=fold(naq, 8, HD), op=ALU.add, axis=AX.X).then_inc(sub_sum, 1)
                dve.wait_ge(sub_std, l + 1)
                nc.vector.reciprocal(gs[:, 2, 0:8], gs[:, 1, 0:8])
                nc.vector.drain()
                nc.vector.tensor_tensor(dh4, dh4, fold(gs[:, 2, 0:8], NT, 4).unsqueeze(3).to_broadcast([P, NT, 4, HD]), ALU.mult)
                nc.vector.drain()
                nc.vector.tensor_tensor(dh4, dh4, nak[:, 0:HD].unsqueeze(1).unsqueeze(1).to_broadcast([P, NT, 4, HD]),
                                        ALU.mult).then_inc(mix_ready, 1)
                dve_split(dve, 3 * l + 1, ps8)
                for j in range(3):
                    dve_lo(dve, l, C1_O + j + SPLIT)
                dve_post(dve, 2 * l)
                dve_norm(dve, 2 * l + 1, 3 * l + 2, l, C1_FFN + 1)
                dve_ffn(dve, l, C1_FFN, l, 0, l)
                dve_post(dve, 2 * l + 1)
                add_out(dve, l, 11)
            nc.vector.tensor_scalar(nsink[:], prow2[:, 0:32], -1.0, None, ALU.mult)
            for n in range(DEPTH2):
                kind, c0, b0, g = KINDS2[n], BASE2[n], bank0[n], DEPTH1 + n
                nin = len(IN2[kind])
                nc.vector.scalar_tensor_tensor(out=acol[:, 0:8], in0=mod[:, n, 8:16], scalar=1.0,
                                               in1=pcol2[:, 16 * n:16 * n + 8], op0=ALU.add, op1=ALU.mult)
                nc.vector.scalar_tensor_tensor(out=acol[:, 8:16], in0=mod[:, n, 32:40], scalar=1.0,
                                               in1=pcol2[:, 16 * n + 8:16 * n + 16], op0=ALU.add, op1=ALU.mult).then_inc(acol_ready, 1)
                dve_norm(dve, 2 * g, 3 * g, DEPTH1, c0 + 1)
                dve.wait_ge(cb2_loaded, 16)
                {"swa": dve_swa, "gla": dve_gla, "fox": dve_fox}[kind](dve, n, c0, b0)
                dve_split(dve, 3 * g + 1, ps8)
                for j in range(3):
                    dve_lo(dve, DEPTH1, c0 + nin + j + SPLIT)
                dve_gated(dve, n, 0, c0 + nin + 3)
                dve_norm(dve, 2 * g + 1, 3 * g + 2, DEPTH1, c0 + nin + 5)
                dve_ffn(dve, DEPTH1, c0 + nin + 4, g, (b0 + nin) % 2, g if g < ADA_LAYERS else None)
                dve_gated(dve, n, 1, c0 + nin + 4 + FFN_UNITS - 1)
                if g < ADA_LAYERS:
                    add_out(dve, g, 11)
            m = 2 * (DEPTH1 + DEPTH2)
            dve.wait_ge(gain_loaded, 16 * 5)
            for t in range(NT):
                dve.wait_ge(std_ready, NT * m + t + 1)
                nc.vector.reciprocal(rs[:, t:t + 1], sd[:, t:t + 1])
                nc.vector.drain()
                nc.vector.scalar_tensor_tensor(out=rows[:, t], in0=x[:, t], scalar=rs[:, t:t + 1], in1=gain[:],
                                               op0=ALU.mult, op1=ALU.mult).then_inc(out_ready, 1)


def _unit(a):
    k, n = a.shape[0] // P, a.shape[1]
    u = np.zeros((P, UNIT), np.float32)
    u[:, :k * n] = a.reshape(k, P, n).transpose(1, 0, 2).reshape(P, k * n)
    return u


def _cols(v):
    return v.reshape(-1, P).T


def _ffn_units(gu, down):
    out = []

    def f_unit(f):
        c = slice(f * P, (f + 1) * P)
        return _unit(np.concatenate([gu[:, :DFF][:, c], gu[:, DFF:][:, c]], 1))

    out += [f_unit(0), f_unit(1)]
    for s in range(1, NF // 2):
        out += [f_unit(2 * s), f_unit(2 * s + 1), _unit(down[(s - 1) * 256:s * 256])]
    return out + [_unit(down[-256:])]


def _column_units(a, n=None):
    return [_unit(a[:, i:i + 256]) for i in range(0, a.shape[1], 256)][:n]


def _weights(a):
    units = []
    for l in range(DEPTH1):
        win = a["w_in"][l]
        q = win[:, 1536:1792].reshape(D, 4, HD)[:, [0, 2, 1, 3]].reshape(D, 256)
        win = np.concatenate([win[:, :1536], q, win[:, 1792:]], 1)
        columns = _column_units(win)
        small = np.zeros((P, UNIT), np.float32)
        small[:, :768] = a["mla_w_uq"][l].reshape(2, P, 384).transpose(1, 0, 2).reshape(P, 768)
        small[:, 768:1280] = a["mla_w_ukv"][l]
        units += [small if u is None else columns[u] for u in W_IN1]
        units += _column_units(a["w_o"][l]) + _ffn_units(a["ffn_w_gate_up"][l], a["ffn_w_down"][l])
    seen = {"swa": 0, "gla": 0, "fox": 0}
    for n, kind in enumerate(KINDS2):
        i = seen[kind]
        seen[kind] += 1
        win = a[f"{kind}_w_in_2"][i]
        if kind == "swa":
            order = [(2 * (c // 4) + half) * 4 + c % 4 for c in range(8) for half in range(2)]
            q = win[:, :D].reshape(D, 16, HD)[:, order].reshape(D, D)
            units += _column_units(np.concatenate([q, win[:, D:]], 1))
        elif kind == "gla":
            low = np.zeros((D, P), np.float32)
            low[:, :16] = win[:, 3072:]
            units += _column_units(win[:, :1024]) + [_unit(low)] + _column_units(win[:, 1024:3072])
        else:
            columns = _column_units(win)
            units += columns[12:] + columns[:12]
        units += _column_units(a[f"{kind}_w_o_2"][i]) + _ffn_units(a["ffn_w_gu_2"][n], a["ffn_w_down_2"][n])
    return np.stack(units)


def _constants():
    tok = np.arange(SEQ)

    def by_tile(t):
        return t.reshape(NT, P, -1).transpose(1, 0, 2).reshape(P, -1).astype(np.float32)

    def pair(t):
        return np.concatenate([t[:P, :P], t[P:]], 1).astype(np.float32)

    def turn(pos, d, theta, old=True):
        inv = (np.float32(theta) ** (-np.arange(0, d, 2, dtype=np.float32) / np.float32(d))).astype(np.float32)
        ang = (pos.astype(np.float32)[:, None] * inv[None]).astype(np.float32).astype(np.float64)
        return np.concatenate([np.cos(ang)] * 2, 1), np.concatenate([-np.sin(ang), np.sin(ang)], 1)

    rc, rs_ = turn(tok // GRID, 32, 10000.0)
    cc, cs = turn(tok % GRID, 32, 10000.0)
    ax_c, ax_s = np.tile(np.concatenate([rc, cc], 1), (1, 4)), np.tile(np.concatenate([rs_, cs], 1), (1, 4))
    mc, ms = (np.tile(v, (1, 4)) for v in turn(tok, 32, 10000.0))
    dist = -np.abs(tok[:, None] - tok[None])
    cq, ck = (np.arange(P) % GRID)[:, None], np.arange(GRID)[None]
    start = np.clip(cq - 8, 0, GRID - 16)
    na = np.where((ck >= start) & (ck < start + 16), 0.0, NEG)
    c1 = np.concatenate([by_tile(dist), na, by_tile(ax_c), by_tile(ax_s), by_tile(mc), by_tile(ms)], 1)
    sc, ss_ = (np.tile(v, (1, 4)) for v in turn(tok, HD, 150000.0))
    q, k = tok[:, None], tok[None]
    causal = np.where(k <= q, 0.0, NEG)
    window = np.where((k <= q) & (k > q - P), 0.0, NEG)
    upto = (q <= k).astype(np.float32)
    s, t = np.arange(P)[:, None], np.arange(P)[None]
    same = s // 64 == t // 64
    levels = [(s == t)]
    for lv in range(1, 7):
        m = 64 >> lv
        levels.append((s // (2 * m) == t // (2 * m)) & (s % (2 * m) < m) & (t % (2 * m) >= m))
    c2 = np.concatenate([by_tile(sc), by_tile(ss_), pair(causal), pair(window), by_tile(upto), same & (s <= t),
                         *levels], 1)
    assert c1.shape[1] == NCB1 and c2.shape[1] == NCB2
    return np.ascontiguousarray(c1, np.float32), np.ascontiguousarray(c2, np.float32)


def layout(a):
    c1, c2 = _constants()
    ada = a["ada_w_2"].reshape(4, 2, 4, P, 12, ADA).transpose(0, 4, 1, 3, 2, 5).reshape(96, P, UNIT)
    lam = [0.8 - 0.6 * math.exp(-0.3 * l) for l in range(DEPTH1)]
    row1 = np.stack([np.concatenate([a["diff_subln"][l], a["gqa_q_norm"][l], a["gqa_k_norm"][l],
                                     a["diff_lambda_q1"][l], a["diff_lambda_q2"][l], a["diff_lambda_k1"][l],
                                     a["diff_lambda_k2"][l], np.float32([lam[l], 1.0 - lam[l]])]) for l in range(DEPTH1)])
    col1 = np.stack([np.concatenate([_cols(a["pre_mix_norm"][l]), _cols(a["pre_ffn_norm"][l]),
                                     _cols(a["mla_q_norm"][l]), _cols(a["mla_kv_norm"][l])], 1) for l in range(DEPTH1)])
    col2 = np.concatenate([_cols(a["norm_gain_2"][n, i]) for n in range(DEPTH2) for i in range(2)], 1)
    row2 = np.concatenate([a["swa_sinks_2"].reshape(-1), a["fox_b_f_2"].reshape(-1), a["gla_head_norm_2"].reshape(-1)])
    x = a["x"][0].reshape(NT, P, D).transpose(1, 0, 2)
    return {
        "wts": _weights(a), "ada": ada, "ada_b": _cols(a["ada_b_2"]).reshape(P, 4, 48), "x_in": x, "c_col": _cols(a["c_2"][0]),
        "rel_bias": a["na_rel_bias"], "col1": col1, "row1": row1, "gain_mix": a["post_mix_norm"],
        "gain_ffn": a["post_ffn_norm"], "col2": col2, "row2": row2, "gate_w": a["gla_w_gate_up_2"][0],
        "gate_b": a["gla_b_gate_2"], "final_gain": a["final_norm_2"].reshape(1, D), "ident_in": np.eye(P, dtype=np.float32),
        "cst1": c1, "cst2": c2,
    }


def kernel(**inputs):
    import concourse.bacc as bacc
    from concourse.bass_utils import run_bass_kernel_spmd

    arrays = {k: np.ascontiguousarray(v, np.float32) for k, v in layout({k: np.asarray(v) for k, v in inputs.items()}).items()}
    nc = bacc.Bacc("TRN2", target_bir_lowering=False, num_devices=1)
    args = {k: nc.dram_tensor(k, v.shape, mybir.dt.float32, kind="ExternalInput").ap() for k, v in arrays.items()}
    out = nc.dram_tensor("out", (P, NT, D), mybir.dt.float32, kind="ExternalOutput").ap()
    build(nc, **args, out=out)
    r = run_bass_kernel_spmd(nc, [arrays], core_ids=[0])
    return r.results[0]["out"].transpose(1, 0, 2).reshape(1, SEQ, D)
```
